# Optimizing a Trainium2 kernel written in Bass

```python
import math
import jax, jax.numpy as jnp
from jax import lax
import numpy as np

D_MODEL = 1024
BATCH = 1
SEQ = 512
DEPTH = 1

GRID_W = 64
CTX_LEN = 256
N_FOURIER_GROUPS = 4
FOURIER_GROUP_DIM = 128
FOURIER_WIDTH = N_FOURIER_GROUPS * FOURIER_GROUP_DIM
DN_HEADS = 8
DN_HEAD_DIM = 128
DN_WIDTH = DN_HEADS * DN_HEAD_DIM
DN_CONV = 3
DN_CHUNK = 64
N_DIR = 2
N_BRANCH = 2
D_FF = 2816
FFN_CONV = 3
NORM_EPS = 1e-6
L2_EPS = 1e-6

OFF_F = 0
OFF_Q = OFF_F + FOURIER_WIDTH
OFF_K = OFF_Q + DN_WIDTH
OFF_V = OFF_K + DN_WIDTH
OFF_Z = OFF_V + DN_WIDTH
OFF_B = OFF_Z + DN_WIDTH
OFF_A = OFF_B + N_DIR * DN_HEADS
OFF_G = OFF_A + N_DIR * DN_HEADS
IN_WIDTH = OFF_G + N_BRANCH * D_MODEL


def rms_norm(x, w):
    xf = x.astype(jnp.float32)
    y = xf * lax.rsqrt(jnp.mean(xf * xf, axis=-1, keepdims=True) + NORM_EPS)
    return (y * w.astype(jnp.float32)).astype(x.dtype)

def l2norm(x):
    return x * lax.rsqrt(jnp.sum(x * x, axis=-1, keepdims=True) + L2_EPS)

def modulate(h, shift, scale):
    return h * (1 + scale) + shift

def dwconv1d(x, w):
    k = w.shape[0]
    pad = (k - 1) // 2
    return lax.conv_general_dilated(
        x, w[:, None, :].astype(x.dtype), window_strides=(1,), padding=[(pad, pad)],
        dimension_numbers=('NWC', 'WIO', 'NWC'), feature_group_count=x.shape[-1])

def dwconv2d(x, w, rows, cols):
    b, t, ch = x.shape
    kh, kw = w.shape[0], w.shape[1]
    y = lax.conv_general_dilated(
        x.reshape(b, rows, cols, ch), w[:, :, None, :].astype(x.dtype), window_strides=(1, 1),
        padding=[((kh - 1) // 2, (kh - 1) // 2), ((kw - 1) // 2, (kw - 1) // 2)],
        dimension_numbers=('NHWC', 'HWIO', 'NHWC'), feature_group_count=ch)
    return y.reshape(b, t, ch)

def fourier_mix(f):
    b, t, _ = f.shape
    fg = f.astype(jnp.float32).reshape(b, t, N_FOURIER_GROUPS, FOURIER_GROUP_DIM)
    out = jnp.fft.fft2(fg, axes=(1, 3), norm="ortho").real
    return out.reshape(b, t, FOURIER_WIDTH).astype(f.dtype)

def chunk_gated_delta(q, k, v, g, beta, state):
    b, t, h, dk = q.shape
    dv = v.shape[-1]
    n = t // DN_CHUNK

    def chunks(a):
        a = a.reshape((b, n, DN_CHUNK, h) + a.shape[3:])
        return jnp.moveaxis(a, (1, 3), (0, 2))

    qc, kc, vc = chunks(q), chunks(k), chunks(v)
    gc = jnp.cumsum(chunks(g), axis=-1)
    bc = chunks(beta)
    idx = jnp.arange(DN_CHUNK)
    lower_strict = idx[:, None] > idx[None, :]
    lower_incl = idx[:, None] >= idx[None, :]
    decay = jnp.exp(jnp.where(lower_incl, gc[..., :, None] - gc[..., None, :], -jnp.inf))
    kk = jnp.einsum('nbhcd,nbhsd->nbhcs', kc, kc)
    l_mat = jnp.where(lower_strict, bc[..., :, None] * kk * decay, 0.0)
    rhs = jnp.concatenate([vc * bc[..., None], kc * (bc * jnp.exp(gc))[..., None]], axis=-1)
    sol = lax.linalg.triangular_solve(l_mat, rhs, left_side=True, lower=True, unit_diagonal=True)
    u, w = sol[..., :dv], sol[..., dv:]
    qk = jnp.einsum('nbhcd,nbhsd->nbhcs', qc, kc) * decay
    g_last = gc[..., -1]
    k_tail = kc * jnp.exp(g_last[..., None] - gc)[..., None]
    q_head = qc * jnp.exp(gc)[..., None]

    def step(s, xs):
        q_h, qk_i, u_i, w_i, k_t, gl = xs
        v_new = u_i - jnp.einsum('bhcd,bhde->bhce', w_i, s)
        o = jnp.einsum('bhcd,bhde->bhce', q_h, s) + jnp.einsum('bhcs,bhse->bhce', qk_i, v_new)
        s = s * jnp.exp(gl)[..., None, None] + jnp.einsum('bhcd,bhce->bhde', k_t, v_new)
        return s, o

    state, o = lax.scan(step, state, (q_head, qk, u, w, k_tail, g_last))
    o = jnp.moveaxis(o, (0, 2), (1, 3)).reshape(b, t, h, dv)
    return o, state

def mixer_core(h, init_states, w_in, conv_qkv, a_log, dt_bias):
    b, t, _ = h.shape
    p = h @ w_in
    f_in = p[..., OFF_F:OFF_Q]
    qkv = jax.nn.silu(dwconv1d(p[..., OFF_Q:OFF_Z], conv_qkv)).astype(jnp.float32)
    q, k, v = [a.reshape(b, t, DN_HEADS, DN_HEAD_DIM) for a in jnp.split(qkv, 3, axis=-1)]
    q = l2norm(q) * (DN_HEAD_DIM ** -0.5)
    k = l2norm(k)
    z = p[..., OFF_Z:OFF_B]
    beta = jax.nn.sigmoid(p[..., OFF_B:OFF_A].astype(jnp.float32)).reshape(b, t, N_DIR, DN_HEADS)
    a = p[..., OFF_A:OFF_G].astype(jnp.float32).reshape(b, t, N_DIR, DN_HEADS)
    g = -jnp.exp(a_log.astype(jnp.float32)) * jax.nn.softplus(a + dt_bias.astype(jnp.float32))
    gates = jax.nn.sigmoid(p[..., OFF_G:]).reshape(b, t, N_BRANCH, D_MODEL)
    flip = lambda arr: jnp.flip(arr, axis=1)
    o_f, s_f = chunk_gated_delta(q, k, v, g[:, :, 0], beta[:, :, 0], init_states[0])
    o_b, s_b = chunk_gated_delta(flip(q), flip(k), flip(v), flip(g[:, :, 1]), flip(beta[:, :, 1]),
                                 init_states[1])
    return f_in, o_f + flip(o_b), z, gates, (s_f, s_b)

def merge_branches(f_in, o_dn, z, gates, dn_norm, w_fourier, w_dn, w_out):
    b, t, _ = z.shape
    zh = z.reshape(b, t, DN_HEADS, DN_HEAD_DIM).astype(jnp.float32)
    o = (rms_norm(o_dn, dn_norm) * jax.nn.silu(zh)).astype(z.dtype).reshape(b, t, DN_WIDTH)
    y_f = fourier_mix(f_in) @ w_fourier
    y_d = o @ w_dn
    return (gates[:, :, 0] * y_f + gates[:, :, 1] * y_d) @ w_out

def ffn_sublayer(stream, shift, scale, gate, g_pre, g_post, w_up, conv_w, w_down, rows, cols):
    h = modulate(rms_norm(stream, g_pre), shift, scale)
    a, u = jnp.split(h @ w_up, 2, axis=-1)
    a = dwconv2d(a, conv_w, rows, cols)
    y = (jax.nn.silu(a) * u) @ w_down
    return stream + gate * rms_norm(y, g_post)

def first_inputs(seed: int = 0) -> dict:
    key = jax.random.key(seed)
    ks = jax.random.split(key, 24)
    nrm = lambda k, shape, scale: jax.random.normal(k, shape, jnp.float32) * scale
    gain = lambda k, n: 1.0 + nrm(k, (DEPTH, n), 0.02)
    x = nrm(ks[0], (BATCH, SEQ, D_MODEL), 1.0)
    c = nrm(ks[1], (BATCH, D_MODEL), 1.0)
    ctx = nrm(ks[2], (BATCH, CTX_LEN, D_MODEL), 1.0)
    c_ctx = nrm(ks[3], (D_MODEL,), 1.0)
    w_ada = nrm(ks[4], (DEPTH, D_MODEL, 6 * D_MODEL), 0.5 * D_MODEL ** -0.5)
    b_ada = nrm(ks[5], (DEPTH, 6 * D_MODEL), 0.01)
    norm_pre_mix = gain(ks[6], D_MODEL)
    norm_post_mix = gain(ks[7], D_MODEL)
    norm_pre_ffn = gain(ks[8], D_MODEL)
    norm_post_ffn = gain(ks[9], D_MODEL)
    w_in = nrm(ks[10], (DEPTH, D_MODEL, IN_WIDTH), D_MODEL ** -0.5)
    conv_qkv = nrm(ks[11], (DEPTH, DN_CONV, 3 * DN_WIDTH), DN_CONV ** -0.5)
    a_log = jnp.log(jax.random.uniform(ks[12], (DEPTH, N_DIR, DN_HEADS), jnp.float32, 1.0, 16.0))
    dt = jnp.exp(jax.random.uniform(ks[13], (DEPTH, N_DIR, DN_HEADS), jnp.float32,
                                    math.log(1e-3), math.log(1e-1)))
    dt_bias = dt + jnp.log(-jnp.expm1(-dt))
    dn_norm = gain(ks[14], DN_HEAD_DIM)
    w_fourier = nrm(ks[15], (DEPTH, FOURIER_WIDTH, D_MODEL), FOURIER_WIDTH ** -0.5)
    w_dn = nrm(ks[16], (DEPTH, DN_WIDTH, D_MODEL), DN_WIDTH ** -0.5)
    w_out = nrm(ks[17], (DEPTH, D_MODEL, D_MODEL), D_MODEL ** -0.5)
    w_up = nrm(ks[18], (DEPTH, D_MODEL, 2 * D_FF), D_MODEL ** -0.5)
    conv_ffn = nrm(ks[19], (DEPTH, FFN_CONV, FFN_CONV, D_FF), 1.0 / FFN_CONV)
    w_down = nrm(ks[20], (DEPTH, D_FF, D_MODEL), D_FF ** -0.5)
    return {"x": x, "c": c, "ctx": ctx, "c_ctx": c_ctx, "w_ada": w_ada, "b_ada": b_ada,
            "norm_pre_mix": norm_pre_mix, "norm_post_mix": norm_post_mix,
            "norm_pre_ffn": norm_pre_ffn, "norm_post_ffn": norm_post_ffn,
            "w_in": w_in, "conv_qkv": conv_qkv, "a_log": a_log, "dt_bias": dt_bias,
            "dn_norm": dn_norm, "w_fourier": w_fourier, "w_dn": w_dn, "w_out": w_out,
            "w_up": w_up, "conv_ffn": conv_ffn, "w_down": w_down}

def first_block(x, c, ctx, c_ctx, w_ada, b_ada, norm_pre_mix, norm_post_mix, norm_pre_ffn,
              norm_post_ffn, w_in, conv_qkv, a_log, dt_bias, dn_norm, w_fourier, w_dn, w_out,
              w_up, conv_ffn, w_down):
    bsz, seq, _ = x.shape
    rows = seq // GRID_W
    ctx_len = ctx.shape[1]
    for l in range(DEPTH):
        mod_x = (jax.nn.silu(c) @ w_ada[l] + b_ada[l])[:, None, :]
        mod_c = (jax.nn.silu(c_ctx) @ w_ada[l] + b_ada[l])[None, None, :]
        sh1, sc1, gt1, sh2, sc2, gt2 = jnp.split(mod_x, 6, axis=-1)
        csh1, csc1, cgt1, csh2, csc2, cgt2 = jnp.split(mod_c, 6, axis=-1)
        zero = jnp.zeros((bsz, DN_HEADS, DN_HEAD_DIM, DN_HEAD_DIM), jnp.float32)

        hc = modulate(rms_norm(ctx, norm_pre_mix[l]), csh1, csc1)
        fc, oc, zc, gtc, ctx_states = mixer_core(hc, (zero, zero), w_in[l], conv_qkv[l],
                                                 a_log[l], dt_bias[l])

        hx = modulate(rms_norm(x, norm_pre_mix[l]), sh1, sc1)
        fx, ox, zx, gtx, _ = mixer_core(hx, ctx_states, w_in[l], conv_qkv[l], a_log[l], dt_bias[l])
        yx = merge_branches(fx, ox, zx, gtx, dn_norm[l], w_fourier[l], w_dn[l], w_out[l])
        x = x + gt1 * rms_norm(yx, norm_post_mix[l])
        x = ffn_sublayer(x, sh2, sc2, gt2, norm_pre_ffn[l], norm_post_ffn[l], w_up[l],
                         conv_ffn[l], w_down[l], rows, GRID_W)

        if l < DEPTH - 1:
            yc = merge_branches(fc, oc, zc, gtc, dn_norm[l], w_fourier[l], w_dn[l], w_out[l])
            ctx = ctx + cgt1 * rms_norm(yc, norm_post_mix[l])
            ctx = ffn_sublayer(ctx, csh2, csc2, cgt2, norm_pre_ffn[l], norm_post_ffn[l], w_up[l],
                               conv_ffn[l], w_down[l], 1, ctx_len)
    return x


DEPTH_2 = 2

HEAD_DIM = 64
N_HEADS = D_MODEL // HEAD_DIM
INNER = N_HEADS * HEAD_DIM
ROT_DIM = HEAD_DIM // 4
ROPE_THETA = 500000.0
DSWA_GROUPS = ((128, 1), (512, 4), (2048, 16))
N_GROUPS = len(DSWA_GROUPS)
BLOCK = 128
N_MIXERS = 2
EPS = 1e-6
FOX_IN = 4 * INNER + N_HEADS
DSW_IN = 3 * N_GROUPS * INNER + INNER


def rms_norm_2(x, g):
    xf = x.astype(jnp.float32)
    y = xf * lax.rsqrt(jnp.mean(xf * xf, axis=-1, keepdims=True) + EPS) * g.astype(jnp.float32)
    return y.astype(x.dtype)

def rotary_tables(positions):
    inv_freq = ROPE_THETA ** (-jnp.arange(0, ROT_DIM, 2, dtype=jnp.float32) / ROT_DIM)
    ang = positions.astype(jnp.float32)[..., None] * inv_freq
    return jnp.cos(ang), jnp.sin(ang)

def apply_partial_rotary(t, cos, sin):
    half = ROT_DIM // 2
    c = cos[:, :, None, None, :].astype(t.dtype)
    s = sin[:, :, None, None, :].astype(t.dtype)
    t1, t2, rest = t[..., :half], t[..., half:ROT_DIM], t[..., ROT_DIM:]
    return jnp.concatenate([t1 * c - t2 * s, t2 * c + t1 * s, rest], axis=-1)

def fox_attention(q, k, v, c):
    B, S, H, dh = q.shape
    nq = S // BLOCK
    scale = dh ** -0.5
    qb = q.reshape(B, nq, BLOCK, H, dh).transpose(1, 0, 2, 3, 4)
    cb = c.reshape(B, nq, BLOCK, H).transpose(1, 0, 3, 2)
    c_k = c.transpose(0, 2, 1)
    key_pos = jnp.arange(S)

    def one_block(args):
        qi, ci, bi = args
        s = jnp.einsum('bqhd,bkhd->bhqk', qi, k).astype(jnp.float32) * scale
        s = s + ci[..., None] - c_k[:, :, None, :]
        q_pos = bi * BLOCK + jnp.arange(BLOCK)
        mask = key_pos[None, :] <= q_pos[:, None]
        s = jnp.where(mask, s, -jnp.inf)
        p = jax.nn.softmax(s, axis=-1).astype(v.dtype)
        return jnp.einsum('bhqk,bkhd->bqhd', p, v)

    o = lax.map(one_block, (qb, cb, jnp.arange(nq)))
    return o.transpose(1, 0, 2, 3, 4).reshape(B, S, H, dh)

def fox_mixer(h, w_in, b_f, q_g, k_g):
    B, S, _ = h.shape
    proj = h @ w_in
    q = rms_norm_2(proj[..., :INNER].reshape(B, S, N_HEADS, HEAD_DIM), q_g)
    k = rms_norm_2(proj[..., INNER:2 * INNER].reshape(B, S, N_HEADS, HEAD_DIM), k_g)
    v = proj[..., 2 * INNER:3 * INNER].reshape(B, S, N_HEADS, HEAD_DIM)
    gate = proj[..., 3 * INNER:4 * INNER]
    f_logit = proj[..., 4 * INNER:].astype(jnp.float32) + b_f.astype(jnp.float32)
    c = jnp.cumsum(jax.nn.log_sigmoid(f_logit), axis=1)
    o = fox_attention(q, k, v, c)
    return o.reshape(B, S, INNER), gate

def _band(t):
    prev = jnp.concatenate([jnp.zeros_like(t[:, :1]), t[:, :-1]], axis=1)
    return jnp.concatenate([prev, t], axis=2)

def dilated_window_attention(q, k, v, window, dilation):
    B, S, H, dh = q.shape
    r = dilation
    L = S // r
    n_back = window // r
    nb = -(-L // BLOCK)
    Lp = nb * BLOCK
    scale = dh ** -0.5

    def to_blocks(t):
        t = t.reshape(B, L, r, H, dh).transpose(0, 2, 1, 3, 4).reshape(B * r, L, H, dh)
        t = jnp.pad(t, ((0, 0), (0, Lp - L), (0, 0), (0, 0)))
        return t.reshape(B * r, nb, BLOCK, H, dh)

    qb, kb, vb = to_blocks(q), to_blocks(k), to_blocks(v)
    s = jnp.einsum('znqhd,znkhd->znhqk', qb, _band(kb)).astype(jnp.float32) * scale
    q_idx = jnp.arange(nb)[:, None] * BLOCK + jnp.arange(BLOCK)[None, :]
    k_idx = jnp.arange(nb)[:, None] * BLOCK - BLOCK + jnp.arange(2 * BLOCK)[None, :]
    dist = q_idx[:, :, None] - k_idx[:, None, :]
    mask = (dist >= 0) & (dist <= n_back) & (k_idx[:, None, :] >= 0)
    s = jnp.where(mask[None, :, None], s, -jnp.inf)
    lse = jax.nn.logsumexp(s, axis=-1)
    p = jnp.exp(s - lse[..., None]).astype(v.dtype)
    o = jnp.einsum('znhqk,znkhd->znqhd', p, _band(vb))
    o = o.reshape(B * r, Lp, H, dh)[:, :L]
    o = o.reshape(B, r, L, H, dh).transpose(0, 2, 1, 3, 4).reshape(B, S, H, dh)
    lse = lse.transpose(0, 1, 3, 2).reshape(B * r, Lp, H)[:, :L]
    lse = lse.reshape(B, r, L, H).transpose(0, 2, 1, 3).reshape(B, S, H)
    return o, lse

def dsw_mixer(h, cos, sin, w_in, q_g, k_g):
    B, S, _ = h.shape
    proj = h @ w_in
    qkv = proj[..., :3 * N_GROUPS * INNER].reshape(B, S, 3, N_GROUPS, N_HEADS, HEAD_DIM)
    gate = proj[..., 3 * N_GROUPS * INNER:]
    q = apply_partial_rotary(rms_norm_2(qkv[:, :, 0], q_g[:, None, :]), cos, sin)
    k = apply_partial_rotary(rms_norm_2(qkv[:, :, 1], k_g[:, None, :]), cos, sin)
    v = qkv[:, :, 2]
    outs, lses = [], []
    for g, (window, dilation) in enumerate(DSWA_GROUPS):
        o_g, lse_g = dilated_window_attention(q[:, :, g], k[:, :, g], v[:, :, g], window, dilation)
        outs.append(o_g)
        lses.append(lse_g)
    wts = jax.nn.softmax(jnp.stack(lses, axis=0), axis=0).astype(v.dtype)
    o = jnp.einsum('gbsh,gbshd->bshd', wts, jnp.stack(outs, axis=0))
    return o.reshape(B, S, INNER), gate

def second_inputs(seed: int = 0) -> dict:
    key = jax.random.key(seed)
    ks = jax.random.split(key, 13)
    n_fox = (DEPTH_2 + 1) // N_MIXERS
    n_dsw = DEPTH_2 // N_MIXERS
    f32 = jnp.float32
    x = jax.random.normal(ks[0], (BATCH, SEQ, D_MODEL), f32)
    offset = jax.random.randint(ks[1], (BATCH, 1), 0, 4096, dtype=jnp.int32)
    positions = offset + jnp.arange(SEQ, dtype=jnp.int32)[None, :]
    norm_g = 1.0 + 0.02 * jax.random.normal(ks[2], (DEPTH_2, D_MODEL), f32)
    fox_w_in = jax.random.normal(ks[3], (n_fox, D_MODEL, FOX_IN), f32) * D_MODEL ** -0.5
    fox_b_f = jax.random.uniform(ks[4], (n_fox, N_HEADS), f32, minval=1.0, maxval=4.0)
    fox_q_norm = 1.0 + 0.02 * jax.random.normal(ks[5], (n_fox, HEAD_DIM), f32)
    fox_k_norm = 1.0 + 0.02 * jax.random.normal(ks[6], (n_fox, HEAD_DIM), f32)
    fox_w_out = jax.random.normal(ks[7], (n_fox, INNER, D_MODEL), f32) * (2 * INNER) ** -0.5
    dsw_w_in = jax.random.normal(ks[8], (n_dsw, D_MODEL, DSW_IN), f32) * D_MODEL ** -0.5
    dsw_q_norm = 1.0 + 0.02 * jax.random.normal(ks[9], (n_dsw, N_GROUPS, HEAD_DIM), f32)
    dsw_k_norm = 1.0 + 0.02 * jax.random.normal(ks[10], (n_dsw, N_GROUPS, HEAD_DIM), f32)
    dsw_w_out = jax.random.normal(ks[11], (n_dsw, INNER, D_MODEL), f32) * (2 * INNER) ** -0.5
    return {"x": x, "positions": positions, "norm_g": norm_g,
            "fox_w_in": fox_w_in, "fox_b_f": fox_b_f, "fox_q_norm": fox_q_norm,
            "fox_k_norm": fox_k_norm, "fox_w_out": fox_w_out,
            "dsw_w_in": dsw_w_in, "dsw_q_norm": dsw_q_norm, "dsw_k_norm": dsw_k_norm,
            "dsw_w_out": dsw_w_out}

def second_block(x, positions, norm_g, fox_w_in, fox_b_f, fox_q_norm, fox_k_norm, fox_w_out,
              dsw_w_in, dsw_q_norm, dsw_k_norm, dsw_w_out):
    cos, sin = rotary_tables(positions)
    for i in range(DEPTH_2):
        j = i // N_MIXERS
        h = rms_norm_2(x, norm_g[i])
        if i % N_MIXERS == 0:
            o, gate = fox_mixer(h, fox_w_in[j], fox_b_f[j], fox_q_norm[j], fox_k_norm[j])
            w_out = fox_w_out[j]
        else:
            o, gate = dsw_mixer(h, cos, sin, dsw_w_in[j], dsw_q_norm[j], dsw_k_norm[j])
            w_out = dsw_w_out[j]
        x = x + (o * jax.nn.silu(gate)) @ w_out
    return x


def setup_inputs(seed=0):
    out = dict(first_inputs(seed))
    for name, value in second_inputs(seed + 1).items():
        if name != "x":
            out[name + "_2"] = value
    return out


def reference(
    x, c, ctx, c_ctx, w_ada, b_ada, norm_pre_mix, norm_post_mix, norm_pre_ffn, norm_post_ffn,
    w_in, conv_qkv, a_log, dt_bias, dn_norm, w_fourier, w_dn, w_out, w_up, conv_ffn, w_down,
    positions_2, norm_g_2, fox_w_in_2, fox_b_f_2, fox_q_norm_2, fox_k_norm_2, fox_w_out_2,
    dsw_w_in_2, dsw_q_norm_2, dsw_k_norm_2, dsw_w_out_2,
):
    x = first_block(
        x, c, ctx, c_ctx, w_ada, b_ada, norm_pre_mix, norm_post_mix, norm_pre_ffn,
        norm_post_ffn, w_in, conv_qkv, a_log, dt_bias, dn_norm, w_fourier, w_dn, w_out, w_up,
        conv_ffn, w_down,
    )
    return second_block(
        x, positions_2, norm_g_2, fox_w_in_2, fox_b_f_2, fox_q_norm_2, fox_k_norm_2,
        fox_w_out_2, dsw_w_in_2, dsw_q_norm_2, dsw_k_norm_2, dsw_w_out_2,
    )


_drawn_inputs = setup_inputs


def setup_inputs(seed=0):
    import zlib

    import numpy as np

    out = dict(_drawn_inputs(seed))
    spreads = {}
    factors = {'ctx': 4.86,
     'c_ctx': 8.0,
     'b_ada': 3.541,
     'norm_pre_mix': 6.587,
     'norm_post_mix': 8.0,
     'norm_pre_ffn': 7.285,
     'norm_post_ffn': 8.0,
     'dn_norm': 8.0,
     'norm_g_2': 8.0,
     'fox_q_norm_2': 8.0,
     'fox_k_norm_2': 8.0,
     'dsw_q_norm_2': 8.0,
     'dsw_k_norm_2': 8.0}
    for name, (base, spread) in spreads.items():
        noise = np.random.default_rng([zlib.crc32(name.encode()), seed]).standard_normal(out[name].shape)
        drawn = base * np.exp(spread * noise) if base else spread * noise
        out[name] = __import__('jax').numpy.asarray(drawn.astype(out[name].dtype))
    for name, factor in factors.items():
        out[name] = (out[name] * factor).astype(out[name].dtype)
    return out
```

```python
import math
from contextlib import ExitStack, contextmanager

import concourse.bass as bass
import numpy as np
from concourse import mybir

F32 = mybir.dt.float32
I32 = mybir.dt.int32
ALU = mybir.AluOpType
ACT = mybir.ActivationFunctionType
AX = mybir.AxisListType.X
P = 128
SEQ, CTX, DM = 512, 256, 1024
TX, TC, TT = SEQ // P, CTX // P, (SEQ + CTX) // P
KT = DM // P
HD, HE = 8, 128
FW = 512
DFF = 2816
FT = DFF // P
GRID_R, GRID_C = 8, 64
NA, DA = 16, 64
NG = 3
ROT = 16
EPS = 1e-6
NEG = -1.0e30
LEVELS = 7
OFF_Q, OFF_K, OFF_V, OFF_Z = 512, 1536, 2560, 3584
OFF_B = 4608
OFF_G = 4640

ROWS_A = {"b_ada": (0, 48), "pre_mix": (48, 8), "pre_ffn": (56, 8), "dn": (64, 1), "g2": (65, 16),
          "c": (81, 8), "cc": (89, 8)}


def constants():
    i = np.arange(P)
    m = {}
    m["ident"] = np.eye(P)
    m["le"] = (i[:, None] <= i[None, :])
    m["gt"] = (i[:, None] > i[None, :])
    m["ge"] = (i[:, None] >= i[None, :])
    m["lt"] = (i[:, None] < i[None, :])
    m["ones"] = np.ones((P, P))
    sq = np.stack([m[k] for k in ("ident", "le", "gt", "ge", "lt", "ones")], 1)
    lev = []
    for n in range(LEVELS):
        b = i >> n
        f = (b[None, :] == b[:, None] + 1) & (b[:, None] % 2 == 0)
        lev.append(np.stack([f, f.T], 1))
    lev = np.stack(lev, 1)
    j = i[:, None]
    k = i[None, :]
    att = [np.where(k >= j, 0, NEG), np.where(k <= j, 0, NEG),
           np.where((k <= j) & (k % 4 == j % 4), 0, NEG)]
    att = np.stack(att, 1)
    t = np.arange(SEQ)
    ang = 2 * np.pi * ((t[:, None] * t[None, :]) % SEQ) / SEQ
    ct = np.stack([np.cos(ang), -np.sin(ang)]) / np.sqrt(SEQ * P)
    ct = ct.reshape(2, TX, P, SEQ).transpose(2, 0, 1, 3)
    ang = 2 * np.pi * ((i[:, None] * i[None, :]) % P) / P
    cc = np.concatenate([np.cos(ang), np.sin(ang)], 1)
    inv = 500000.0 ** (-np.arange(0, ROT, 2) / ROT)
    hs = np.zeros((NA, NA // 2, P))
    for h in range(NA):
        hs[h, h // 2, (h % 2) * DA:(h % 2 + 1) * DA] = 1
    oh = np.zeros((NA, NA, P))
    for h in range(NA):
        oh[h, h, :] = 1
    f = lambda a: np.ascontiguousarray(a, dtype=np.float32)
    return {"k_sq": f(sq), "k_lev": f(lev), "k_att": f(att), "k_dft_t": f(ct), "k_dft_c": f(cc),
            "k_inv": f(np.broadcast_to(inv, (P, 8))), "k_hs": f(hs), "k_oh": f(oh)}


def build(nc, d, out, dbg=None, upto=99, inject=None):
    es = ExitStack()
    nsem = [0]

    def sem(name):
        return es.enter_context(nc.semaphore(name))

    def sb(stack, name, shape, dt=F32):
        return stack.enter_context(nc.sbuf_tensor(name, shape, dt))

    @contextmanager
    def local_sems():
        taken = []

        def take(name):
            taken.append(nc.alloc_semaphore(name=name))
            return taken[-1]

        yield take
        nc.clear_and_free_semaphores(taken)
        nc.all_engine_barrier()

    class Link:

        def __init__(self, eng, s, start=0, turn=None, per=0):
            self.eng, self.s, self.n, self.turn, self.per, self.start = eng, s, start, turn, per, start

        def __call__(self, ins):
            ins.then_inc(self.s, 1)
            self.n += 1
            v = self.n if self.turn is None else self.turn * self.per + self.n
            self.eng.wait_ge(self.s, v)

        def end(self):
            assert self.turn is None or self.n - self.start == self.per, (self.n, self.start, self.per)

    class Ring:

        def __init__(self, buf):
            self.buf = buf
            self.ready = [sem(f"slab_ready{j}") for j in range(2)]
            self.used = [sem(f"slab_used{j}") for j in range(2)]
            self.n = [0, 0]

        def load(self, sp, slot, src, turn=0):
            o = self.view(slot, src.shape)
            sp.wait_ge(self.used[slot], turn + (self.n[slot] + 1))
            sp.dma_start(o, src).then_inc(self.ready[slot], 16)

        def view(self, slot, shape):
            n = int(np.prod(shape[1:]))
            v = self.buf[:, slot, 0:n]
            if len(shape) == 3:
                return v.rearrange("p (a b) -> p a b", a=shape[1])
            if len(shape) == 4:
                return v.rearrange("p (a b c) -> p a b c", a=shape[1], b=shape[2])
            return v

        def wait(self, pe, slot, turn=0):
            pe.wait_ge(self.ready[slot], turn * 16 + 16 * (self.n[slot] + 1))

        def passed(self, a, b):
            self.n = [self.n[0] + a, self.n[1] + b]

    with es:
        bank = [es.enter_context(nc.psum_tensor(f"bank{i}", [P, 512], F32)) for i in range(8)]
        sq = sb(es, "squares", [P, 6, P])
        ident, m_le, m_gt, m_ge, m_lt, m_ones = (sq[:, i, :] for i in range(6))
        col = sb(es, "columns", [P, 97])
        colconv = sb(es, "conv_columns", [P, 72])
        colffn = sb(es, "ffn_conv_columns", [P, 198])
        wsc = sb(es, "norm_scale", [P, 3, KT])
        shf = sb(es, "norm_shift", [P, 3, KT])
        gtrow = sb(es, "gate_rows", [P, 2, DM])
        att = sb(es, "attention_masks", [P, 3, P])
        half = sb(es, "minus_half", [P, P])
        small = sb(es, "small_constants", [P, 3, 16])
        xt = sb(es, "x_tm", [P, TX, DM])
        ring = Ring(sb(es, "slab_ring", [P, 2, 4096]))
        s_mm, s_ev, s_st = sem("product_done"), sem("evacuated"), sem("staged")

        def colof(name, i=0):
            o, n = ROWS_A[name]
            return col[:, o + i:o + i + 1]

        with ExitStack() as ph:
            rowA = sb(ph, "rows_a", [97, P])
            rowB = sb(ph, "rows_b", [72, P])
            rowC = sb(ph, "rows_c", [99, 2, P])
            cs = sb(ph, "c_silu", [P, KT, 2])
            csrep = sb(ph, "c_silu_rep", [P, KT, P])
            grow = sb(ph, "rows_to_fold", [P, 4, DM])
            modc = sb(ph, "mod_columns", [P, 32, 2])
            s_row, s_tr, s_col, s_cs, s_mc, s_gr, s_mv, s_g = map(
                sem, "ada_rows ada_tr ada_col ada_cs ada_mod_cols ada_gate_rows ada_moved ada_grow".split())
            s_d = sem("ada_dve_chain")
            w_v = d["w_ada"][0].rearrange("(k p) n -> p k n", p=P)
            with nc.Block() as block:
                @block.sync
                def _(sp):
                    sp.dma_start(sq[:], d["k_sq"]).then_inc(s_row, 16)
                    sp.dma_start(att[:], d["k_att"]).then_inc(s_row, 16)
                    for src, name in ((d["b_ada"][0].rearrange("(n p) -> n p", p=P), "b_ada"),
                                      (d["norm_pre_mix"][0].rearrange("(n p) -> n p", p=P), "pre_mix"),
                                      (d["norm_pre_ffn"][0].rearrange("(n p) -> n p", p=P), "pre_ffn"),
                                      (d["dn_norm"], "dn"),
                                      (d["norm_g_2"].rearrange("a (n p) -> (a n) p", p=P), "g2"),
                                      (d["c"][0].rearrange("(n p) -> n p", p=P), "c"),
                                      (d["c_ctx"].rearrange("(n p) -> n p", p=P), "cc")):
                        o, n = ROWS_A[name]
                        sp.dma_start(rowA[o:o + n, :], src).then_inc(s_row, 16)
                    sp.dma_start(rowB[:], d["conv_qkv"][0].rearrange("a (n p) -> (a n) p", p=P)).then_inc(s_row, 16)
                    sp.dma_start(rowC[:], d["conv_ffn"][0].rearrange("a b (n p) -> (a b n) p", p=P)
                                 .rearrange("(j r) p -> r j p", j=2)).then_inc(s_row, 16)
                    for j in range(2):
                        sp.sem_inc(ring.used[j], 1)
                    with sp.Fori(0, 6) as i:
                        for j in range(2):
                            ring.load(sp, j, w_v[:, :, bass.ds(i * 1024 + j * 512, 512)], i)

                @block.gpsimd
                def _(pool):
                    nc.gpsimd.memset(half[:], -0.5)
                    nc.gpsimd.memset(small[:, 0, :], EPS)
                    nc.gpsimd.memset(small[:, 1, :], HE * EPS)
                    nc.gpsimd.memset(small[:, 2, :], HE ** -0.5)

                @block.scalar
                def _(act):
                    for i, src in enumerate((d["b_ada"][0:1, 2 * DM:3 * DM], d["b_ada"][0:1, 5 * DM:6 * DM],
                                             d["norm_post_mix"], d["norm_post_ffn"])):
                        act.dma_start(grow[:, i, :], src.broadcast_to([P, DM])).then_inc(s_g, 16)
                    act.wait_ge(s_tr, 1)
                    nc.scalar.copy(col[:], bank[0][:, 0:97]).then_inc(s_col, 1)
                    nc.scalar.copy(colconv[:], bank[0][:, 128:200]).then_inc(s_col, 1)
                    nc.scalar.copy(colffn[:], bank[0][:, 256:454]).then_inc(s_col, 1)
                    nc.scalar.activation(cs[:, :, 0], bank[0][:, 81:89], ACT.Silu).then_inc(s_col, 1)
                    nc.scalar.activation(cs[:, :, 1], bank[0][:, 89:97], ACT.Silu).then_inc(s_col, 1)

                @block.tensor
                def _(pe):
                    pe.wait_ge(s_row, 16 * 11)
                    nc.tensor.transpose(bank[0][:, 0:97], rowA[:], ident[0:97, 0:97])
                    nc.tensor.transpose(bank[0][:, 128:200], rowB[:], ident[0:72, 0:72])
                    for j in range(2):
                        last = nc.tensor.transpose(bank[0][:, 256 + 99 * j:355 + 99 * j], rowC[:, j, :], ident[0:99, 0:99])
                    last.then_inc(s_tr, 1)
                    pe.wait_ge(s_cs, 1)
                    for part in range(2):
                        with pe.Fori(0, 2) as i:
                            for j in range(2):
                                ring.wait(pe, j, i + 3 * part)
                                for m in range(4):
                                    o = bank[1][:, bass.ds(i * 16 + 2 * (16 * part + 4 * j + m), 2)]
                                    for k in range(KT):
                                        last = nc.tensor.matmul(o, ring.view(j, [P, KT, 512])[:, k, m * P:(m + 1) * P], cs[:, k, :],
                                                                start=(k == 0), stop=(k == KT - 1))
                                last.then_inc(ring.used[j], 1)
                        for j in range(2):
                            ring.wait(pe, j, 3 * part + 2)
                            for k in range(KT):
                                last = nc.tensor.matmul(bank[2 + 2 * part + j][:], csrep[:, k, :], ring.view(j, [P, KT, 512])[:, k, :],
                                                        start=(k == 0), stop=(k == KT - 1))
                            last.then_inc(ring.used[j], 1)

                @block.vector
                def _(dve):
                    link = Link(dve, s_d)
                    dve.wait_ge(s_col, 5)
                    nc.vector.tensor_copy(csrep[:], cs[:, :, 0:1].broadcast_to([P, KT, P])).then_inc(s_cs, 1)
                    for j in range(2):
                        dve.wait_ge(ring.used[j], 7)
                    b = bank[1][:, 0:64].rearrange("p (m c) -> p m c", c=2)
                    for c in range(2):
                        link(nc.vector.tensor_tensor(modc[:, 0:16, c], b[:, 0:16, c], col[:, 0:16], ALU.add))
                        link(nc.vector.tensor_tensor(modc[:, 16:32, c], b[:, 16:32, c], col[:, 24:40], ALU.add))
                    for v, (w, m, c) in enumerate((("pre_mix", 0, 0), ("pre_mix", 0, 1), ("pre_ffn", 16, 0))):
                        o, n = ROWS_A[w]
                        link(nc.vector.tensor_copy(shf[:, v, :], modc[:, m:m + 8, c]))
                        link(nc.vector.scalar_tensor_tensor(wsc[:, v, :], modc[:, m + 8:m + 16, c], 1.0, col[:, o:o + n],
                                                            ALU.add, ALU.mult))
                    dve.wait_ge(s_g, 64)
                    for part in range(2):
                        for j in range(2):
                            c = slice(512 * j, 512 * j + 512)
                            link(nc.vector.tensor_tensor(gtrow[:, part, c], bank[2 + 2 * part + j][:], grow[:, part, c], ALU.add))
                            link(nc.vector.tensor_tensor(gtrow[:, part, c], gtrow[:, part, c], grow[:, 2 + part, c], ALU.mult))
        ring.passed(6, 6)
        if dbg is not None and upto == 1:
            dbg("gtrow", gtrow[:]); dbg("wsc", wsc[:]); dbg("shf", shf[:]); dbg("colffn", colffn[:])


        if upto <= 1:
            return

        s_ss, s_rs, s_xn, s_tp, s_he, s_ld = map(sem, "norm_sums norm_rstd normed norm_transposed norm_stored norm_loaded".split())
        norm_n = {"ss": 0, "rs": 0, "xn": 0, "tp": 0, "ev": [0, 0], "ld": 0}
        s_hev = [sem("norm_stored_act"), sem("norm_stored_dve")]

        def norm_stage(name, srcs, hT, prefetch=None):
            nb = sum(s[0].shape[1] for s in srcs)
            blocks = [(s[0], t, u) for u, s in enumerate(srcs) for t in range(s[0].shape[1])]
            jobs = [(u, k) for u in range(len(srcs)) for k in range(KT)]
            first = [sum(s[0].shape[1] for s in srcs[:u]) for u in range(len(srcs))]
            z = norm_n
            with ExitStack() as ph:
                xn = sb(ph, name + "_normed", [P, nb, DM])
                ss = sb(ph, name + "_sums", [P, 3, nb])
                with nc.Block() as block:
                    @block.sync
                    def _(sp):
                        if prefetch:
                            prefetch(sp)

                    @block.scalar
                    def _(act):
                        for n, (src, t, u) in enumerate(blocks):
                            nc.scalar.activation(xn[:, n, :], src[:, t, :], ACT.Square, accum_out=ss[:, 0, n:n + 1]).then_inc(s_ss, 1)
                        for n, (u, k) in enumerate(jobs):
                            if n % 2 == 0:
                                src, c, sc, sh = srcs[u]
                                w = src.shape[1] * P
                                act.wait_ge(s_tp, z["tp"] + n + 1)
                                nc.scalar.activation(hT[:, k, c:c + w], bank[n % 8][:, 0:w], ACT.Identity,
                                                     scale=sc[:, k:k + 1],
                                                     bias=sh[:, k:k + 1] if sh is not None else 0.0).then_inc(s_hev[0], 1)

                    @block.gpsimd
                    def _(pool):
                        pool.wait_ge(s_ss, z["ss"] + nb)
                        nc.gpsimd.tensor_scalar(ss[:, 1, :], ss[:, 0, :], 1.0 / DM, EPS, ALU.mult, ALU.add).then_inc(s_rs, 1)
                        pool.wait_ge(s_rs, z["rs"] + 1)
                        nc.gpsimd.tensor_tensor(ss[:, 2, :], ss[:, 1, :], half[:, 0:nb], ALU.pow).then_inc(s_rs, 1)

                    @block.vector
                    def _(dve):
                        dve.wait_ge(s_rs, z["rs"] + 2)
                        for n, (src, t, u) in enumerate(blocks):
                            nc.vector.tensor_scalar(xn[:, n, :], src[:, t, :], ss[:, 2, n:n + 1], None, ALU.mult).then_inc(s_xn, 1)
                        for n, (u, k) in enumerate(jobs):
                            if n % 2 == 1:
                                src, c, sc, sh = srcs[u]
                                w = src.shape[1] * P
                                dve.wait_ge(s_tp, z["tp"] + n + 1)
                                nc.vector.tensor_scalar(hT[:, k, c:c + w], bank[n % 8][:, 0:w], sc[:, k:k + 1],
                                                        sh[:, k:k + 1] if sh is not None else None, ALU.mult,
                                                        ALU.add if sh is not None else ALU.bypass).then_inc(s_hev[1], 1)

                    @block.tensor
                    def _(pe):
                        for n, (u, k) in enumerate(jobs):
                            nt = srcs[u][0].shape[1]
                            if n >= 8:
                                pe.wait_ge(s_hev[n % 2], z["ev"][n % 2] + (n - 8) // 2 + 1)
                            for t in range(nt):
                                if n == 0 or (u == 1 and k == 0):
                                    pe.wait_ge(s_xn, z["xn"] + first[u] + t + 1)
                                last = nc.tensor.transpose(bank[n % 8][:, t * P:(t + 1) * P],
                                                           xn[:, first[u] + t, k * P:(k + 1) * P], ident)
                            last.then_inc(s_tp, 1)
            z["ss"] += nb
            z["rs"] += 2
            z["xn"] += nb
            z["tp"] += len(jobs)
            for e in range(2):
                z["ev"][e] += len(jobs) // 2

        def post_norm(part, ph, name):
            ss = sb(ph, name + "_post_sums", [P, 3, 8])
            junk = sb(ph, name + "_post_squares_buf", [P, 2, 512])
            s_sq, s_rs, s_o = sem(name + "_post_squares"), sem(name + "_post_rstd"), sem(name + "_post_out")

            def act_(act, ready):
                for b in range(8):
                    ready(act, b)
                    if b >= 2:
                        act.wait_ge(s_sq, b - 1)
                    nc.scalar.activation(junk[:, b % 2], bank[b][:], ACT.Square, accum_out=ss[:, 0, b:b + 1]).then_inc(s_sq, 1)

            def pool_(pool):
                pool.wait_ge(s_sq, 8)
                v = ss[:, 0, :].rearrange("p (t a) -> p t a", a=2)
                nc.gpsimd.tensor_tensor(ss[:, 1, 0:4], v[:, :, 0], v[:, :, 1], ALU.add).then_inc(s_rs, 1)
                pool.wait_ge(s_rs, 1)
                nc.gpsimd.tensor_scalar(ss[:, 1, 0:4], ss[:, 1, 0:4], 1.0 / DM, EPS, ALU.mult, ALU.add).then_inc(s_rs, 1)
                pool.wait_ge(s_rs, 2)
                nc.gpsimd.tensor_tensor(ss[:, 2, 0:4], ss[:, 1, 0:4], half[:, 0:4], ALU.pow).then_inc(s_rs, 1)

            def dve_(dve):
                dve.wait_ge(s_rs, 3)
                for b in range(8):
                    t, c = b // 2, slice(512 * (b % 2), 512 * (b % 2) + 512)
                    if b >= 2:
                        dve.wait_ge(s_o, 2 * b - 2)
                    nc.vector.scalar_tensor_tensor(junk[:, b % 2], bank[b][:], ss[:, 2, t:t + 1], gtrow[:, part, c],
                                                   ALU.mult, ALU.mult).then_inc(s_o, 1)
                    dve.wait_ge(s_o, 2 * b + 1)
                    nc.vector.tensor_tensor(xt[:, t, c], xt[:, t, c], junk[:, b % 2], ALU.add).then_inc(s_o, 1)

            return act_, pool_, dve_

        def first_mixer():
            delta = es.enter_context(ExitStack())
            hT = sb(delta, "h_fm", [P, KT, SEQ + CTX])
            win = d["w_in"][0].rearrange("(k p) n -> p k n", p=P)

            def head_slab(sp, h):
                for j, o in enumerate((OFF_Q, OFF_K, OFF_V, OFF_Z)):
                    src = win[:, :, bass.ds(h * P + o, P)]
                    sp.dma_start(ring.view(0, [P, 4, KT, P])[:, j], src).then_inc(ring.ready[0], 16)

            with ExitStack() as ph:
                ct = sb(ph, "ctx_tm", [P, TC, DM])
                x0 = sb(ph, "x_in", [P, TX, DM])
                with nc.Block() as block:
                    @block.sync
                    def _(sp):
                        sp.dma_start(ct[:], d["ctx"][0].rearrange("(t p) n -> p t n", p=P)).then_inc(s_ld, 16)
                        sp.dma_start(x0[:], d["x"][0].rearrange("(t p) n -> p t n", p=P)).then_inc(s_ld, 16)
                        sp.wait_ge(s_ld, 32)
                norm_stage("mix", [(x0, 0, wsc[:, 0, :], shf[:, 0, :]), (ct, SEQ, wsc[:, 1, :], shf[:, 1, :])], hT)
            if dbg is not None and upto == 2:
                dbg("hT", hT[:]); return

            NU = 2 * TT
            gu = sb(delta, "log_decay", [P, HD, NU])
            bu = sb(delta, "beta", [P, HD, NU])
            eg = sb(delta, "exp_decay_from_start", [P, HD, NU])
            et = sb(delta, "exp_decay_to_end", [P, HD, NU])
            el = sb(delta, "exp_decay_of_chunk", [P, HD, NU])
            lev = sb(delta, "level_masks", [P, LEVELS, 2, P])
            with ExitStack() as ph:
                wba = sb(ph, "w_beta_alpha", [P, KT, 32])
                rows = sb(ph, "decay_rows", [P, 2, 16])
                t = sb(ph, "decay_work", [P, 8, TT, 16])
                e_ld, e_mm, e_dv, e_ac, e_pl = map(sem, "decay_loads decay_products decay_dve decay_act decay_cumsum".split())
                with nc.Block() as block:
                    @block.sync
                    def _(sp):
                        sp.dma_start(wba[:], win[:, :, OFF_B:OFF_G]).then_inc(e_ld, 16)
                        sp.dma_start(rows[:, 0, :], d["a_log"].rearrange("a b c -> a (b c)").broadcast_to([P, 16])).then_inc(e_ld, 16)
                        sp.dma_start(rows[:, 1, :], d["dt_bias"].rearrange("a b c -> a (b c)").broadcast_to([P, 16])).then_inc(e_ld, 16)
                        sp.dma_start(lev[:], d["k_lev"]).then_inc(e_ld, 16)
                        sp.wait_ge(ring.used[0], ring.n[0] + 1)
                        head_slab(sp, 0)

                    @block.tensor
                    def _(pe):
                        pe.wait_ge(e_ld, 64)
                        for c in range(TT):
                            for k in range(KT):
                                last = nc.tensor.matmul(bank[0][:, 32 * c:32 * c + 32], hT[:, k, c * P:(c + 1) * P], wba[:, k, :],
                                                        start=(k == 0), stop=(k == KT - 1))
                        last.then_inc(e_mm, 1)
                        pe.wait_ge(e_dv, 13)
                        g = gu[:].rearrange("p h u -> p (h u)")
                        for n, m in enumerate((m_le, m_ge, m_gt, m_lt, m_ones)):
                            last = nc.tensor.matmul(bank[1][:, n * 96:(n + 1) * 96], m, g, start=True, stop=True)
                        last.then_inc(e_mm, 1)

                    @block.scalar
                    def _(act):
                        act.wait_ge(e_dv, 1)
                        b = bank[0][:, 0:192].rearrange("p (c n) -> p c n", n=32)
                        nc.scalar.activation(t[:, 0], b[:, :, 0:16], ACT.Sigmoid).then_inc(e_ac, 1)
                        nc.scalar.activation(rows[:, 0, :], rows[:, 0, :], ACT.Exp).then_inc(e_ac, 1)
                        act.wait_ge(e_dv, 3)
                        nc.scalar.activation(t[:, 3], t[:, 2], ACT.Exp).then_inc(e_ac, 1)
                        act.wait_ge(e_ac, 3)
                        nc.scalar.activation(t[:, 4], t[:, 3], ACT.Ln, bias=1.0).then_inc(e_ac, 1)
                        act.wait_ge(e_mm, 2)
                        b = bank[1][:, 0:480].rearrange("p (n h g d c) -> p n h g d c", n=5, h=HD, g=3, d=2)
                        v = lambda x: x[:].rearrange("p h (g d c) -> p h g d c", g=3, d=2)
                        for dr in range(2):
                            nc.scalar.activation(v(eg)[:, :, :, dr], b[:, dr, :, :, dr], ACT.Exp)
                            nc.scalar.activation(v(et)[:, :, :, dr], b[:, 2 + dr, :, :, dr], ACT.Exp)
                        nc.scalar.activation(el[:].rearrange("p h u -> p (h u)"), bank[1][:, 384:480], ACT.Exp).then_inc(e_ac, 1)

                    @block.vector
                    def _(dve):
                        link = Link(dve, e_dv)
                        dve.wait_ge(e_mm, 1)
                        b = bank[0][:, 0:192].rearrange("p (c n) -> p c n", n=32)
                        row = lambda r: rows[:, r:r + 1, :].broadcast_to([P, TT, 16])
                        link(nc.vector.tensor_tensor(t[:, 1], b[:, :, 16:32], row(1), ALU.add))
                        link(nc.vector.tensor_scalar(t[:, 5], t[:, 1], -1.0, None, ALU.mult))
                        link(nc.vector.tensor_tensor(t[:, 2], t[:, 1], t[:, 5], ALU.min))
                        dve.wait_ge(e_ac, 4)
                        link(nc.vector.tensor_scalar(t[:, 6], t[:, 3], 1.0, None, ALU.add))
                        link(nc.vector.tensor_scalar(t[:, 6], t[:, 6], -1.0, None, ALU.add))
                        link(nc.vector.tensor_tensor(t[:, 6], t[:, 3], t[:, 6], ALU.subtract))
                        link(nc.vector.tensor_tensor(t[:, 6], t[:, 4], t[:, 6], ALU.add))
                        link(nc.vector.scalar_tensor_tensor(t[:, 6], t[:, 1], 0.0, t[:, 6], ALU.max, ALU.add))
                        link(nc.vector.scalar_tensor_tensor(t[:, 7], t[:, 6], -1.0, row(0), ALU.mult, ALU.mult))
                        for dst, src in ((bu, 0), (gu, 7)):
                            s = t[:, src].rearrange("p (g c) n -> p n g c", g=3)
                            v = dst[:].rearrange("p h (g d c) -> p h g d c", g=3, d=2)
                            for dr in range(2):
                                for g in range(3):
                                    last = nc.vector.tensor_copy(v[:, :, g, dr], s[:, dr * HD:(dr + 1) * HD, g])
                                link(last)
            ring.passed(0, 0)
            if dbg is not None and upto == 3:
                dbg("gu", gu[:]); dbg("bu", bu[:]); dbg("eg", eg[:]); dbg("et", et[:]); dbg("el", el[:]); return

            oT = sb(delta, "mix_out_fm", [P, HD, SEQ])
            W3 = SEQ + 2 + CTX
            with ExitStack() as ph:
                dsem = ph.enter_context(local_sems())
                cin = sb(ph, "conv_in", [P, 3, W3 + 2])
                y = sb(ph, "conv_out", [P, 3, W3])
                zs = sb(ph, "z_silu", [P, SEQ])
                qk = sb(ph, "qk_tm", [P, TX + TT, P])
                vt = sb(ph, "v_tm", [P, TT, P])
                sqr = sb(ph, "squares_or_out", [P, TX + TT, P])
                qn = sb(ph, "qk_normed", [P, TX + TT, P])
                ns = sb(ph, "norm_work", [P, 4, TX + TT])
                qkT = sb(ph, "qk_fm", [P, TX + TT, P])
                xf = xt[:].rearrange("p t n -> p (t n)")
                R = xf[:, 0:2560].rearrange("p (u n) -> p u n", u=20)
                bm = xf[:, 2560:4096].rearrange("p (u n) -> p u n", u=12)
                D = sb(ph, "decay_units", [P, 12, P])
                DT = sb(ph, "decay_units_t", [P, 8, P])
                L = sb(ph, "l_units", [P, 12, P])
                X = sb(ph, "inverse", [P, 12, P])
                Y = sb(ph, "inverse_t", [P, 12, P])
                Ts = sb(ph, "level_product", [P, 12, P])
                S = sb(ph, "state", [P, 2, 2, P])
                VN = sb(ph, "v_new", [P, 2, 2, P])
                PT, QeT, NW, oacc = DT, L, X, sqr
                Ke, Qe, Kt = R[:, 0:12, :], R[:, 12:20, :], bm
                units = lambda a, n=3: a[:, 0:4 * n, :].rearrange("p (g d c) n -> p g d c n", g=n, d=2)
                per_unit = lambda a, h, dr, n=3: (a[:, bass.ds(h, 1), :].rearrange("p a (g d c) -> p (a g) d c", g=3, d=2)
                                                  [:, 0:n, dr, :].unsqueeze(3).broadcast_to([P, n, 2, P]))
                mask = lambda m, n=3: m.rearrange("p (a b n) -> p a b n", a=1, b=1).broadcast_to([P, n, 2, P])
                grp = lambda b: b[:].rearrange("p (u n) -> p u n", u=4)
                bankg = lambda b: b[:].rearrange("p (d c n) -> p d c n", d=2, c=2)

                class Event:

                    def __init__(self, name, per):
                        self.s, self.per = dsem("dn_" + name), per

                    def wait(self, eng, h, n):
                        eng.wait_ge(self.s, h * self.per + n)

                    def last(self, eng, h):
                        eng.wait_ge(self.s, h * self.per)

                ev = {n: Event(n, k) for n, k in dict(
                    projected=5, conv_in_filled=5, z_ready=1, conv_done=3, conv_silu=3, tm_turned=4, tm_stored=4,
                    squared=1, qk_sums=1, qk_rstd=3, qk_scaled=1, fm_turned=3, fm_stored=3, steps_ready=4, decay_products=5, decay_exp=5,
                    beta_masked=2, decay_masked=2, decay_masked_t=2, kk_products=3, l_ready=3, p_ready=2, x_first=6, y_first=3, y_stored=3,
                    level_t=18, level_ts=18, level_dy=18, level_y=18, level_x_turned=15, level_x=15,
                    y_beta=3, k_scaled=6, q_turned=2, q_stored=2, w_products=3, w_stored=3,
                    v_products=6, v_stored=6, o_products=4, o_stored=4, s_products=6, s_stored=6,
                    o_squared=1, o_sums=1, o_rstd=2, o_normed=1, o_turned=1, o_gated=1).items()}
                s_chain = dsem("delta_dve_chain")
                inc = lambda ins, n: ins.then_inc(ev[n].s, 1)
                STEPS = [(4, 5), (5, 4), (0, 3), (1, 2), (2, 1), (3, 0)]
                unit = lambda c, dr: (c // 2) * 4 + dr * 2 + c % 2
                VB, OB, SB = (3, 4), (5, 0), (6, 7)
                turned = ((0, 5), (4, 6), (0, 7))
                with nc.Block() as block:
                    @block.sync
                    def _(sp):
                        with sp.Fori(1, HD) as h:
                            sp.wait_ge(ev["projected"].s, h * 5)
                            head_slab(sp, h)
                        sp.wait_ge(ev["projected"].s, 5 * HD)
                        sp.sem_inc(ring.used[0], 4 * HD)

                    @block.tensor
                    def _(pe):
                        with pe.Fori(0, HD) as h:
                            w = ring.view(0, [P, 4, KT, P])
                            pe.wait_ge(ring.ready[0], h * 64 + (16 * ring.n[0] + 64))
                            ev["o_gated"].last(pe, h)
                            for b, j, cols, o in ((0, 0, slice(0, SEQ), 0), (1, 1, slice(0, SEQ), 0), (3, 2, slice(0, SEQ), 0),
                                                  (2, 1, slice(SEQ, SEQ + CTX), 0), (2, 2, slice(SEQ, SEQ + CTX), CTX), (4, 3, slice(0, SEQ), 0)):
                                n = cols.stop - cols.start
                                for k in range(KT):
                                    last = nc.tensor.matmul(bank[b][:, o:o + n], w[:, j, k, :], hT[:, k, cols],
                                                            start=(k == 0), stop=(k == KT - 1))
                                if (b, j) != (2, 1):
                                    last = inc(last, "projected")
                            for j in range(3):
                                ev["conv_silu"].wait(pe, h, j + 1)
                                b = turned[j][1]
                                for t in range(TX):
                                    last = nc.tensor.transpose(bank[b][:, t * P:(t + 1) * P], y[:, j, t * P:(t + 1) * P], ident)
                                inc(last, "tm_turned")
                            ev["conv_in_filled"].wait(pe, h, 1)
                            for j in (1, 2):
                                for t in range(TC):
                                    o = SEQ + 2 + t * P
                                    last = nc.tensor.transpose(bank[0][:, ((j - 1) * 2 + t) * P:((j - 1) * 2 + t + 1) * P], y[:, j, o:o + P], ident)
                            inc(last, "tm_turned")
                            ev["qk_scaled"].wait(pe, h, 1)
                            ev["conv_in_filled"].wait(pe, h, 5)
                            for n, (b, t0, nt) in enumerate(((1, 0, 4), (2, 4, 4), (3, 8, 2))):
                                for t in range(nt):
                                    last = nc.tensor.transpose(bank[b][:, t * P:(t + 1) * P], qn[:, t0 + t, :], ident)
                                inc(last, "fm_turned")
                            ev["steps_ready"].wait(pe, h, 4)
                            ev["z_ready"].wait(pe, h, 1)
                            ev["tm_stored"].wait(pe, h, 4)
                            for n, b in enumerate((4, 5, 6, 7, 0)):
                                u0 = 4 * n
                                for dr in range(2):
                                    m = ((m_le, m_ge), (m_gt, m_lt))[n // 3][dr]
                                    last = nc.tensor.matmul(bank[b][:, 256 * dr:256 * dr + 256], m, R[:, u0 + 2 * dr:u0 + 2 * dr + 2, :], start=True, stop=True)
                                inc(last, "decay_products")
                            ev["fm_stored"].wait(pe, h, 3)
                            for n, (b, cs_, qo) in enumerate(((1, (0, 1, 2, 3), 4), (2, (4, 5), 4), (3, (0, 1, 2, 3), 0))):
                                for i, c in enumerate(cs_):
                                    last = nc.tensor.matmul(bank[b][:, i * P:(i + 1) * P], qkT[:, 4 + c, :], qkT[:, qo + c, :], start=True, stop=True)
                                inc(last, "kk_products")
                            for g in range(3):
                                ev["decay_exp"].wait(pe, h, 3) if g == 0 else None
                                ev["x_first"].wait(pe, h, 2 * g + 2)
                                for i in range(4):
                                    last = nc.tensor.transpose(bank[4 + g][:, i * P:(i + 1) * P], X[:, 4 * g + i, :], ident)
                                inc(last, "y_first")
                            ev["decay_exp"].wait(pe, h, 5)
                            ev["p_ready"].wait(pe, h, 2)
                            for n in range(1, LEVELS):
                                for g in range(3):
                                    if n == 1:
                                        ev["y_stored"].wait(pe, h, g + 1)
                                    else:
                                        ev["level_x"].wait(pe, h, 3 * (n - 2) + g + 1)
                                    for i in range(4):
                                        u = 4 * g + i
                                        last = nc.tensor.matmul(bank[g][:, i * P:(i + 1) * P], L[:, u, :], Y[:, u, :], start=True, stop=True)
                                    inc(last, "level_t")
                                for g in range(3):
                                    ev["level_ts"].wait(pe, h, 3 * (n - 1) + g + 1)
                                    for i in range(4):
                                        u = 4 * g + i
                                        last = nc.tensor.matmul(bank[4 + g][:, i * P:(i + 1) * P], X[:, u, :], Ts[:, u, :], start=True, stop=True)
                                    inc(last, "level_dy")
                                if n < LEVELS - 1:
                                    for g in range(3):
                                        ev["level_y"].wait(pe, h, 3 * (n - 1) + g + 1)
                                        for i in range(4):
                                            u = 4 * g + i
                                            last = nc.tensor.transpose(bank[g][:, i * P:(i + 1) * P], Y[:, u, :], ident)
                                        inc(last, "level_x_turned")
                            ev["k_scaled"].wait(pe, h, 6)
                            for n, b in enumerate((3, 7)):
                                for i in range(4):
                                    last = nc.tensor.transpose(bank[b][:, i * P:(i + 1) * P], Qe[:, 4 * n + i, :], ident)
                                inc(last, "q_turned")
                            for g in range(3):
                                ev["y_beta"].wait(pe, h, g + 1)
                                for i in range(4):
                                    u = 4 * g + i
                                    last = nc.tensor.matmul(bank[g][:, i * P:(i + 1) * P], Ke[:, u, :], Y[:, u, :], start=True, stop=True)
                                inc(last, "w_products")
                            ev["q_stored"].wait(pe, h, 2)
                            no = 0
                            for s, cd in enumerate(STEPS):
                                vb, sbk = bank[VB[s % 2]], bank[SB[s % 2]]
                                if s >= 2:
                                    ev["v_stored"].wait(pe, h, s - 1)
                                if s > 0:
                                    ev["w_stored"].wait(pe, h, 3) if s == 1 else None
                                    ev["s_stored"].wait(pe, h, s)
                                for dr, c in enumerate(cd):
                                    u = unit(c, dr)
                                    last = nc.tensor.matmul(vb[:, dr * P:(dr + 1) * P], Y[:, u, :], vt[:, c, :], start=True, stop=(s == 0))
                                    if s > 0:
                                        last = nc.tensor.matmul(vb[:, dr * P:(dr + 1) * P], NW[:, u, :], S[:, s % 2, dr, :], start=False, stop=True)
                                inc(last, "v_products")
                                ev["v_stored"].wait(pe, h, s + 1)
                                if s == 0:
                                    ev["level_y"].wait(pe, h, 18)
                                for dr, c in enumerate(cd):
                                    last = nc.tensor.matmul(sbk[:, dr * P:(dr + 1) * P], Kt[:, unit(c, dr), :], VN[:, s % 2, dr, :], start=True, stop=True)
                                inc(last, "s_products")
                                if s >= 2:
                                    ob = bank[OB[no % 2]]
                                    if no >= 2:
                                        ev["o_stored"].wait(pe, h, no - 1)
                                    for dr, c in enumerate(cd):
                                        u = unit(c, dr)
                                        nc.tensor.matmul(ob[:, dr * P:(dr + 1) * P], QeT[:, u, :], S[:, s % 2, dr, :], start=True, stop=False)
                                        last = nc.tensor.matmul(ob[:, dr * P:(dr + 1) * P], PT[:, u, :], VN[:, s % 2, dr, :], start=False, stop=True)
                                    inc(last, "o_products")
                                    no += 1
                            ev["o_normed"].wait(pe, h, 1)
                            for t in range(TX):
                                last = nc.tensor.transpose(bank[1][:, t * P:(t + 1) * P], qn[:, t, :], ident)
                            inc(last, "o_turned")

                    @block.scalar
                    def _(act):
                        act.wait_ge(s_chain, 1)
                        with act.Fori(0, HD) as h:
                            ev["o_gated"].last(act, h)
                            n = 0
                            for b, j, o, src in ((0, 0, 1, 0), (1, 1, 1, 0), (3, 2, 1, 0), (2, 1, SEQ + 3, 0), (2, 2, SEQ + 3, CTX)):
                                w = CTX if b == 2 else SEQ
                                if not (b == 2 and src):
                                    n += 1
                                    ev["projected"].wait(act, h, n)
                                inc(nc.scalar.copy(cin[:, j, o:o + w], bank[b][:, src:src + w]), "conv_in_filled")
                            ev["projected"].wait(act, h, 5)
                            inc(nc.scalar.activation(zs[:], bank[4][:], ACT.Silu), "z_ready")
                            ev["conv_done"].wait(act, h, 1)
                            inc(nc.scalar.activation(y[:, 0, 0:SEQ], y[:, 0, 0:SEQ], ACT.Silu), "conv_silu")
                            for j in (1, 2):
                                ev["conv_done"].wait(act, h, j + 1)
                                inc(nc.scalar.activation(y[:, j, :], y[:, j, :], ACT.Silu), "conv_silu")
                            for j, dst in enumerate((qk[:, 0:4, :], qk[:, 4:8, :], vt[:, 0:4, :])):
                                ev["tm_turned"].wait(act, h, j + 1)
                                inc(nc.scalar.copy(dst, grp(bank[turned[j][1]])), "tm_stored")
                            ev["tm_turned"].wait(act, h, 4)
                            nc.scalar.copy(qk[:, 8:10, :], grp(bank[0])[:, 0:2])
                            inc(nc.scalar.copy(vt[:, 4:6, :], grp(bank[0])[:, 2:4]), "tm_stored")
                            for n, (b, t0, nt) in enumerate(((1, 0, 4), (2, 4, 4), (3, 8, 2))):
                                ev["fm_turned"].wait(act, h, n + 1)
                                inc(nc.scalar.copy(qkT[:, t0:t0 + nt, :], grp(bank[b])[:, 0:nt]), "fm_stored")
                            for n, b in enumerate((4, 5, 6, 7, 0)):
                                ev["decay_products"].wait(act, h, n + 1)
                                dst = D[:, 4 * n:4 * n + 4, :] if n < 3 else DT[:, 4 * n - 12:4 * n - 8, :]
                                inc(nc.scalar.activation(dst, grp(bank[b]), ACT.Exp), "decay_exp")
                            for g in range(3):
                                ev["y_first"].wait(act, h, g + 1)
                                inc(nc.scalar.copy(Y[:, 4 * g:4 * g + 4, :], grp(bank[4 + g])), "y_stored")
                            for n in range(1, LEVELS - 1):
                                for g in range(3):
                                    ev["level_x_turned"].wait(act, h, 3 * (n - 1) + g + 1)
                                    inc(nc.scalar.copy(X[:, 4 * g:4 * g + 4, :], grp(bank[g])), "level_x")
                            ev["level_t"].wait(act, h, 18)
                            for n, b in enumerate((3, 7)):
                                ev["q_turned"].wait(act, h, n + 1)
                                inc(nc.scalar.copy(QeT[:, 4 * n:4 * n + 4, :], grp(bank[b])), "q_stored")
                            ev["level_dy"].wait(act, h, 18)
                            for g in range(3):
                                ev["w_products"].wait(act, h, g + 1)
                                inc(nc.scalar.mul(NW[:, 4 * g:4 * g + 4, :], grp(bank[g]), -1.0), "w_stored")
                            for s in range(6):
                                ev["v_products"].wait(act, h, s + 1)
                                if s >= 2:
                                    ev["s_products"].wait(act, h, s - 1)
                                if s >= 4:
                                    ev["o_products"].wait(act, h, s - 3)
                                inc(nc.scalar.copy(VN[:, s % 2], bank[VB[s % 2]][:, 0:256].rearrange("p (d n) -> p d n", d=2)), "v_stored")

                    @block.gpsimd
                    def _(pool):
                        with pool.Fori(0, HD) as h:
                            ev["o_gated"].last(pool, h)
                            for dr in range(2):
                                inc(nc.gpsimd.tensor_tensor(units(R)[:, :, dr], per_unit(gu, h, dr), mask((m_gt, m_lt)[dr]), ALU.mult), "steps_ready")
                            rt = R[:, 12:20, :].rearrange("p (g d c) n -> p g d c n", g=2, d=2)
                            for dr in range(2):
                                inc(nc.gpsimd.tensor_tensor(rt[:, :, dr], per_unit(gu, h, dr, 2), mask((m_le, m_ge)[dr], 2), ALU.mult), "steps_ready")
                            for dr in range(2):
                                inc(nc.gpsimd.tensor_tensor(units(bm)[:, :, dr], per_unit(bu, h, dr), mask((m_gt, m_lt)[dr]), ALU.mult), "beta_masked")
                            ev["qk_sums"].wait(pool, h, 1)
                            inc(nc.gpsimd.tensor_tensor(ns[:, 1, :], ns[:, 0, :], small[:, 0, 0:TX + TT], ALU.add), "qk_rstd")
                            ev["qk_rstd"].wait(pool, h, 1)
                            inc(nc.gpsimd.tensor_tensor(ns[:, 2, :], ns[:, 1, :], half[:, 0:TX + TT], ALU.pow), "qk_rstd")
                            ev["qk_rstd"].wait(pool, h, 2)
                            inc(nc.gpsimd.tensor_tensor(ns[:, 2, 0:4], ns[:, 2, 0:4], small[:, 2, 0:4], ALU.mult), "qk_rstd")
                            ev["beta_masked"].wait(pool, h, 2)
                            for dr in range(2):
                                ev["decay_exp"].wait(pool, h, 3)
                                inc(nc.gpsimd.tensor_tensor(units(D)[:, :, dr], units(D)[:, :, dr], units(bm)[:, :, dr], ALU.mult), "decay_masked")
                            for dr in range(2):
                                ev["decay_exp"].wait(pool, h, 5)
                                inc(nc.gpsimd.tensor_tensor(units(DT, 2)[:, :, dr], units(DT, 2)[:, :, dr], mask((m_le, m_ge)[dr], 2), ALU.mult), "decay_masked_t")
                            ev["qk_scaled"].wait(pool, h, 1)
                            ev["decay_products"].wait(pool, h, 5)
                            ev["decay_masked"].wait(pool, h, 2)
                            kv = qn[:, 4:10, :].rearrange("p (g c) n -> p g c n", g=3)
                            qv = qn[:, 0:4, :].rearrange("p (g c) n -> p g c n", g=2)
                            for dr in range(2):
                                inc(nc.gpsimd.tensor_tensor(units(Qe, 2)[:, :, dr], qv, per_unit(eg, h, dr, 2), ALU.mult), "k_scaled")
                            for dr in range(2):
                                inc(nc.gpsimd.tensor_tensor(units(Ke)[:, :, dr], kv, per_unit(eg, h, dr), ALU.mult), "k_scaled")
                                inc(nc.gpsimd.tensor_tensor(units(Kt)[:, :, dr], kv, per_unit(et, h, dr), ALU.mult), "k_scaled")
                            ev["o_sums"].wait(pool, h, 1)
                            inc(nc.gpsimd.tensor_tensor(ns[:, 1, 0:4], ns[:, 0, 0:4], small[:, 1, 0:4], ALU.add), "o_rstd")
                            ev["o_rstd"].wait(pool, h, 1)
                            inc(nc.gpsimd.tensor_tensor(ns[:, 2, 0:4], ns[:, 1, 0:4], half[:, 0:4], ALU.pow), "o_rstd")

                    @block.vector
                    def _(dve):
                        nc.vector.memset(cin[:], 0.0).then_inc(s_chain, 1)
                        dve.wait_ge(s_chain, 1)
                        with dve.Fori(0, HD) as h:
                            link = Link(dve, s_chain, start=1, turn=h, per=7)
                            link.n = 1
                            for j in range(3):
                                ev["conv_in_filled"].wait(dve, h, (1, 4, 5)[j])
                                w = SEQ if j == 0 else W3
                                tap = lambda a: colconv[:, bass.ds(h + (a * 24 + j * HD), 1)]
                                link(nc.vector.tensor_scalar(y[:, j, 0:w], cin[:, j, 1:1 + w], tap(1), None, ALU.mult))
                                link(nc.vector.scalar_tensor_tensor(y[:, j, 0:w], cin[:, j, 0:w], tap(0), y[:, j, 0:w], ALU.mult, ALU.add))
                                inc(nc.vector.scalar_tensor_tensor(y[:, j, 0:w], cin[:, j, 2:2 + w], tap(2), y[:, j, 0:w], ALU.mult, ALU.add), "conv_done")
                            ev["tm_stored"].wait(dve, h, 4)
                            inc(nc.vector.tensor_tensor(sqr[:], qk[:], qk[:], ALU.mult), "squared")
                            ev["squared"].wait(dve, h, 1)
                            inc(nc.vector.reduce_sum(ns[:, 0, :], sqr[:], axis=AX), "qk_sums")
                            ev["qk_rstd"].wait(dve, h, 3)
                            inc(nc.vector.tensor_tensor(qn[:], qk[:], ns[:, 2, :].unsqueeze(2).broadcast_to([P, TX + TT, P]), ALU.mult), "qk_scaled")
                            ev["decay_masked"].wait(dve, h, 2)
                            for g in range(3):
                                ev["kk_products"].wait(dve, h, 1 if g < 2 else 2)
                                kk = (grp(bank[1])[:, 2 * g:2 * g + 2] if g < 2 else grp(bank[2])[:, 0:2])
                                kk = kk.unsqueeze(1).broadcast_to([P, 2, 2, P])
                                inc(nc.vector.tensor_tensor(units(L)[:, g], kk, units(D)[:, g], ALU.mult), "l_ready")
                            ev["decay_masked_t"].wait(dve, h, 2)
                            ev["kk_products"].wait(dve, h, 3)
                            for g in range(2):
                                kq = grp(bank[3])[:, 2 * g:2 * g + 2].unsqueeze(1).broadcast_to([P, 2, 2, P])
                                inc(nc.vector.tensor_tensor(units(PT, 2)[:, g], kq, units(DT, 2)[:, g], ALU.mult), "p_ready")
                            for g in range(3):
                                ev["l_ready"].wait(dve, h, g + 1)
                                for dr in range(2):
                                    m = lev[:, 0, 1 - dr:2 - dr, :].broadcast_to([P, 2, P])
                                    last = nc.vector.tensor_tensor(units(X)[:, g, dr], units(L)[:, g, dr], m, ALU.mult)
                                inc(last, "x_first")
                                ev["x_first"].wait(dve, h, 2 * g + 1)
                                idb = ident.unsqueeze(1).broadcast_to([P, 4, P])
                                inc(nc.vector.tensor_tensor(X[:, 4 * g:4 * g + 4, :], idb, X[:, 4 * g:4 * g + 4, :], ALU.subtract), "x_first")
                            for n in range(1, LEVELS):
                                for g in range(3):
                                    ev["level_t"].wait(dve, h, 3 * (n - 1) + g + 1)
                                    m = lev[:, n].unsqueeze(2).broadcast_to([P, 2, 2, P])
                                    inc(nc.vector.tensor_tensor(units(Ts)[:, g], bankg(bank[g]), m, ALU.mult), "level_ts")
                                for g in range(3):
                                    ev["level_dy"].wait(dve, h, 3 * (n - 1) + g + 1)
                                    yv = Y[:, 4 * g:4 * g + 4, :]
                                    inc(nc.vector.tensor_tensor(yv, yv, grp(bank[4 + g]), ALU.subtract), "level_y")
                            for g in range(3):
                                ev["level_y"].wait(dve, h, 15 + g + 1)
                                yv = Y[:, 4 * g:4 * g + 4, :]
                                bv = bu[:, bass.ds(h, 1), 4 * g:4 * g + 4].rearrange("p a u -> p (a u)").unsqueeze(2).broadcast_to([P, 4, P])
                                inc(nc.vector.tensor_tensor(yv, yv, bv, ALU.mult), "y_beta")
                            for s, cd in enumerate(STEPS):
                                ev["s_products"].wait(dve, h, s + 1)
                                b = bank[SB[s % 2]]
                                if s >= 1:
                                    ev["v_products"].wait(dve, h, s)
                                for dr, c in enumerate(cd):
                                    src = b[:, dr * P:(dr + 1) * P]
                                    dst = S[:, (s + 1) % 2, dr, :]
                                    if s == 0:
                                        last = nc.vector.tensor_copy(dst, src)
                                    else:
                                        if dr == 0:
                                            ev["s_stored"].wait(dve, h, s)
                                            if s >= 3:
                                                ev["o_products"].wait(dve, h, s - 2)
                                        dec = el[:, bass.ds(h, 1), unit(c, dr)]
                                        last = nc.vector.scalar_tensor_tensor(dst, S[:, s % 2, dr, :], dec, src, ALU.mult, ALU.add)
                                inc(last, "s_stored")
                                if s >= 2:
                                    ev["o_products"].wait(dve, h, s - 1)
                                    ob = bank[OB[s % 2]]
                                    if s >= 4:
                                        ev["o_stored"].wait(dve, h, 2)
                                    for dr, c in enumerate(cd):
                                        src = ob[:, dr * P:(dr + 1) * P]
                                        dst = oacc[:, c, :]
                                        if s < 4:
                                            last = nc.vector.tensor_copy(dst, src)
                                        else:
                                            last = nc.vector.tensor_tensor(dst, dst, src, ALU.add)
                                    inc(last, "o_stored")
                            ev["o_stored"].wait(dve, h, 4)
                            inc(nc.vector.tensor_tensor(sqr[:, 4:8, :], oacc[:, 0:4, :], oacc[:, 0:4, :], ALU.mult), "o_squared")
                            ev["o_squared"].wait(dve, h, 1)
                            inc(nc.vector.reduce_sum(ns[:, 0, 0:4], sqr[:, 4:8, :], axis=AX), "o_sums")
                            ev["o_rstd"].wait(dve, h, 2)
                            inc(nc.vector.tensor_tensor(qn[:, 0:4, :], oacc[:, 0:4, :], ns[:, 2, 0:4].unsqueeze(2).broadcast_to([P, 4, P]), ALU.mult), "o_normed")
                            ev["o_turned"].wait(dve, h, 1)
                            link(nc.vector.tensor_scalar(y[:, 0, 0:SEQ], bank[1][:], colof("dn"), HE ** 0.5, ALU.mult, ALU.mult))
                            inc(nc.vector.tensor_tensor(oT[:, bass.ds(h, 1), :].rearrange("p a n -> p (a n)"), y[:, 0, 0:SEQ], zs[:], ALU.mult), "o_gated")
                            link.start = 1
                            link.end()
                if dbg is not None and upto == 4:
                    for nme, bf in dict(qn=qn, vt=vt, D=D, DT=DT, Y=Y, S=S, oacc=oacc, Kt=Kt, zs=zs).items():
                        dbg(nme, bf[:])
            ring.passed(4 * HD, 0)
            if dbg is not None and upto == 4:
                dbg("oT", oT[:]); return

            with ExitStack() as ph:
                fT = sb(ph, "fourier_in_fm", [P, 4, SEQ])
                fa = sb(ph, "fourier_channels", [P, TX, 4, 2 * P])
                dft = sb(ph, "dft_tokens", [P, 2, TX, SEQ])
                dfc = sb(ph, "dft_channels", [P, 2 * P])
                fo = sb(ph, "fourier_out_fm", [P, 4, SEQ])
                ga = sb(ph, "gates", [P, 2, 4, SEQ])
                mg = sb(ph, "merged_fm", [P, KT, SEQ])
                m_ld, m_f, m_fe, m_pr, m_g, m_yf, m_t, m_m, m_w = map(sem, (
                    "mix_loads fourier_products fourier_stored mix_products gates_ready fourier_gated delta_gated merged mix_out").split())
                wf_v = d["w_fourier"][0].rearrange("(k p) n -> p k n", p=P)
                wd_v = d["w_dn"][0].rearrange("(k p) n -> p k n", p=P)
                wo_v = d["w_out"][0].rearrange("(k p) n -> p k n", p=P)
                post_act, post_pool, post_dve = post_norm(0, ph, "mix")
                with nc.Block() as block:
                    @block.sync
                    def _(sp):
                        ring.load(sp, 0, win[:, :, 0:FW])
                        sp.dma_start(dfc[:], d["k_dft_c"]).then_inc(m_ld, 16)
                        sp.dma_start(dft[:], d["k_dft_t"]).then_inc(m_ld, 16)
                        sp.dma_start(xt[:], d["x"][0].rearrange("(t p) n -> p t n", p=P)).then_inc(m_ld, 16)
                        for i in range(2):
                            ring.load(sp, 1, win[:, :, bass.ds(i * 512 + OFF_G, 512)], i * 2)
                            ring.load(sp, 0, win[:, :, bass.ds(i * 512 + (OFF_G + DM), 512)], i * 2 + 1)
                            ring.load(sp, 1, wf_v[:, :, bass.ds(i * 512, 512)], i * 2 + 1)
                            ring.load(sp, 0, wd_v[:, :, bass.ds(i * 512, 512)], i * 2 + 2)
                        for j in range(2):
                            ring.load(sp, 1 - j, wo_v[:, :, 512 * j:512 * j + 512], 4 + j)

                    @block.tensor
                    def _(pe):
                        ring.wait(pe, 0)
                        w = ring.view(0, [P, KT, 512])
                        for m in range(4):
                            for k in range(KT):
                                last = nc.tensor.matmul(bank[m][:], w[:, k, m * P:(m + 1) * P], hT[:, k, 0:SEQ], start=(k == 0), stop=(k == KT - 1))
                            last.then_inc(m_f, 1)
                        pe.wait_ge(m_ld, 48)
                        pe.wait_ge(m_fe, 4)
                        pe.sem_inc(ring.used[0], 1)
                        for t in range(TX):
                            for g in range(4):
                                last = nc.tensor.matmul(bank[4 + t][:, (g % 2) * 256:(g % 2) * 256 + 256] if g < 2 else
                                                        bank[t][:, (g % 2) * 256:(g % 2) * 256 + 256],
                                                        fT[:, g, t * P:(t + 1) * P], dfc[:], start=True, stop=True)
                                if g % 2:
                                    last.then_inc(m_f, 1)
                        for g in range(4):
                            pe.wait_ge(m_fe, 12)
                            n = 0
                            for t in range(TX):
                                for c in range(2):
                                    last = nc.tensor.matmul(bank[4 + g][:], fa[:, t, g, c * P:(c + 1) * P], dft[:, c, t, :], start=(n == 0), stop=(n == 7))
                                    n += 1
                            last.then_inc(m_f, 1)
                        with pe.Fori(0, 2) as i:
                            for n, (slot, src, nk) in enumerate(((1, hT, KT), (0, hT, KT), (1, fo, 4), (0, oT, KT))):
                                ring.wait(pe, slot, (i * 2, i * 2 + 1, i * 2 + 1, i * 2 + 2)[n])
                                w = ring.view(slot, [P, nk, 512])
                                if n == 0:
                                    pe.wait_ge(m_yf, i * 4)
                                if n == 1:
                                    pe.wait_ge(m_fe, 16)
                                    pe.wait_ge(m_t, i * 4)
                                for m in range(4):
                                    if n >= 2:
                                        pe.wait_ge(m_g, i * 8 + (4 * (n - 2) + m + 1))
                                    for k in range(nk):
                                        last = nc.tensor.matmul(bank[4 * (n % 2) + m][:], w[:, k, m * P:(m + 1) * P], src[:, k, 0:SEQ],
                                                                start=(k == 0), stop=(k == nk - 1))
                                    last.then_inc(m_pr, 1)
                                pe.wait_ge(m_pr, i * 16 + (4 * n + 4))
                                pe.sem_inc(ring.used[slot], 1)
                        pe.wait_ge(m_m, 8)
                        for j in range(2):
                            ring.wait(pe, 1 - j, 4 + j)
                            w = ring.view(1 - j, [P, KT, 512])
                            for t in range(TX):
                                for k in range(KT):
                                    last = nc.tensor.matmul(bank[2 * t + j][:], mg[:, k, t * P:(t + 1) * P], w[:, k, :], start=(k == 0), stop=(k == KT - 1))
                                last.then_inc(m_w, 1)
                            pe.wait_ge(m_w, 4 * j + 4)
                            pe.sem_inc(ring.used[1 - j], 1)

                    @block.scalar
                    def _(act):
                        for m in range(4):
                            act.wait_ge(m_f, m + 1)
                            nc.scalar.copy(fT[:, m, :], bank[m][:]).then_inc(m_fe, 1)
                        for t in range(TX):
                            for a in range(2):
                                act.wait_ge(m_f, 4 + 2 * t + a + 1)
                                b = bank[4 + t] if a == 0 else bank[t]
                                nc.scalar.copy(fa[:, t, 2 * a:2 * a + 2, :], b[:].rearrange("p (g n) -> p g n", g=2)).then_inc(m_fe, 1)
                        for g in range(4):
                            act.wait_ge(m_f, 12 + g + 1)
                            nc.scalar.copy(fo[:, g, :], bank[4 + g][:]).then_inc(m_fe, 1)
                        with act.Fori(0, 2) as i:
                            act.wait_ge(m_m, i * 4)
                            for n in range(2):
                                for m in range(4):
                                    act.wait_ge(m_pr, i * 16 + (4 * n + m + 1))
                                    nc.scalar.activation(ga[:, n, m, :], bank[4 * n + m][:], ACT.Sigmoid).then_inc(m_g, 1)
                        post_act(act, lambda e, b: e.wait_ge(m_w, 8 if b % 2 else b // 2 + 1))

                    @block.gpsimd
                    def _(pool):
                        post_pool(pool)

                    @block.vector
                    def _(dve):
                        with dve.Fori(0, 2) as i:
                            for m in range(4):
                                dve.wait_ge(m_pr, i * 16 + (8 + m + 1))
                                nc.vector.tensor_tensor(ga[:, 0, m, :], ga[:, 0, m, :], bank[m][:], ALU.mult).then_inc(m_yf, 1)
                            for m in range(4):
                                dve.wait_ge(m_pr, i * 16 + (12 + m + 1))
                                nc.vector.tensor_tensor(ga[:, 1, m, :], ga[:, 1, m, :], bank[4 + m][:], ALU.mult).then_inc(m_t, 1)
                                dve.wait_ge(m_t, i * 4 + (m + 1))
                                dve.wait_ge(m_yf, i * 4 + (m + 1))
                                o = mg[:, bass.ds(i * 4 + m, 1), :].rearrange("p a n -> p (a n)")
                                nc.vector.tensor_tensor(o, ga[:, 0, m, :], ga[:, 1, m, :], ALU.add).then_inc(m_m, 1)
                        post_dve(dve)
            ring.passed(6, 5)
            if dbg is not None and upto == 5:
                dbg("x1", xt[:]); return
            delta.close()

        if dbg is None or inject is None:
            first_mixer()
            if upto <= 5:
                return
        else:
            with nc.Block() as block:
                @block.sync
                def _(sp):
                    s_inj = sem("inject")
                    sp.dma_start(xt[:], d["inject"].rearrange("(t p) n -> p t n", p=P)).then_inc(s_inj, 16)
                    sp.wait_ge(s_inj, 16)

        def ffn():
            with ExitStack() as fs:
                gT = sb(fs, "ffn_gated_fm", [P, FT, SEQ])
                wu_v = d["w_up"][0].rearrange("(k p) (a n) -> p k a n", p=P, a=2)
                wd_v = d["w_down"][0].rearrange("(k p) n -> p k n", p=P)

                def up_slab(sp, j, turn):
                    for a in range(2):
                        if a == 0:
                            sp.wait_ge(ring.used[j], turn * 2 + (ring.n[j] + 1))
                        sp.dma_start(ring.view(j, [P, 2, KT, P])[:, a], wu_v[:, :, a, bass.ds(turn * 256 + j * P, P)]).then_inc(ring.ready[j], 16)

                with ExitStack() as ph:
                    h2 = sb(ph, "ffn_h_fm", [P, KT, SEQ])
                    norm_stage("ffn", [(xt, 0, wsc[:, 2, :], shf[:, 2, :])], h2)
                    pad = sb(ph, "ffn_grid", [P, 2, GRID_R + 2, GRID_C + 2])
                    acc = sb(ph, "ffn_conv", [P, 2, GRID_R, GRID_C])
                    f_a, f_u, f_in, f_c, f_s, f_g, f_z = map(sem, (
                        "ffn_a_product ffn_u_product ffn_grid_filled ffn_conv_chain ffn_silu ffn_gated ffn_padding").split())
                    with nc.Block() as block:
                        @block.sync
                        def _(sp):
                            with sp.Fori(0, FT // 2) as i:
                                for j in range(2):
                                    up_slab(sp, j, i)

                        @block.tensor
                        def _(pe):
                            with pe.Fori(0, FT // 2) as i:
                                for j in range(2):
                                    w = ring.view(j, [P, 2, KT, P])
                                    pe.wait_ge(ring.ready[j], i * 32 + (16 * ring.n[j] + 32))
                                    pe.wait_ge(f_in, i * 2 + j)
                                    for k in range(KT):
                                        last = nc.tensor.matmul(bank[j][:], w[:, 0, k, :], h2[:, k, :], start=(k == 0), stop=(k == KT - 1))
                                    last.then_inc(f_a, 1)
                                    pe.wait_ge(f_g, i * 2)
                                    for k in range(KT):
                                        last = nc.tensor.matmul(bank[2 + j][:], w[:, 1, k, :], h2[:, k, :], start=(k == 0), stop=(k == KT - 1))
                                    last.then_inc(f_u, 1)
                                    pe.wait_ge(f_u, i * 2 + (j + 1))
                                    pe.sem_inc(ring.used[j], 2)

                        @block.scalar
                        def _(act):
                            act.wait_ge(f_z, 1)
                            with act.Fori(0, FT // 2) as i:
                                for j in range(2):
                                    act.wait_ge(f_a, i * 2 + (j + 1))
                                    act.wait_ge(f_c, i * 18 + 9 * j)
                                    nc.scalar.copy(pad[:, j, 1:1 + GRID_R, 1:1 + GRID_C],
                                                   bank[j][:].rearrange("p (r c) -> p r c", r=GRID_R)).then_inc(f_in, 1)
                                for j in range(2):
                                    act.wait_ge(f_c, i * 18 + (9 * j + 9))
                                    nc.scalar.activation(acc[:, j], acc[:, j], ACT.Silu).then_inc(f_s, 1)

                        @block.vector
                        def _(dve):
                            nc.vector.memset(pad[:], 0.0).then_inc(f_z, 1)
                            with dve.Fori(0, FT // 2) as i:
                                link = Link(dve, f_c, turn=i, per=18)
                                dve.wait_ge(f_g, i * 2)
                                for j in range(2):
                                    dve.wait_ge(f_in, i * 2 + (j + 1))
                                    for n, (a, b) in enumerate([(1, 1)] + [(a, b) for a in range(3) for b in range(3) if (a, b) != (1, 1)]):
                                        tap = colffn[:, bass.ds(i * 2 + ((a * 3 + b) * FT + j), 1)]
                                        src = pad[:, j, a:a + GRID_R, b:b + GRID_C]
                                        if n == 0:
                                            link(nc.vector.tensor_scalar(acc[:, j], src, tap, None, ALU.mult))
                                        else:
                                            link(nc.vector.scalar_tensor_tensor(acc[:, j], src, tap, acc[:, j], ALU.mult, ALU.add))
                                link.end()
                                for j in range(2):
                                    dve.wait_ge(f_s, i * 2 + (j + 1))
                                    dve.wait_ge(f_u, i * 2 + (j + 1))
                                    o = gT[:, bass.ds(i * 2 + j, 1), :].rearrange("p a n -> p (a n)")
                                    nc.vector.tensor_tensor(o, acc[:, j].rearrange("p r c -> p (r c)"), bank[2 + j][:], ALU.mult).then_inc(f_g, 1)
                ring.passed(FT, FT)
                with ExitStack() as ph:
                    w_o = sem("ffn_out_products")
                    post_act, post_pool, post_dve = post_norm(1, ph, "ffn")
                    NS = (FT + 3) // 4
                    with nc.Block() as block:
                        @block.sync
                        def _(sp):
                            for n in range(NS):
                                ring.load(sp, n % 2, wd_v[:, 4 * n:min(4 * n + 4, FT), :], n // 2)

                        @block.tensor
                        def _(pe):
                            for n in range(NS):
                                nk = min(4, FT - 4 * n)
                                ring.wait(pe, n % 2, n // 2)
                                w = ring.view(n % 2, [P, nk, DM])
                                for t in range(TX):
                                    for a in range(2):
                                        for k in range(nk):
                                            last = nc.tensor.matmul(bank[2 * t + a][:], gT[:, 4 * n + k, t * P:(t + 1) * P], w[:, k, 512 * a:512 * a + 512],
                                                                    start=(n == 0 and k == 0), stop=(n == NS - 1 and k == nk - 1))
                                        if n == NS - 1 and not (t == TX - 1 and a == 1):
                                            last.then_inc(w_o, 1)
                                if n < NS - 1:
                                    last.then_inc(ring.used[n % 2], 1)
                                else:
                                    last.then_inc(w_o, 1)
                            pe.wait_ge(w_o, 8)
                            pe.sem_inc(ring.used[(NS - 1) % 2], 1)

                        @block.scalar
                        def _(act):
                            post_act(act, lambda e, b: e.wait_ge(w_o, b + 1))

                        @block.gpsimd
                        def _(pool):
                            post_pool(pool)

                        @block.vector
                        def _(dve):
                            post_dve(dve)
                ring.passed(NS // 2 + NS % 2, NS // 2)

        ffn()
        if upto == 6:
            dbg("x2", xt[:])
            return

        def qk_project(name, h, w_of, QK, gain, rope=None):
            with ExitStack() as ph:
                sem = ph.enter_context(local_sems())
                sqb = sb(ph, name + "_sq", [P, 2, 512])
                ss = sb(ph, name + "_ss", [P, 3, 8, 8])
                qn = sb(ph, name + "_qn", [P, 2, TX, 512])
                wk = sb(ph, name + "_rope_work", [P, 2, 4, 8, 8]) if rope else None
                q_pr, q_sq, q_sm, q_rs, q_n, q_t, q_st, q_ch = (sem(name + x) for x in (
                    "_projected", "_squared", "_sums", "_rstd", "_normed", "_turned", "_stored", "_rope_chain"))
                with nc.Block() as block:
                    @block.sync
                    def _(sp):
                        for i in range(2):
                            for j in range(2):
                                ring.load(sp, j, w_of(i, j), i)

                    @block.tensor
                    def _(pe):
                        with pe.Fori(0, 2) as i:
                            for j in range(2):
                                ring.wait(pe, j, i)
                                w = ring.view(j, [P, KT, 512])
                                for t in range(TX):
                                    pe.wait_ge(q_n, i * 8 + (0 if j == 0 else t + 1))
                                    for k in range(KT):
                                        last = nc.tensor.matmul(bank[t][:], h[:, k, t * P:(t + 1) * P], w[:, k, :], start=(k == 0), stop=(k == KT - 1))
                                    last.then_inc(q_pr, 1)
                                pe.wait_ge(q_pr, i * 8 + (4 * j + 4))
                                pe.sem_inc(ring.used[j], 1)
                            for j in range(2):
                                for t in range(TX):
                                    n = 4 * j + t
                                    pe.wait_ge(q_n, i * 8 + (n + 1))
                                    pe.wait_ge(q_st, i * 8 + (0 if j == 0 else t + 1))
                                    for m in range(4):
                                        last = nc.tensor.transpose(bank[4 + t][:, m * P:(m + 1) * P], qn[:, j, t, m * P:(m + 1) * P], ident)
                                    last.then_inc(q_t, 1)

                    @block.scalar
                    def _(act):
                        with act.Fori(0, 2) as i:
                            for n in range(8):
                                act.wait_ge(q_pr, i * 8 + (n + 1))
                                act.wait_ge(q_sm, i * 8 + (n - 1) if n else i * 8)
                                nc.scalar.activation(sqb[:, n % 2], bank[n % 4][:], ACT.Square).then_inc(q_sq, 1)
                            for j in range(2):
                                for t in range(TX):
                                    act.wait_ge(q_t, i * 8 + (4 * j + t + 1))
                                    dst = QK[:, bass.ds(i, 1), 4 * j:4 * j + 4, t * P:(t + 1) * P].rearrange("p a m n -> p (a m) n")
                                    src = bank[4 + t][:].rearrange("p (m n) -> p m n", m=4)
                                    if gain is not None:
                                        nc.scalar.activation(dst, src, ACT.Identity, scale=gain(i)).then_inc(q_st, 1)
                                    else:
                                        nc.scalar.copy(dst, src).then_inc(q_st, 1)

                    @block.gpsimd
                    def _(pool):
                        with pool.Fori(0, 2) as i:
                            for n in range(8):
                                pool.wait_ge(q_sm, i * 8 + (n + 1))
                                nc.gpsimd.tensor_tensor(ss[:, 1, n, :], ss[:, 0, n, :], small[:, 1, 0:8], ALU.add).then_inc(q_rs, 1)
                                pool.wait_ge(q_rs, i * 16 + (2 * n + 1))
                                nc.gpsimd.tensor_tensor(ss[:, 2, n, :], ss[:, 1, n, :], half[:, 0:8], ALU.pow).then_inc(q_rs, 1)

                    @block.vector
                    def _(dve):
                        with dve.Fori(0, 2) as i:
                            link = Link(dve, q_ch, turn=i, per=8 * (5 if rope else 0))
                            for j in range(2):
                                for t in range(TX):
                                    n = 4 * j + t
                                    dve.wait_ge(q_sq, i * 8 + (n + 1))
                                    nc.vector.reduce_sum(ss[:, 0, n, :], sqb[:, n % 2].rearrange("p (h n) -> p h n", h=8), axis=AX).then_inc(q_sm, 1)
                                    dve.wait_ge(q_rs, i * 16 + (2 * n + 2))
                                    if t == 0:
                                        dve.wait_ge(q_t, i * 8)
                                    q8 = qn[:, j, t].rearrange("p (h n) -> p h n", h=8)
                                    rs = ss[:, 2, n, :].unsqueeze(2).broadcast_to([P, 8, DA])
                                    o = nc.vector.tensor_tensor(q8, bank[t][:].rearrange("p (h n) -> p h n", h=8), rs, ALU.mult)
                                    if rope is None:
                                        o.then_inc(q_n, 1)
                                    else:
                                        link(o)
                                        rope(dve, link, q8, i, t, wk).then_inc(q_n, 1)
                            link.end()
            ring.passed(2, 2)

        def v_project(name, h, w_v, V, stride=1, gate=None):
            v_p, v_s = sem(name + "_v_products"), sem(name + "_v_stored")
            with nc.Block() as block:
                @block.sync
                def _(sp):
                    n = 0
                    for w in (w_v,) if gate is None else (w_v, gate[0]):
                        for j in range(2):
                            ring.load(sp, j, w[:, :, 512 * j:512 * j + 512], n)
                        n += 1

                @block.tensor
                def _(pe):
                    for j in range(2):
                        ring.wait(pe, j)
                        w = ring.view(j, [P, KT, 512])
                        for t in range(TX):
                            hv = h[:, :, t * P:(t + 1) * P] if stride == 1 else h[:, :, :].rearrange("p k (n s) -> p k s n", s=stride)[:, :, t]
                            for k in range(KT):
                                last = nc.tensor.matmul(bank[4 * j + t][:], hv[:, k, :], w[:, k, :], start=(k == 0), stop=(k == KT - 1))
                            last.then_inc(v_p, 1)
                        pe.wait_ge(v_p, 4 * j + 4)
                        pe.sem_inc(ring.used[j], 1)
                    if gate is not None:
                        for j in range(2):
                            ring.wait(pe, j, 1)
                            w = ring.view(j, [P, KT, 512])
                            for m in range(4):
                                pe.wait_ge(v_s, 4 * j + m + 1)
                                for k in range(KT):
                                    last = nc.tensor.matmul(bank[4 * j + m][:], w[:, k, m * P:(m + 1) * P], h[:, k, 0:SEQ], start=(k == 0), stop=(k == KT - 1))
                                last.then_inc(v_p, 1)
                            pe.wait_ge(v_p, 8 + 4 * j + 4)
                            pe.sem_inc(ring.used[j], 1)

                @block.scalar
                def _(act):
                    for j in range(2):
                        for t in range(TX):
                            act.wait_ge(v_p, 4 * j + t + 1)
                            nc.scalar.copy(V[:, t, 512 * j:512 * j + 512], bank[4 * j + t][:]).then_inc(v_s, 1)
                    if gate is not None:
                        for m in range(8):
                            act.wait_ge(v_p, 8 + m + 1)
                            nc.scalar.activation(gate[1][:, m, :], bank[m][:], ACT.Silu).then_inc(v_s, 1)
            n = 1 if gate is None else 2
            ring.passed(n, n)

        def attend(name, QK, V, units, add, out, stride=1, ncT=None, gs=None, stats=None):
            NP = sum(u[4] for u in units)
            NU_ = len(units)
            NB = (NP + 3) // 4
            with ExitStack() as ph:
                sem = ph.enter_context(local_sems())
                qs = sb(ph, name + "_q_pair", [P, 2, SEQ])
                sc = sb(ph, name + "_scores", [P, 2, NP, P])
                pT = sb(ph, name + "_probs_t", [P, 2, NP, P])
                nm = sb(ph, name + "_stats", [P, 3, 2, TX])
                osb = sb(ph, name + "_out_tm", [P, TX, 2, DA])
                cm = sb(ph, name + "_c_masked", [NA, 2, SEQ]) if ncT is not None else None
                crep = sb(ph, name + "_c_rep", [P, 2, SEQ]) if ncT is not None else None
                a_q, a_cm, a_cp, a_cr, a_s, a_mx, a_ex, a_t, a_st, a_o, a_rc, a_os, a_ot, a_out = (sem(name + x) for x in (
                    "_pair_copied", "_c_one_head", "_c_product", "_c_ready", "_scores_ready", "_max_ready", "_probs_ready", "_probs_turned",
                    "_probs_stored", "_out_products", "_sum_inverse", "_out_scaled", "_out_turned", "_out_stored"))
                a_go = sem(name + "_max_begun")
                nbank = 1 + max(u[1] for u in units)
                with nc.Block() as block:
                    @block.gpsimd
                    def _(pool):
                        with pool.Fori(0, KT) as m:
                            pool.wait_ge(a_s, m * (2 * nbank))
                            for w in range(2):
                                src = QK[:, w, bass.ds(m, 1), :].rearrange("p a n -> p (a n)")
                                if stride > 1:
                                    nc.gpsimd.tensor_copy(qs[:, w].rearrange("p (s n) -> p s n", s=stride),
                                                          src.rearrange("p (n s) -> p s n", s=stride)).then_inc(a_q, 1)
                                else:
                                    nc.gpsimd.tensor_copy(qs[:, w], src).then_inc(a_q, 1)

                    @block.tensor
                    def _(pe):
                        with pe.Fori(0, KT) as m:
                            if ncT is not None:
                                for a in range(2):
                                    pe.wait_ge(a_cm, m * 2 + (a + 1))
                                    pe.wait_ge(a_cr, m * 2 + a)
                                    pe.wait_ge(a_out, m * 1)
                                    nc.tensor.matmul(bank[7][:], m_ones[0:NA, :], cm[:, a, :], start=True, stop=True).then_inc(a_cp, 1)
                            pe.wait_ge(a_q, m * 2 + 2)
                            pe.wait_ge(a_st, m * (2 * NB))
                            for a in range(2):
                                r = slice(DA * a, DA * a + DA)
                                for n, (q, b, c, k0, nk) in enumerate(units):
                                    o = bank[3 * a + b][:, c:c + nk * P]
                                    last = nc.tensor.matmul(o, qs[r, 0, q * P:(q + 1) * P], qs[r, 1, k0 * P:(k0 + nk) * P], start=True, stop=(ncT is None))
                                    if ncT is not None:
                                        last = nc.tensor.matmul(bank[3 * a + b][:, c + (nk - 1) * P:c + nk * P], ident, att[:, 1, :], start=False, stop=True)
                                    if n == NU_ - 1 or units[n + 1][1] != b:
                                        last.then_inc(a_s, 1)
                            for a in range(2):
                                pe.wait_ge(a_ex, m * (2 * NU_) + (a + 1) * NU_)
                                for g in range(NB):
                                    for i in range(min(4, NP - 4 * g)):
                                        last = nc.tensor.transpose(bank[3 * a + g][:, i * P:(i + 1) * P], sc[:, a, 4 * g + i, :], ident)
                                    last.then_inc(a_t, 1)
                            for a in range(2):
                                pe.wait_ge(a_st, m * (2 * NB) + (a + 1) * NB)
                                if a == 0:
                                    pe.wait_ge(a_os, m * 1)
                                i = 0
                                for q, b, c, k0, nk in units:
                                    for k in range(nk):
                                        v = V[:, k0 + k, bass.ds(m * P + DA * a, DA)]
                                        last = nc.tensor.matmul(bank[6][:, q * P + DA * a:q * P + DA * a + DA], pT[:, a, i, :], v, start=(k == 0), stop=(k == nk - 1))
                                        i += 1
                                last.then_inc(a_o, 1)
                            pe.wait_ge(a_os, m * 1 + 1)
                            if ncT is not None:
                                pe.wait_ge(a_cr, m * 2 + 2)
                            pe.wait_ge(a_out, m * 1)
                            for t in range(TX):
                                last = nc.tensor.transpose(bank[7][:, t * P:(t + 1) * P], osb[:, t].rearrange("p a n -> p (a n)"), ident)
                            last.then_inc(a_ot, 1)

                    @block.scalar
                    def _(act):
                        with act.Fori(0, KT) as m:
                            if ncT is not None:
                                for a in range(2):
                                    act.wait_ge(a_cp, m * 2 + (a + 1))
                                    act.wait_ge(a_mx, m * (2 * NU_))
                                    nc.scalar.copy(crep[:, a, :], bank[7][:]).then_inc(a_cr, 1)
                            act.wait_ge(a_t, m * (2 * NB))
                            for a in range(2):
                                i = 0
                                for n, (q, b, c, k0, nk) in enumerate(units):
                                    act.wait_ge(a_mx, m * (2 * NU_) + (a * NU_ + n + 1))
                                    nc.scalar.activation(sc[:, a, i:i + nk, :], sc[:, a, i:i + nk, :], ACT.Exp, scale=-1.0, bias=nm[:, 0, a, q:q + 1],
                                                         accum_out=nm[:, 1, a, q:q + 1]).then_inc(a_ex, 1)
                                    i += nk
                            for a in range(2):
                                if a == 0:
                                    act.wait_ge(a_o, m * 2)
                                for g in range(NB):
                                    w = min(4, NP - 4 * g)
                                    act.wait_ge(a_t, m * (2 * NB) + (a * NB + g + 1))
                                    nc.scalar.copy(pT[:, a, 4 * g:4 * g + w, :], grp4(bank[3 * a + g])[:, 0:w]).then_inc(a_st, 1)

                    @block.vector
                    def _(dve):
                        with dve.Fori(0, KT) as m:
                            if ncT is not None:
                                dve.wait_ge(a_cp, m * 2)
                                for a in range(2):
                                    nc.vector.tensor_scalar(cm[:, a, :], ncT[:], ident[0:NA, bass.ds(m * 2 + a, 1)], None, ALU.mult).then_inc(a_cm, 1)
                            dve.wait_ge(a_t, m * (2 * NB))
                            dve.wait_ge(a_rc, m * 3)
                            for a in range(2):
                                if ncT is not None:
                                    dve.wait_ge(a_cr, m * 2 + (a + 1))
                                i = 0
                                for n, (q, b, c, k0, nk) in enumerate(units):
                                    if n == 0 or units[n - 1][1] != b:
                                        dve.wait_ge(a_s, m * (2 * nbank) + (a * nbank + b + 1))
                                        dve.sem_inc(a_go, 1)
                                    plus = crep[:, a, 0:nk * P] if ncT is not None else add(nk)
                                    nc.vector.tensor_tensor_reduce(
                                        out=sc[:, a, i:i + nk, :].rearrange("p u n -> p (u n)"), in0=bank[3 * a + b][:, c:c + nk * P], in1=plus,
                                        scale=-1.0, scalar=3.0e38, op0=ALU.add, op1=ALU.min, accum_out=nm[:, 0, a, q:q + 1]).then_inc(a_mx, 1)
                                    i += nk
                            dve.wait_ge(a_ex, m * (2 * NU_) + 2 * NU_)
                            for kind in range(2):
                                if stats is None:
                                    dve.sem_inc(a_rc, 1)
                                else:
                                    nc.vector.tensor_copy(stats[:, kind, bass.ds(m * 2, 2), :], nm[:, kind]).then_inc(a_rc, 1)
                            nc.vector.reciprocal(nm[:, 2], nm[:, 1]).then_inc(a_rc, 1)
                            inv = nm[:, 2].rearrange("p a u -> p u a")
                            dve.wait_ge(a_rc, m * 3 + 3)
                            dve.wait_ge(a_o, m * 2 + 2)
                            dve.wait_ge(a_ot, m * 1)
                            nc.vector.tensor_tensor(osb[:], bank[6][:].rearrange("p (u a n) -> p u a n", u=TX, a=2),
                                                    inv.unsqueeze(3).broadcast_to([P, TX, 2, DA]), ALU.mult).then_inc(a_os, 1)
                            dve.wait_ge(a_ot, m * 1 + 1)
                            o = out[:, bass.ds(m, 1), :].rearrange("p a n -> p (a n)")
                            if gs is not None:
                                g = gs[:, bass.ds(m, 1), :].rearrange("p a n -> p (a n)")
                                nc.vector.tensor_tensor(o, bank[7][:], g, ALU.mult).then_inc(a_out, 1)
                            elif stride > 1:
                                nc.vector.tensor_copy(o.rearrange("p (n s) -> p s n", s=stride),
                                                      bank[7][:].rearrange("p (s n) -> p s n", s=stride)).then_inc(a_out, 1)
                            else:
                                nc.vector.tensor_copy(o, bank[7][:]).then_inc(a_out, 1)

        def out_project(name, oT_, w_o):
            o_p, o_a = sem(name + "_wo_products"), sem(name + "_residual_added")
            with nc.Block() as block:
                @block.sync
                def _(sp):
                    for j in range(2):
                        ring.load(sp, j, w_o[:, :, 512 * j:512 * j + 512])

                @block.tensor
                def _(pe):
                    for j in range(2):
                        ring.wait(pe, j)
                        w = ring.view(j, [P, KT, 512])
                        for t in range(TX):
                            for k in range(KT):
                                last = nc.tensor.matmul(bank[2 * t + j][:], oT_[:, k, t * P:(t + 1) * P], w[:, k, :], start=(k == 0), stop=(k == KT - 1))
                            last.then_inc(o_p, 1)
                        pe.wait_ge(o_p, 4 * j + 4)
                        pe.sem_inc(ring.used[j], 1)

                @block.vector
                def _(dve):
                    for j in range(2):
                        for t in range(TX):
                            dve.wait_ge(o_p, 4 * j + t + 1)
                            c = slice(512 * j, 512 * j + 512)
                            nc.vector.tensor_tensor(xt[:, t, c], xt[:, t, c], bank[2 * t + j][:], ALU.add).then_inc(o_a, 1)
            ring.passed(1, 1)

        grp4 = lambda b: b[:].rearrange("p (u n) -> p u n", u=4)
        CAUSAL = [(0, 0, 0, 0, 1), (1, 0, P, 0, 2), (2, 1, 0, 0, 3), (3, 2, 0, 0, 4)]
        s_hc = sem("head_constants")

        def fox():
            fw = d["fox_w_in_2"][0].rearrange("(k p) n -> p k n", p=P)
            with ExitStack() as fs:
                QK = sb(fs, "fox_qk_fm", [P, 2, KT, SEQ])
                V = sb(fs, "fox_v_tm", [P, TX, DM])
                gs = sb(fs, "fox_gate_fm", [P, KT, SEQ])
                ncT = sb(fs, "fox_minus_c", [NA, SEQ])
                h = sb(fs, "fox_h_fm", [P, KT, SEQ])
                gcol = sb(fs, "fox_gains", [P, 2])
                wf = sb(fs, "fox_w_f", [P, KT, NA])
                bf = sb(fs, "fox_b_f", [P, NA])
                t = sb(fs, "fox_forget_work", [P, 6, TX, NA])
                with nc.Block() as block:
                    @block.sync
                    def _(sp):
                        sp.dma_start(wf[:], fw[:, :, 4 * DM:4 * DM + NA]).then_inc(s_hc, 16)
                        sp.dma_start(bf[:], d["fox_b_f_2"].broadcast_to([P, NA])).then_inc(s_hc, 16)
                        for a in range(2):
                            for i, g in enumerate(("fox_q_norm_2", "fox_k_norm_2")):
                                sp.dma_start(gcol[DA * a:DA * a + DA, i:i + 1], d[g].rearrange("a n -> n a")).then_inc(s_hc, 16)
                        sp.wait_ge(s_hc, 16 * 6)
                o, n = ROWS_A["g2"]
                norm_stage("fox", [(xt, 0, col[:, o:o + KT], None)], h)
                g_mm, g_d, g_a = sem("forget_products"), sem("forget_dve_chain"), sem("forget_act")
                with nc.Block() as block:
                    @block.tensor
                    def _(pe):
                        for b in range(TX):
                            for k in range(KT):
                                last = nc.tensor.matmul(bank[0][:, NA * b:NA * b + NA], h[:, k, b * P:(b + 1) * P], wf[:, k, :], start=(k == 0), stop=(k == KT - 1))
                        last.then_inc(g_mm, 1)
                        pe.wait_ge(g_d, 10)
                        for b in range(TX):
                            for s in range(b + 1):
                                last = nc.tensor.matmul(bank[1][0:NA, b * P:(b + 1) * P], t[:, 5, s, :], m_le if s == b else m_ones, start=(s == 0), stop=(s == b))
                        last.then_inc(g_mm, 1)

                    @block.vector
                    def _(dve):
                        link = Link(dve, g_d)
                        dve.wait_ge(g_mm, 1)
                        f = bank[0][:, 0:TX * NA].rearrange("p (b n) -> p b n", n=NA)
                        link(nc.vector.tensor_scalar(gcol[:, 1:2], gcol[:, 1:2], float(DA) ** 0.5, None, ALU.mult))
                        link(nc.vector.tensor_tensor(t[:, 0], f, bf[:].unsqueeze(1).broadcast_to([P, TX, NA]), ALU.add))
                        link(nc.vector.tensor_scalar(t[:, 1], t[:, 0], -1.0, None, ALU.mult))
                        link(nc.vector.tensor_tensor(t[:, 2], t[:, 0], t[:, 1], ALU.min))
                        dve.wait_ge(g_a, 2)
                        link(nc.vector.tensor_scalar(t[:, 1], t[:, 3], 1.0, None, ALU.add))
                        link(nc.vector.tensor_scalar(t[:, 1], t[:, 1], -1.0, None, ALU.add))
                        link(nc.vector.tensor_tensor(t[:, 1], t[:, 3], t[:, 1], ALU.subtract))
                        link(nc.vector.tensor_tensor(t[:, 1], t[:, 4], t[:, 1], ALU.add))
                        link(nc.vector.tensor_scalar(t[:, 0], t[:, 0], 0.0, None, ALU.min))
                        link(nc.vector.tensor_tensor(t[:, 5], t[:, 0], t[:, 1], ALU.subtract))

                    @block.scalar
                    def _(act):
                        act.wait_ge(g_d, 4)
                        nc.scalar.activation(t[:, 3], t[:, 2], ACT.Exp).then_inc(g_a, 1)
                        act.wait_ge(g_a, 1)
                        nc.scalar.activation(t[:, 4], t[:, 3], ACT.Ln, bias=1.0).then_inc(g_a, 1)
                        act.wait_ge(g_mm, 2)
                        nc.scalar.mul(ncT[:], bank[1][0:NA, :], -1.0).then_inc(g_a, 1)
                qk_project("fox", h, lambda i, j: fw[:, :, DM * i + 512 * j:DM * i + 512 * j + 512], QK, lambda i: gcol[:, bass.ds(i, 1)])
                v_project("fox", h, fw[:, :, 2 * DM:3 * DM], V, gate=(fw[:, :, 3 * DM:4 * DM], gs))
                attend("fox", QK, V, CAUSAL, None, h, ncT=ncT, gs=gs)
                out_project("fox", h, d["fox_w_out_2"][0].rearrange("(k p) n -> p k n", p=P))

        if upto != 8:
            fox()
        if upto == 7:
            dbg("x3", xt[:])
            return

        def gate_project(name, h, w, dst):
            p, s = sem(name + "_gate_products"), sem(name + "_gate_stored")
            with nc.Block() as block:
                @block.sync
                def _(sp):
                    for j in range(2):
                        ring.load(sp, j, w[:, :, 512 * j:512 * j + 512])

                @block.tensor
                def _(pe):
                    for j in range(2):
                        ring.wait(pe, j)
                        v = ring.view(j, [P, KT, 512])
                        for m in range(4):
                            for k in range(KT):
                                last = nc.tensor.matmul(bank[4 * j + m][:], v[:, k, m * P:(m + 1) * P], h[:, k, :], start=(k == 0), stop=(k == KT - 1))
                            last.then_inc(p, 1)
                        pe.wait_ge(p, 4 * j + 4)
                        pe.sem_inc(ring.used[j], 1)

                @block.scalar
                def _(act):
                    for m in range(8):
                        act.wait_ge(p, m + 1)
                        nc.scalar.activation(dst[:, m, :], bank[m][:], ACT.Silu).then_inc(s, 1)
            ring.passed(1, 1)

        def dsw():
            dw = d["dsw_w_in_2"][0].rearrange("(k p) n -> p k n", p=P)
            C1 = 6.28125
            C2 = float(np.float32(round((2 * math.pi - C1) * 2.0 ** 19) / 2.0 ** 19))
            C3 = 2 * math.pi - C1 - C2
            MAGIC = 1.5 * 2.0 ** 23
            TOP = 3.1415925
            with ExitStack() as fs:
                O = sb(fs, "dsw_out_fm", [P, NG, KT, SEQ])
                h = sb(fs, "dsw_h_fm", [P, KT, SEQ])
                QK = sb(fs, "dsw_qk_fm", [P, 2, KT, SEQ])
                V = sb(fs, "dsw_v_tm", [P, TX, DM])
                stats = sb(fs, "dsw_stats", [P, NG, 2, NA, TX])
                gains = sb(fs, "dsw_gains", [P, NG, 2, DA])
                cs = sb(fs, "rope_cos_sin", [P, 2, TX, 8])
                with ExitStack() as ph:
                    pi = sb(ph, "positions", [P, TX], I32)
                    inv = sb(ph, "inverse_frequencies", [P, 8])
                    t = sb(ph, "rope_setup", [P, 6, TX, 8])
                    r_l, r_d, r_a = sem("rope_loads"), sem("rope_setup_chain"), sem("rope_tables")
                    with nc.Block() as block:
                        @block.sync
                        def _(sp):
                            for b in range(TX):
                                sp.dma_start(pi[:, b:b + 1], d["positions_2"][:, b * P:(b + 1) * P].rearrange("a p -> p a")).then_inc(r_l, 16)
                            sp.dma_start(inv[:], d["k_inv"]).then_inc(r_l, 16)
                            for i, g in enumerate(("dsw_q_norm_2", "dsw_k_norm_2")):
                                sp.dma_start(gains[:, :, i, :], d[g].broadcast_to([P, NG, DA])).then_inc(r_l, 16)

                        @block.vector
                        def _(dve):
                            link = Link(dve, r_d)
                            dve.wait_ge(r_l, 16 * (TX + 3))
                            link(nc.vector.tensor_scalar(gains[:, :, 1, :], gains[:, :, 1, :], float(DA) ** 0.5, None, ALU.mult))
                            link(nc.vector.tensor_copy(t[:, 0, :, 0], pi[:]))
                            link(nc.vector.tensor_tensor(t[:, 1], t[:, 0, :, 0:1].broadcast_to([P, TX, 8]), inv[:].unsqueeze(1).broadcast_to([P, TX, 8]), ALU.mult))
                            link(nc.vector.tensor_scalar(t[:, 2], t[:, 1], 1.0 / (2 * math.pi), MAGIC, ALU.mult, ALU.add))
                            link(nc.vector.tensor_scalar(t[:, 2], t[:, 2], -MAGIC, None, ALU.add))
                            for c in (C1, C2, C3):
                                link(nc.vector.scalar_tensor_tensor(t[:, 1], t[:, 2], -c, t[:, 1], ALU.mult, ALU.add))
                            link(nc.vector.tensor_scalar(t[:, 3], t[:, 1], TOP, -TOP, ALU.min, ALU.max))
                            link(nc.vector.tensor_scalar(t[:, 4], t[:, 1], math.pi / 2, None, ALU.add))
                            link(nc.vector.tensor_scalar(t[:, 5], t[:, 4], math.pi, -2 * math.pi, ALU.is_gt, ALU.mult))
                            link(nc.vector.tensor_tensor(t[:, 4], t[:, 4], t[:, 5], ALU.add))
                            link(nc.vector.tensor_scalar(t[:, 4], t[:, 4], TOP, -TOP, ALU.min, ALU.max))

                        @block.scalar
                        def _(act):
                            act.wait_ge(r_d, 13)
                            nc.scalar.activation(cs[:, 0], t[:, 4], ACT.Sin).then_inc(r_a, 1)
                            nc.scalar.activation(cs[:, 1], t[:, 3], ACT.Sin).then_inc(r_a, 1)
                o, n = ROWS_A["g2"]
                norm_stage("dsw", [(xt, 0, col[:, o + KT:o + 2 * KT], None)], h)
                for g in range(NG):
                    def rope(dve, link, q8, i, t, wk, g=g):
                        gv = gains[:, g, bass.ds(i, 1), :].broadcast_to([P, 8, DA])
                        link(nc.vector.tensor_tensor(q8, q8, gv, ALU.mult))
                        r = q8[:, :, 0:ROT].rearrange("p h (a n) -> p a h n", a=2)
                        c = cs[:, 0, t, :].unsqueeze(1).broadcast_to([P, 8, 8])
                        s = cs[:, 1, t, :].unsqueeze(1).broadcast_to([P, 8, 8])
                        for a in range(2):
                            last = nc.vector.tensor_tensor(wk[:, t % 2, a], r[:, a], c, ALU.mult)
                        link(last)
                        link(nc.vector.tensor_tensor(wk[:, t % 2, 2], r[:, 1], s, ALU.mult))
                        link(nc.vector.tensor_tensor(wk[:, t % 2, 3], r[:, 0], s, ALU.mult))
                        nc.vector.tensor_tensor(r[:, 0], wk[:, t % 2, 0], wk[:, t % 2, 2], ALU.subtract)
                        return nc.vector.tensor_tensor(r[:, 1], wk[:, t % 2, 1], wk[:, t % 2, 3], ALU.add)

                    name = f"dsw{g}"
                    qk_project(name, h, lambda i, j: dw[:, :, NG * DM * i + DM * g + 512 * j:NG * DM * i + DM * g + 512 * j + 512], QK, None, rope)
                    st = 1 if g == 0 else 4
                    v_project(name, h, dw[:, :, (2 * NG + g) * DM:(2 * NG + g + 1) * DM], V, stride=st)
                    attend(name, QK, V, BAND if g == 0 else BLOCKS,
                           (lambda nk: att[:, 2 - nk:2, :].rearrange("p a n -> p (a n)")) if g == 0 else (lambda nk, g=g: att[:, g, :]),
                           O[:, g], stride=st, stats=stats[:, g])
                gs = QK[:, 0]
                gate_project("dsw", h, dw[:, :, 3 * NG * DM:3 * NG * DM + DM], gs)
                with ExitStack() as ph:
                    lse = sb(ph, "dsw_lse", [P, NG, TX, NA])
                    lt = sb(ph, "dsw_group_weights", [NA, NG + 2, SEQ])
                    hs = sb(ph, "head_to_rows", [NA, NA // 2, P])
                    w = sb(ph, "dsw_mix_work", [P, 2, NG, SEQ])
                    c_l, c_a, c_d, c_t, c_e, c_r, c_m, c_o = map(sem, (
                        "combine_loads combine_ln combine_dve combine_turned combine_act combine_rep combine_scaled combine_out").split())
                    with nc.Block() as block:
                        @block.sync
                        def _(sp):
                            sp.dma_start(hs[:], d["k_hs"]).then_inc(c_l, 16)

                        @block.scalar
                        def _(act):
                            nc.scalar.activation(stats[:, :, 1], stats[:, :, 1], ACT.Ln).then_inc(c_a, 1)
                            for g in range(NG):
                                act.wait_ge(c_t, g + 1)
                                if g == 0:
                                    nc.scalar.copy(lt[:, g, :], bank[g][0:NA, :]).then_inc(c_a, 1)
                                else:
                                    nc.scalar.copy(lt[:, g, :].rearrange("p (n s) -> p s n", s=4), bank[g][0:NA, :].rearrange("p (s n) -> p s n", s=4)).then_inc(c_a, 1)
                            act.wait_ge(c_d, 6)
                            nc.scalar.activation(lt[:, 0:NG, :], lt[:, 0:NG, :], ACT.Exp).then_inc(c_a, 1)

                        @block.tensor
                        def _(pe):
                            pe.wait_ge(c_d, 1)
                            for g in range(NG):
                                for b in range(TX):
                                    last = nc.tensor.transpose(bank[g][0:NA, b * P:(b + 1) * P], lse[:, g, b, :], ident)
                                last.then_inc(c_t, 1)
                            pe.wait_ge(c_l, 16)
                            pe.wait_ge(c_d, 10)
                            for m in range(KT):
                                for g in range(NG):
                                    if m >= 2:
                                        pe.wait_ge(c_m, NG * (m - 2) + g + 1)
                                    nc.tensor.matmul(bank[3 * (m % 2) + g][:], hs[:, m, :], lt[:, g, :], start=True, stop=True).then_inc(c_r, 1)

                        @block.vector
                        def _(dve):
                            link = Link(dve, c_d)
                            dve.wait_ge(c_a, 1)
                            link(nc.vector.tensor_tensor(lse[:].rearrange("p g t h -> p g h t"), stats[:, :, 1], stats[:, :, 0], ALU.subtract))
                            dve.wait_ge(c_a, 4)
                            link(nc.vector.tensor_tensor(lt[:, 3, :], lt[:, 0, :], lt[:, 1, :], ALU.max))
                            link(nc.vector.tensor_tensor(lt[:, 3, :], lt[:, 3, :], lt[:, 2, :], ALU.max))
                            for g in range(NG):
                                link(nc.vector.tensor_tensor(lt[:, g, :], lt[:, g, :], lt[:, 3, :], ALU.subtract))
                            dve.wait_ge(c_a, 5)
                            link(nc.vector.tensor_tensor(lt[:, 3, :], lt[:, 0, :], lt[:, 1, :], ALU.add))
                            link(nc.vector.tensor_tensor(lt[:, 3, :], lt[:, 3, :], lt[:, 2, :], ALU.add))
                            link(nc.vector.reciprocal(lt[:, 4, :], lt[:, 3, :]))
                            link(nc.vector.tensor_tensor(lt[:, 0:NG, :], lt[:, 0:NG, :], lt[:, 4:5, :].broadcast_to([NA, NG, SEQ]), ALU.mult))
                            for m in range(KT):
                                if m >= 2:
                                    dve.wait_ge(c_o, 3 * (m - 1))
                                for g in range(NG):
                                    dve.wait_ge(c_r, NG * m + g + 1)
                                    nc.vector.tensor_tensor(w[:, m % 2, g], O[:, g, m, :], bank[3 * (m % 2) + g][:], ALU.mult).then_inc(c_m, 1)

                        @block.gpsimd
                        def _(pool):
                            for m in range(KT):
                                pool.wait_ge(c_m, NG * (m + 1))
                                v = w[:, m % 2]
                                nc.gpsimd.tensor_tensor(v[:, 0], v[:, 0], v[:, 1], ALU.add).then_inc(c_o, 1)
                                pool.wait_ge(c_o, 3 * m + 1)
                                nc.gpsimd.tensor_tensor(v[:, 0], v[:, 0], v[:, 2], ALU.add).then_inc(c_o, 1)
                                pool.wait_ge(c_o, 3 * m + 2)
                                nc.gpsimd.tensor_tensor(h[:, m, :], v[:, 0], gs[:, m, :], ALU.mult).then_inc(c_o, 1)
                out_project("dsw", h, d["dsw_w_out_2"][0].rearrange("(k p) n -> p k n", p=P))

        BAND = [(0, 0, 0, 0, 1), (1, 0, P, 0, 2), (2, 1, 0, 1, 2), (3, 1, 2 * P, 2, 2)]
        BLOCKS = [(b, 0, P * b, b, 1) for b in range(TX)]
        dsw()
        s_out = sem("out_stored")
        with nc.Block() as block:
            @block.sync
            def _(sp):
                sp.dma_start(out[0].rearrange("(t p) n -> p t n", p=P), xt[:]).then_inc(s_out, 16)
                sp.wait_ge(s_out, 16)



_OUTS = [((1, SEQ, DM), "float32")]
_INS = ["x", "c", "ctx", "c_ctx", "w_ada", "b_ada", "norm_pre_mix", "norm_post_mix", "norm_pre_ffn", "norm_post_ffn",
        "w_in", "conv_qkv", "a_log", "dt_bias", "dn_norm", "w_fourier", "w_dn", "w_out", "w_up", "conv_ffn", "w_down",
        "positions_2", "norm_g_2", "fox_w_in_2", "fox_b_f_2", "fox_q_norm_2", "fox_k_norm_2", "fox_w_out_2",
        "dsw_w_in_2", "dsw_q_norm_2", "dsw_k_norm_2", "dsw_w_out_2"]


def kernel(**inputs):
    import concourse.bacc as bacc
    from concourse.bass_utils import run_bass_kernel_spmd

    nc = bacc.Bacc("TRN2", target_bir_lowering=False, num_devices=1)
    arrays, d = {}, {}
    for name, a in [(n, inputs[n]) for n in _INS] + list(constants().items()):
        a = np.ascontiguousarray(a)
        arrays["in_" + name] = a
        d[name] = nc.dram_tensor("in_" + name, a.shape, mybir.dt.from_np(a.dtype), kind="ExternalInput").ap()
    shape, dtype = _OUTS[0]
    out = nc.dram_tensor("out_0_dram", shape, F32, kind="ExternalOutput").ap()
    build(nc, d, out)
    r = run_bass_kernel_spmd(nc, [arrays], core_ids=[0])
    return r.results[0]["out_0_dram"]
```

```python
import math
from contextlib import ExitStack, contextmanager

import concourse.bass as bass
import numpy as np
from concourse import mybir

F32 = mybir.dt.float32
F32R = mybir.dt.float32r
I32 = mybir.dt.int32
ALU = mybir.AluOpType
ACT = mybir.ActivationFunctionType
AX = mybir.AxisListType.X
P = 128
SEQ, CTX, DM = 512, 256, 1024
TX, TC, TT = SEQ // P, CTX // P, (SEQ + CTX) // P
KT = DM // P
HD, HE = 8, 128
FW = 512
DFF = 2816
FT = DFF // P
GRID_R, GRID_C = 8, 64
NA, DA = 16, 64
NG = 3
ROT = 16
EPS = 1e-6
NEG = -1.0e30
LEVELS = 7
OFF_Q, OFF_K, OFF_V, OFF_Z = 512, 1536, 2560, 3584
OFF_B = 4608
OFF_G = 4640

ROWS_A = {"b_ada": (0, 48), "pre_mix": (48, 8), "pre_ffn": (56, 8), "dn": (64, 1), "g2": (65, 16),
          "c": (81, 8), "cc": (89, 8)}


def constants():
    i = np.arange(P)
    m = {}
    m["ident"] = np.eye(P)
    m["le"] = (i[:, None] <= i[None, :])
    m["gt"] = (i[:, None] > i[None, :])
    m["ge"] = (i[:, None] >= i[None, :])
    m["lt"] = (i[:, None] < i[None, :])
    m["ones"] = np.ones((P, P))
    sq = np.stack([m[k] for k in ("ident", "le", "gt", "ge", "lt", "ones")], 1)
    lev = []
    for n in range(LEVELS):
        b = i >> n
        f = (b[None, :] == b[:, None] + 1) & (b[:, None] % 2 == 0)
        lev.append(np.stack([f, f.T], 1))
    lev = np.stack(lev, 1)
    j = i[:, None]
    k = i[None, :]
    att = [np.where(k >= j, 0, NEG), np.where(k <= j, 0, NEG),
           np.where((k <= j) & (k % 4 == j % 4), 0, NEG)]
    att = np.stack(att, 1)
    t = np.arange(SEQ)
    ang = 2 * np.pi * ((t[:, None] * t[None, :]) % SEQ) / SEQ
    ct = np.stack([np.cos(ang), -np.sin(ang)]) / np.sqrt(SEQ * P)
    ct = ct.reshape(2, TX, P, SEQ).transpose(2, 0, 1, 3)
    ang = 2 * np.pi * ((i[:, None] * i[None, :]) % P) / P
    cc = np.concatenate([np.cos(ang), np.sin(ang)], 1)
    inv = 500000.0 ** (-np.arange(0, ROT, 2) / ROT)
    hs = np.zeros((NA, NA // 2, P))
    for h in range(NA):
        hs[h, h // 2, (h % 2) * DA:(h % 2 + 1) * DA] = 1
    oh = np.zeros((NA, NA, P))
    for h in range(NA):
        oh[h, h, :] = 1
    f = lambda a: np.ascontiguousarray(a, dtype=np.float32)
    return {"k_sq": f(sq), "k_lev": f(lev), "k_att": f(att), "k_dft_t": f(ct), "k_dft_c": f(cc),
            "k_inv": f(np.broadcast_to(inv, (P, 8))), "k_hs": f(hs), "k_oh": f(oh)}


def build(nc, d, out, dbg=None, upto=99, inject=None):
    es = ExitStack()
    nsem = [0]

    def sem(name):
        return es.enter_context(nc.semaphore(name))

    def sb(stack, name, shape, dt=F32):
        t = stack.enter_context(nc.sbuf_tensor(name, shape, dt))
        place[t.name] = nc.sbuf_base - 4 * int(np.prod(shape[1:]))
        return t

    place, aliases = {}, {}

    @contextmanager
    def local_sems():
        taken = []

        def take(name):
            taken.append(nc.alloc_semaphore(name=name))
            return taken[-1]

        yield take
        nc.clear_and_free_semaphores(taken)
        nc.all_engine_barrier()

    def rounded(t):
        if t.name not in aliases:
            aliases[t.name] = nc.alloc_sbuf_tensor_at(t.name + "_r", list(t.shape), F32R, offset=place[t.name])
        return aliases[t.name]

    class Link:

        def __init__(self, eng, s, start=0, turn=None, per=0):
            self.eng, self.s, self.n, self.turn, self.per, self.start = eng, s, start, turn, per, start

        def __call__(self, ins):
            ins.then_inc(self.s, 1)
            self.n += 1
            v = self.n if self.turn is None else self.turn * self.per + self.n
            self.eng.wait_ge(self.s, v)

        def end(self):
            assert self.turn is None or self.n - self.start == self.per, (self.n, self.start, self.per)

    class Ring:

        def __init__(self, buf):
            self.buf, self.bufr = buf, rounded(buf)
            self.left = False
            self.ready = [sem(f"slab_ready{j}") for j in range(2)]
            self.used = [sem(f"slab_used{j}") for j in range(2)]
            self.n = [0, 0]

        def load(self, sp, slot, src, turn=0):
            o = self.view(slot, src.shape)
            sp.wait_ge(self.used[slot], turn + (self.n[slot] + 1))
            sp.dma_start(o, src).then_inc(self.ready[slot], 16)

        def view(self, slot, shape):
            n = int(np.prod(shape[1:]))
            v = self.buf[:, slot, 0:n]
            if len(shape) == 3:
                return v.rearrange("p (a b) -> p a b", a=shape[1])
            if len(shape) == 4:
                return v.rearrange("p (a b c) -> p a b c", a=shape[1], b=shape[2])
            return v

        def wait(self, pe, slot, turn=0):
            pe.wait_ge(self.ready[slot], turn * 16 + 16 * (self.n[slot] + 1))

        def passed(self, a, b):
            self.n = [self.n[0] + a, self.n[1] + b]

        def start_split(self, plan, loads0, loads1):
            self.plan, self.base, self.left, self.ready0 = plan, 0, False, [loads0, loads1]
            self.rounded = [sem(f"slab_rounded{j}") for j in range(2)]
            self.split_done = [sem(f"slab_split{j}") for j in range(2)]

        def where(self, q):
            return (self.base + q) % 2, (self.base + q) // 2

        def load_split(self, sp, q):
            if self.base + q < len(self.plan):
                j, n = self.where(q)
                src = self.plan[self.base + q]
                sp.wait_ge(self.used[j], self.n[j] + n + 1)
                dst, half = self.view(j, src.shape), src.shape[1] // 2
                for e in range(2):
                    part = (slice(None), e) if len(src.shape) == 4 else (slice(None), slice(e * half, (e + 1) * half))
                    sp.dma_start(dst[part], src[part]).then_inc(self.ready[j], 16)

        def halves(self, q, shape):
            j, _ = self.where(q)
            n = int(np.prod(shape[1:]))
            out = []
            for o in (2048, 0):
                v = self.bufr[:, j, o:o + n]
                out.append(v.rearrange("p (a b) -> p a b", a=shape[1]) if len(shape) == 3 else
                           v.rearrange("p (a b c) -> p a b c", a=shape[1], b=shape[2]))
            return out

        def split(self, dve, q, turn=0, per=0, size=2048, own=None):
            if self.base + q >= len(self.plan):
                return
            j, n = self.where(q)
            t = turn * (per // 2) if per else 0
            raw, low, hi = self.buf[:, j, 0:size], self.bufr[:, j, 0:size], self.bufr[:, j, 2048:2048 + size]
            dve.wait_ge(self.ready[j], t * 32 + (16 * self.ready0[j] + 32 * (n + 1)))
            nc.vector.tensor_copy(hi, raw).then_inc(self.rounded[j], 1)
            dve.wait_ge(self.rounded[j], t + (n + 1))
            c = own or size
            nc.vector.tensor_tensor(low[:, 0:c], raw[:, 0:c], hi[:, 0:c].bitcast(F32), ALU.subtract).then_inc(self.split_done[j], 1)

        def finish_split(self, dve):
            if self.left:
                self.split(dve, 1)
            self.left = False

        def passed_split(self, n, left=False):
            self.base += n
            self.left = left

        def wait_split(self, pe, q, turn=0, per=0):
            j, n = self.where(q)
            pe.wait_ge(self.split_done[j], (turn * (per // 2) if per else 0) + (n + 1))

    def product3(o, w, a, start, stop):
        for n, (i, j) in enumerate(((0, 0), (0, 1), (1, 0))):
            last = nc.tensor.matmul(o, w[i], a[j], start=start and n == 0, stop=stop and n == 2)
        return last

    def slab_products(pe, ring, q, outs, w_of, a_of, done, value, nk=8, turn=0, per=0, before=None):
        for half in range(2):
            ring.wait_split(pe, q + half, turn, per)
            slab = ring.halves(q + half, [P, nk // 2, 512])
            j, _ = ring.where(q + half)
            for m in range(4):
                if half == 0 and before is not None:
                    before(m)
                for k in range(nk // 2):
                    kk = half * (nk // 2) + k
                    last = product3(outs[m][:], w_of(slab, m, k, kk), a_of(slab, m, k, kk), half == 0 and k == 0, half == 1 and k == nk // 2 - 1)
                if half == 1:
                    last.then_inc(done, 1)
            if half == 0:
                last.then_inc(ring.used[j], 1)
            else:
                pe.wait_ge(done, value)
                pe.sem_inc(ring.used[j], 1)

    def fm(act):
        return (lambda slab, m, k, kk: [x[:, k, m * P:(m + 1) * P] for x in slab]), (lambda slab, m, k, kk: [x[:, kk, 0:SEQ] for x in act])

    def tm(act, tokens=None):
        tokens = tokens or (lambda x, kk, t: x[:, kk, t * P:(t + 1) * P])
        return (lambda slab, m, k, kk: [tokens(x, kk, m) for x in act]), (lambda slab, m, k, kk: [x[:, k, :] for x in slab])

    with es:
        bank = [es.enter_context(nc.psum_tensor(f"bank{i}", [P, 512], F32)) for i in range(8)]
        sq = sb(es, "squares", [P, 6, P])
        ident, m_le, m_gt, m_ge, m_lt, m_ones = (sq[:, i, :] for i in range(6))
        col = sb(es, "columns", [P, 97])
        colconv = sb(es, "conv_columns", [P, 72])
        colffn = sb(es, "ffn_conv_columns", [P, 198])
        wsc = sb(es, "norm_scale", [P, 3, KT])
        shf = sb(es, "norm_shift", [P, 3, KT])
        gtrow = sb(es, "gate_rows", [P, 2, DM])
        att = sb(es, "attention_masks", [P, 3, P])
        half = sb(es, "minus_half", [P, P])
        small = sb(es, "small_constants", [P, 3, 16])
        xt = sb(es, "x_tm", [P, TX, DM])
        ring = Ring(sb(es, "slab_ring", [P, 2, 4096]))
        s_mm, s_ev, s_st = sem("product_done"), sem("evacuated"), sem("staged")

        def colof(name, i=0):
            o, n = ROWS_A[name]
            return col[:, o + i:o + i + 1]

        def k_halves(w, c, nk=KT):
            w = w.rearrange("(k p) n -> p k n", p=P)
            return [w[:, h * nk // 2:(h + 1) * nk // 2, c:c + 512] for h in range(2)]

        def both(w, c, nk=KT):
            return k_halves(w, c, nk) + k_halves(w, c + 512, nk)

        plan_mix = k_halves(d["w_in"][0], 0)
        for i in range(2):
            plan_mix += k_halves(d["w_in"][0], OFF_G + 512 * i) + k_halves(d["w_in"][0], OFF_G + DM + 512 * i)
            plan_mix += k_halves(d["w_fourier"][0], 512 * i, 4) + k_halves(d["w_dn"][0], 512 * i)
        plan_mix += both(d["w_out"][0], 0)
        wu = d["w_up"][0].rearrange("(k p) (a n) -> p a k n", p=P, a=2)
        plan_ffn = [wu[:, :, :, m * P:(m + 1) * P] for m in range(FT)]
        plan_ffn += [d["w_down"][0].rearrange("(k p) n -> p k n", p=P)[:, 2 * n:2 * n + 2, :] for n in range(FT // 2)]
        plan_fox = [x for j in range(4) for x in both(d["fox_w_in_2"][0], j * DM)] + both(d["fox_w_out_2"][0], 0)
        plan_dsw = []
        for g in range(NG):
            plan_dsw += [x for i in range(3) for x in both(d["dsw_w_in_2"][0], (NG * i + g) * DM)]
        plan_dsw += both(d["dsw_w_in_2"][0], 3 * NG * DM) + both(d["dsw_w_out_2"][0], 0)

        def split_all(dve, s, hi, x, lo, base=0):
            nc.vector.tensor_copy(hi, x).then_inc(s, 1)
            dve.wait_ge(s, base + 1)
            nc.vector.tensor_tensor(lo, x, hi.bitcast(F32), ALU.subtract).then_inc(s, 1)

        delta, ctx_in = ExitStack(), ExitStack()
        es.enter_context(delta)
        hT = sb(delta, "h_fm", [P, KT, SEQ + CTX])
        es.enter_context(ctx_in)
        ct = sb(ctx_in, "ctx_tm", [P, TC, DM])
        s_ld = sem("x_ctx_loaded")
        with ExitStack() as ph:
            rb = sb(ph, "mod_rows", [2, 2, 2048])
            s_rw, s_re, s_tc = sem("ada_rows_product"), sem("ada_rows_stored"), sem("ada_rows_turned")
            rowA = sb(ph, "rows_a", [97, P])
            rowB = sb(ph, "rows_b", [72, P])
            rowC = sb(ph, "rows_c", [99, 2, P])
            cs = sb(ph, "c_silu", [P, KT, 2])
            csrep = sb(ph, "c_silu_rep", [P, KT, P])
            grow = sb(ph, "rows_to_fold", [P, 4, DM])
            modc = sb(ph, "mod_columns", [P, 32, 2])
            s_row, s_tr, s_col, s_cs, s_mc, s_gr, s_mv, s_g = map(
                sem, "ada_rows ada_tr ada_col ada_cs ada_mod_cols ada_gate_rows ada_moved ada_grow".split())
            s_d = sem("ada_dve_chain")
            w_v = d["w_ada"][0].rearrange("(k p) n -> p k n", p=P)
            with nc.Block() as block:
                @block.sync
                def _(sp):
                    sp.dma_start(sq[:], d["k_sq"]).then_inc(s_row, 16)
                    sp.dma_start(att[:], d["k_att"]).then_inc(s_row, 16)
                    for src, name in ((d["b_ada"][0].rearrange("(n p) -> n p", p=P), "b_ada"),
                                      (d["norm_pre_mix"][0].rearrange("(n p) -> n p", p=P), "pre_mix"),
                                      (d["norm_pre_ffn"][0].rearrange("(n p) -> n p", p=P), "pre_ffn"),
                                      (d["dn_norm"], "dn"),
                                      (d["norm_g_2"].rearrange("a (n p) -> (a n) p", p=P), "g2"),
                                      (d["c"][0].rearrange("(n p) -> n p", p=P), "c"),
                                      (d["c_ctx"].rearrange("(n p) -> n p", p=P), "cc")):
                        o, n = ROWS_A[name]
                        sp.dma_start(rowA[o:o + n, :], src).then_inc(s_row, 16)
                    sp.dma_start(rowB[:], d["conv_qkv"][0].rearrange("a (n p) -> (a n) p", p=P)).then_inc(s_row, 16)
                    sp.dma_start(rowC[:], d["conv_ffn"][0].rearrange("a b (n p) -> (a b n) p", p=P)
                                 .rearrange("(j r) p -> r j p", j=2)).then_inc(s_row, 16)
                    for j in range(2):
                        sp.sem_inc(ring.used[j], 1)
                    with sp.Fori(0, 6) as i:
                        for j in range(2):
                            ring.load(sp, j, w_v[:, :, bass.ds(i * 1024 + j * 512, 512)], i)
                    sp.dma_start(xt[:], d["x"][0].rearrange("(t p) n -> p t n", p=P)).then_inc(s_ld, 16)
                    sp.dma_start(ct[:], d["ctx"][0].rearrange("(t p) n -> p t n", p=P)).then_inc(s_ld, 16)

                @block.gpsimd
                def _(pool):
                    nc.gpsimd.memset(half[:], -0.5)
                    nc.gpsimd.memset(small[:, 0, :], EPS)
                    nc.gpsimd.memset(small[:, 1, :], HE * EPS)
                    nc.gpsimd.memset(small[:, 2, :], HE ** -0.5)

                @block.scalar
                def _(act):
                    for i, src in enumerate((d["b_ada"][0:1, 2 * DM:3 * DM], d["b_ada"][0:1, 5 * DM:6 * DM],
                                             d["norm_post_mix"], d["norm_post_ffn"])):
                        act.dma_start(grow[:, i, :], src.broadcast_to([P, DM])).then_inc(s_g, 16)
                    act.wait_ge(s_tr, 1)
                    nc.scalar.copy(col[:], bank[0][:, 0:97]).then_inc(s_col, 1)
                    nc.scalar.copy(colconv[:], bank[0][:, 128:200]).then_inc(s_col, 1)
                    nc.scalar.copy(colffn[:], bank[0][:, 256:454]).then_inc(s_col, 1)
                    nc.scalar.activation(cs[:, :, 0], bank[0][:, 81:89], ACT.Silu).then_inc(s_col, 1)
                    nc.scalar.activation(cs[:, :, 1], bank[0][:, 89:97], ACT.Silu).then_inc(s_col, 1)
                    act.sem_inc(s_re, 2)
                    for n in range(8):
                        act.wait_ge(s_rw, n + 1)
                        nc.scalar.copy(rb[:, n // 4, 512 * (n % 4):512 * (n % 4) + 512], bank[6 + n % 2][0:2, :]).then_inc(s_re, 1)

                @block.tensor
                def _(pe):
                    pe.wait_ge(s_row, 16 * 11)
                    nc.tensor.transpose(bank[0][:, 0:97], rowA[:], ident[0:97, 0:97])
                    nc.tensor.transpose(bank[0][:, 128:200], rowB[:], ident[0:72, 0:72])
                    for j in range(2):
                        last = nc.tensor.transpose(bank[0][:, 256 + 99 * j:355 + 99 * j], rowC[:, j, :], ident[0:99, 0:99])
                    last.then_inc(s_tr, 1)
                    pe.wait_ge(s_cs, 1)
                    for part in range(2):
                        with pe.Fori(0, 2) as i:
                            for j in range(2):
                                ring.wait(pe, j, i + 3 * part)
                                pe.wait_ge(s_re, i * 2 + (4 * part + j + 1))
                                for k in range(KT):
                                    last = nc.tensor.matmul(bank[6 + j][0:2, :], cs[:, k, :], ring.view(j, [P, KT, 512])[:, k, :],
                                                            start=(k == 0), stop=(k == KT - 1))
                                last.then_inc(s_rw, 1)
                                pe.wait_ge(s_rw, i * 2 + (4 * part + j + 1))
                                pe.sem_inc(ring.used[j], 1)
                        pe.wait_ge(s_re, 4 * part + 6)
                        for m in range(16):
                            last = nc.tensor.transpose(bank[1][:, 2 * (16 * part + m):2 * (16 * part + m) + 2], rb[:, part, m * P:(m + 1) * P], ident[0:2, 0:2])
                        last.then_inc(s_tc, 1)
                        for j in range(2):
                            ring.wait(pe, j, 3 * part + 2)
                            for k in range(KT):
                                last = nc.tensor.matmul(bank[2 + 2 * part + j][:], csrep[:, k, :], ring.view(j, [P, KT, 512])[:, k, :],
                                                        start=(k == 0), stop=(k == KT - 1))
                            last.then_inc(ring.used[j], 1)

                @block.vector
                def _(dve):
                    link = Link(dve, s_d)
                    dve.wait_ge(s_col, 5)
                    nc.vector.tensor_copy(csrep[:], cs[:, :, 0:1].broadcast_to([P, KT, P])).then_inc(s_cs, 1)
                    dve.wait_ge(s_tc, 2)
                    b = bank[1][:, 0:64].rearrange("p (m c) -> p m c", c=2)
                    for c in range(2):
                        link(nc.vector.tensor_tensor(modc[:, 0:16, c], b[:, 0:16, c], col[:, 0:16], ALU.add))
                        link(nc.vector.tensor_tensor(modc[:, 16:32, c], b[:, 16:32, c], col[:, 24:40], ALU.add))
                    for v, (w, m, c) in enumerate((("pre_mix", 0, 0), ("pre_mix", 0, 1), ("pre_ffn", 16, 0))):
                        o, n = ROWS_A[w]
                        link(nc.vector.tensor_copy(shf[:, v, :], modc[:, m:m + 8, c]))
                        link(nc.vector.scalar_tensor_tensor(wsc[:, v, :], modc[:, m + 8:m + 16, c], 1.0, col[:, o:o + n],
                                                            ALU.add, ALU.mult))
                    dve.wait_ge(s_g, 64)
                    for j in range(2):
                        dve.wait_ge(ring.used[j], 7)
                    for part in range(2):
                        for j in range(2):
                            c = slice(512 * j, 512 * j + 512)
                            link(nc.vector.tensor_tensor(gtrow[:, part, c], bank[2 + 2 * part + j][:], grow[:, part, c], ALU.add))
                            link(nc.vector.tensor_tensor(gtrow[:, part, c], gtrow[:, part, c], grow[:, 2 + part, c], ALU.mult))
        ring.passed(6, 6)
        if dbg is not None and upto == 1:
            dbg("gtrow", gtrow[:]); dbg("wsc", wsc[:]); dbg("shf", shf[:]); dbg("colffn", colffn[:])


        if upto <= 1:
            return

        s_ss, s_rs, s_xn, s_tp = map(sem, "norm_sums norm_rstd normed norm_transposed".split())
        s_spl = sem("norm_split")
        norm_n = {"spl": 0, "ss": 0, "rs": 0, "xn": 0, "tp": 0, "ev": [0, 0], "ld": 0}
        s_hev = [sem("norm_stored_act"), sem("norm_stored_dve")]

        def norm_stage(name, srcs, hT, hi=None, xn=None, loaded=None):
            nb = sum(s[0].shape[1] for s in srcs)
            blocks = [(s[0], t, u) for u, s in enumerate(srcs) for t in range(s[0].shape[1])]
            jobs = [(u, k) for u in range(len(srcs)) for k in range(KT)]
            first = [sum(s[0].shape[1] for s in srcs[:u]) for u in range(len(srcs))]
            z = norm_n
            with ExitStack() as ph:
                xn = xn or sb(ph, name + "_normed", [P, nb, DM])
                ss = sb(ph, name + "_sums", [P, 3, nb])
                with nc.Block() as block:
                    @block.scalar
                    def _(act):
                        if loaded:
                            act.wait_ge(s_ld, loaded)
                        for n, (src, t, u) in enumerate(blocks):
                            nc.scalar.activation(xn[:, n, :], src[:, t, :], ACT.Square, accum_out=ss[:, 0, n:n + 1]).then_inc(s_ss, 1)
                        for n, (u, k) in enumerate(jobs):
                            if n % 2 == 0:
                                src, c, sc, sh = srcs[u]
                                w = src.shape[1] * P
                                act.wait_ge(s_tp, z["tp"] + n + 1)
                                nc.scalar.activation(hT[:, k, c:c + w], bank[n % 8][:, 0:w], ACT.Identity,
                                                     scale=sc[:, k:k + 1],
                                                     bias=sh[:, k:k + 1] if sh is not None else 0.0).then_inc(s_hev[0], 1)

                    @block.gpsimd
                    def _(pool):
                        pool.wait_ge(s_ss, z["ss"] + nb)
                        nc.gpsimd.tensor_scalar(ss[:, 1, :], ss[:, 0, :], 1.0 / DM, EPS, ALU.mult, ALU.add).then_inc(s_rs, 1)
                        pool.wait_ge(s_rs, z["rs"] + 1)
                        nc.gpsimd.tensor_tensor(ss[:, 2, :], ss[:, 1, :], half[:, 0:nb], ALU.pow).then_inc(s_rs, 1)

                    @block.vector
                    def _(dve):
                        dve.wait_ge(s_rs, z["rs"] + 2)
                        for n, (src, t, u) in enumerate(blocks):
                            nc.vector.tensor_scalar(xn[:, n, :], src[:, t, :], ss[:, 2, n:n + 1], None, ALU.mult).then_inc(s_xn, 1)
                        for n, (u, k) in enumerate(jobs):
                            if n % 2 == 1:
                                src, c, sc, sh = srcs[u]
                                w = src.shape[1] * P
                                dve.wait_ge(s_tp, z["tp"] + n + 1)
                                nc.vector.tensor_scalar(hT[:, k, c:c + w], bank[n % 8][:, 0:w], sc[:, k:k + 1],
                                                        sh[:, k:k + 1] if sh is not None else None, ALU.mult,
                                                        ALU.add if sh is not None else ALU.bypass).then_inc(s_hev[1], 1)
                        ring.finish_split(dve)
                        if hi is not None:
                            for k in range(0, KT, 2):
                                for e in range(2):
                                    dve.wait_ge(s_hev[e], z["ev"][e] + k // 2 + 1)
                                split_all(dve, s_spl, rounded(hi)[:, k:k + 2, :], hT[:, k:k + 2, :], rounded(hT)[:, k:k + 2, :], z["spl"] + k)

                    @block.tensor
                    def _(pe):
                        for n, (u, k) in enumerate(jobs):
                            nt = srcs[u][0].shape[1]
                            if n >= 8:
                                pe.wait_ge(s_hev[n % 2], z["ev"][n % 2] + (n - 8) // 2 + 1)
                            for t in range(nt):
                                if n == 0 or (u == 1 and k == 0):
                                    pe.wait_ge(s_xn, z["xn"] + first[u] + t + 1)
                                last = nc.tensor.transpose(bank[n % 8][:, t * P:(t + 1) * P],
                                                           xn[:, first[u] + t, k * P:(k + 1) * P], ident)
                            last.then_inc(s_tp, 1)
            z["ss"] += nb
            z["rs"] += 2
            z["xn"] += nb
            z["tp"] += len(jobs)
            for e in range(2):
                z["ev"][e] += len(jobs) // 2
            if hi is not None:
                z["spl"] += KT

        def post_norm(part, ph, name, xin=None):
            ss = sb(ph, name + "_post_sums", [P, 3, 8])
            junk = sb(ph, name + "_post_squares_buf", [P, 2, 512])
            s_sq, s_rs, s_o = sem(name + "_post_squares"), sem(name + "_post_rstd"), sem(name + "_post_out")

            def act_(act, ready):
                for b in range(8):
                    ready(act, b)
                    if b >= 2:
                        act.wait_ge(s_sq, b - 1)
                    nc.scalar.activation(junk[:, b % 2], bank[b][:], ACT.Square, accum_out=ss[:, 0, b:b + 1]).then_inc(s_sq, 1)

            def pool_(pool):
                pool.wait_ge(s_sq, 8)
                v = ss[:, 0, :].rearrange("p (t a) -> p t a", a=2)
                nc.gpsimd.tensor_tensor(ss[:, 1, 0:4], v[:, :, 0], v[:, :, 1], ALU.add).then_inc(s_rs, 1)
                pool.wait_ge(s_rs, 1)
                nc.gpsimd.tensor_scalar(ss[:, 1, 0:4], ss[:, 1, 0:4], 1.0 / DM, EPS, ALU.mult, ALU.add).then_inc(s_rs, 1)
                pool.wait_ge(s_rs, 2)
                nc.gpsimd.tensor_tensor(ss[:, 2, 0:4], ss[:, 1, 0:4], half[:, 0:4], ALU.pow).then_inc(s_rs, 1)

            def dve_(dve):
                dve.wait_ge(s_rs, 3)
                for b in range(8):
                    t, c = b // 2, slice(512 * (b % 2), 512 * (b % 2) + 512)
                    if b >= 2:
                        dve.wait_ge(s_o, 2 * b - 2)
                    nc.vector.scalar_tensor_tensor(junk[:, b % 2], bank[b][:], ss[:, 2, t:t + 1], gtrow[:, part, c],
                                                   ALU.mult, ALU.mult).then_inc(s_o, 1)
                    dve.wait_ge(s_o, 2 * b + 1)
                    nc.vector.tensor_tensor(xt[:, t, c], (xt if xin is None else xin)[:, t, c], junk[:, b % 2], ALU.add).then_inc(s_o, 1)

            return act_, pool_, dve_

        def first_mixer():
            win = d["w_in"][0].rearrange("(k p) n -> p k n", p=P)

            def head_slab(sp, h):
                for j, o in enumerate((OFF_Q, OFF_K, OFF_V, OFF_Z)):
                    src = win[:, :, bass.ds(h * P + o, P)]
                    sp.dma_start(ring.view(0, [P, 4, KT, P])[:, j], src).then_inc(ring.ready[0], 16)

            norm_stage("mix", [(xt, 0, wsc[:, 0, :], shf[:, 0, :]), (ct, SEQ, wsc[:, 1, :], shf[:, 1, :])], hT, loaded=32)
            ctx_in.close()
            if dbg is not None and upto == 2:
                dbg("hT", hT[:]); return

            NU = 2 * TT
            gu = sb(delta, "log_decay", [P, HD, NU])
            bu = sb(delta, "beta", [P, HD, NU])
            eg = sb(delta, "exp_decay_from_start", [P, HD, NU])
            et = sb(delta, "exp_decay_to_end", [P, HD, NU])
            el = sb(delta, "exp_decay_of_chunk", [P, HD, NU])
            oT = sb(delta, "mix_out_fm", [P, HD, SEQ])
            loop = es.enter_context(ExitStack())
            lev = sb(loop, "level_masks", [P, LEVELS, 2, P])
            with ExitStack() as ph:
                wba = sb(ph, "w_beta_alpha", [P, KT, 32])
                rows = sb(ph, "decay_rows", [P, 2, 16])
                t = sb(ph, "decay_work", [P, 8, TT, 16])
                e_ld, e_mm, e_dv, e_ac, e_pl = map(sem, "decay_loads decay_products decay_dve decay_act decay_cumsum".split())
                with nc.Block() as block:
                    @block.sync
                    def _(sp):
                        sp.dma_start(wba[:], win[:, :, OFF_B:OFF_G]).then_inc(e_ld, 16)
                        sp.dma_start(rows[:, 0, :], d["a_log"].rearrange("a b c -> a (b c)").broadcast_to([P, 16])).then_inc(e_ld, 16)
                        sp.dma_start(rows[:, 1, :], d["dt_bias"].rearrange("a b c -> a (b c)").broadcast_to([P, 16])).then_inc(e_ld, 16)
                        sp.dma_start(lev[:], d["k_lev"]).then_inc(e_ld, 16)
                        sp.wait_ge(ring.used[0], ring.n[0] + 1)
                        head_slab(sp, 0)

                    @block.tensor
                    def _(pe):
                        pe.wait_ge(e_ld, 64)
                        for c in range(TT):
                            for k in range(KT):
                                last = nc.tensor.matmul(bank[0][:, 32 * c:32 * c + 32], hT[:, k, c * P:(c + 1) * P], wba[:, k, :],
                                                        start=(k == 0), stop=(k == KT - 1))
                        last.then_inc(e_mm, 1)
                        pe.wait_ge(e_dv, 13)
                        g = gu[:].rearrange("p h u -> p (h u)")
                        for n, m in enumerate((m_le, m_ge, m_gt, m_lt, m_ones)):
                            last = nc.tensor.matmul(bank[1][:, n * 96:(n + 1) * 96], m, g, start=True, stop=True)
                        last.then_inc(e_mm, 1)

                    @block.scalar
                    def _(act):
                        act.wait_ge(e_dv, 1)
                        b = bank[0][:, 0:192].rearrange("p (c n) -> p c n", n=32)
                        nc.scalar.activation(t[:, 0], b[:, :, 0:16], ACT.Sigmoid).then_inc(e_ac, 1)
                        nc.scalar.activation(rows[:, 0, :], rows[:, 0, :], ACT.Exp).then_inc(e_ac, 1)
                        act.wait_ge(e_dv, 3)
                        nc.scalar.activation(t[:, 3], t[:, 2], ACT.Exp).then_inc(e_ac, 1)
                        act.wait_ge(e_ac, 3)
                        nc.scalar.activation(t[:, 4], t[:, 3], ACT.Ln, bias=1.0).then_inc(e_ac, 1)
                        act.wait_ge(e_mm, 2)
                        b = bank[1][:, 0:480].rearrange("p (n h g d c) -> p n h g d c", n=5, h=HD, g=3, d=2)
                        v = lambda x: x[:].rearrange("p h (g d c) -> p h g d c", g=3, d=2)
                        for dr in range(2):
                            nc.scalar.activation(v(eg)[:, :, :, dr], b[:, dr, :, :, dr], ACT.Exp)
                            nc.scalar.activation(v(et)[:, :, :, dr], b[:, 2 + dr, :, :, dr], ACT.Exp)
                        nc.scalar.activation(el[:].rearrange("p h u -> p (h u)"), bank[1][:, 384:480], ACT.Exp).then_inc(e_ac, 1)

                    @block.vector
                    def _(dve):
                        link = Link(dve, e_dv)
                        dve.wait_ge(e_mm, 1)
                        b = bank[0][:, 0:192].rearrange("p (c n) -> p c n", n=32)
                        row = lambda r: rows[:, r:r + 1, :].broadcast_to([P, TT, 16])
                        link(nc.vector.tensor_tensor(t[:, 1], b[:, :, 16:32], row(1), ALU.add))
                        link(nc.vector.tensor_scalar(t[:, 5], t[:, 1], -1.0, None, ALU.mult))
                        link(nc.vector.tensor_tensor(t[:, 2], t[:, 1], t[:, 5], ALU.min))
                        dve.wait_ge(e_ac, 4)
                        link(nc.vector.tensor_scalar(t[:, 6], t[:, 3], 1.0, None, ALU.add))
                        link(nc.vector.tensor_scalar(t[:, 6], t[:, 6], -1.0, None, ALU.add))
                        link(nc.vector.tensor_tensor(t[:, 6], t[:, 3], t[:, 6], ALU.subtract))
                        link(nc.vector.tensor_tensor(t[:, 6], t[:, 4], t[:, 6], ALU.add))
                        link(nc.vector.scalar_tensor_tensor(t[:, 6], t[:, 1], 0.0, t[:, 6], ALU.max, ALU.add))
                        link(nc.vector.scalar_tensor_tensor(t[:, 7], t[:, 6], -1.0, row(0), ALU.mult, ALU.mult))
                        for dst, src in ((bu, 0), (gu, 7)):
                            s = t[:, src].rearrange("p (g c) n -> p n g c", g=3)
                            v = dst[:].rearrange("p h (g d c) -> p h g d c", g=3, d=2)
                            for dr in range(2):
                                for g in range(3):
                                    last = nc.vector.tensor_copy(v[:, :, g, dr], s[:, dr * HD:(dr + 1) * HD, g])
                                link(last)
            ring.passed(0, 0)
            if dbg is not None and upto == 3:
                dbg("gu", gu[:]); dbg("bu", bu[:]); dbg("eg", eg[:]); dbg("et", et[:]); dbg("el", el[:]); return

            W3 = SEQ + 2 + CTX
            with ExitStack() as ph:
                dsem = ph.enter_context(local_sems())
                cin = sb(ph, "conv_in", [P, 3, W3 + 2])
                y = sb(ph, "conv_out", [P, 3, W3])
                zs = sb(ph, "z_silu", [P, SEQ])
                zr = sb(ph, "z_raw", [P, SEQ])
                qk = sb(ph, "qk_tm", [P, TX + TT, P])
                vt = sb(ph, "v_tm", [P, TT, P])
                sqr = sb(ph, "squares_or_out", [P, TX + TT, P])
                qn = sb(ph, "qk_normed", [P, TX + TT, P])
                ns = sb(ph, "norm_work", [P, 4, TX + TT])
                qkT = sb(ph, "qk_fm", [P, TX + TT, P])
                xf = xt[:].rearrange("p t n -> p (t n)")
                R = xf[:, 0:2560].rearrange("p (u n) -> p u n", u=20)
                bm = xf[:, 2560:4096].rearrange("p (u n) -> p u n", u=12)
                D = sb(ph, "decay_units", [P, 12, P])
                DT = sb(ph, "decay_units_t", [P, 8, P])
                L = sb(ph, "l_units", [P, 12, P])
                X = sb(ph, "inverse", [P, 12, P])
                Y = sb(ph, "inverse_t", [P, 12, P])
                Ts = sb(ph, "level_product", [P, 12, P])
                S = sb(ph, "state", [P, 2, 2, P])
                VN = sb(ph, "v_new", [P, 2, 2, P])
                PT, QeT, NW, oacc = DT, L, X, sqr
                Ke, Qe, Kt = R[:, 0:12, :], R[:, 12:20, :], bm
                units = lambda a, n=3: a[:, 0:4 * n, :].rearrange("p (g d c) n -> p g d c n", g=n, d=2)
                per_unit = lambda a, h, dr, n=3: (a[:, bass.ds(h, 1), :].rearrange("p a (g d c) -> p (a g) d c", g=3, d=2)
                                                  [:, 0:n, dr, :].unsqueeze(3).broadcast_to([P, n, 2, P]))
                mask = lambda m, n=3: m.rearrange("p (a b n) -> p a b n", a=1, b=1).broadcast_to([P, n, 2, P])
                grp = lambda b: b[:].rearrange("p (u n) -> p u n", u=4)
                bankg = lambda b: b[:].rearrange("p (d c n) -> p d c n", d=2, c=2)

                class Event:

                    def __init__(self, name, per):
                        self.s, self.per = dsem("dn_" + name), per

                    def wait(self, eng, h, n, ahead=0):
                        eng.wait_ge(self.s, h * self.per + (ahead * self.per + n))

                    def last(self, eng, h):
                        eng.wait_ge(self.s, h * self.per)

                ev = {n: Event(n, k) for n, k in dict(
                    projected=5, conv_in_filled=5, z_copied=1, z_ready=1, conv_done=3, conv_silu=3, tm_turned=4, tm_stored=4,
                    squared=1, qk_sums=1, qk_rstd=3, qk_scaled=1, fm_turned=3, fm_stored=3, steps_ready=4, decay_products=5, decay_exp=5,
                    beta_masked=2, decay_masked=2, decay_masked_t=2, kk_products=3, l_ready=3, p_ready=2, x_first=6, y_first=3, y_stored=3,
                    level_t=18, level_ts=18, level_dy=18, level_y=18, level_x_turned=15, level_x=15,
                    y_beta=3, k_scaled=6, q_turned=2, q_stored=2, w_products=3, w_stored=3,
                    v_products=6, v_stored=6, o_products=4, o_stored=4, s_products=6, s_stored=6,
                    o_squared=1, o_sums=1, o_rstd=2, o_normed=1, o_turned=1, o_gated=1).items()}
                s_pad, s_conv, s_gate = dsem("dn_padding"), dsem("dn_conv_chain"), dsem("dn_gate_chain")
                PIECES = {"q": [(0, slice(0, SEQ), 7, 0)], "ctx": [(1, slice(SEQ, SEQ + CTX), 1, 0), (2, slice(SEQ, SEQ + CTX), 1, CTX)],
                          "k": [(1, slice(0, SEQ), 2, 0)], "v": [(2, slice(0, SEQ), 1, 0)], "z": [(3, slice(0, SEQ), 2, 0)]}
                FILL = [("ctx", 0, 4), ("ctx", 4, 8), ("ctx", 8, 12), ("ctx", 12, 16), ("k", 0, 2), ("k", 2, 4), ("k", 4, 6), ("k", 6, 8),
                        ("v", 0, 2), ("v", 2, 5), ("v", 5, 8)]
                inc = lambda ins, n: ins.then_inc(ev[n].s, 1)
                STEPS = [(4, 5), (5, 4), (0, 3), (1, 2), (2, 1), (3, 0)]
                unit = lambda c, dr: (c // 2) * 4 + dr * 2 + c % 2
                VB, OB, SB = (3, 4), (5, 0), (6, 7)
                turned = ((0, 5), (4, 6), (0, 7))
                with nc.Block() as block:
                    @block.sync
                    def _(sp):
                        with sp.Fori(1, HD) as h:
                            sp.wait_ge(ev["projected"].s, h * 5)
                            head_slab(sp, h)
                        sp.wait_ge(ev["projected"].s, 5 * HD)
                        sp.sem_inc(ring.used[0], 4 * HD)

                    @block.tensor
                    def _(pe):
                        w = ring.view(0, [P, 4, KT, P])

                        def project(piece, a, b):
                            jobs = [(x, k) for x in PIECES[piece] for k in range(KT)]
                            for (j, cols, bk, o), k in jobs[a:b]:
                                last = nc.tensor.matmul(bank[bk][:, o:o + cols.stop - cols.start], w[:, j, k, :], hT[:, k, cols],
                                                        start=(k == 0), stop=(k == KT - 1))
                            if b == len(jobs):
                                inc(last, "projected")

                        def turn(h, more):
                            ev["o_stored"].last(pe, h)
                            for j in range(3):
                                ev["conv_silu"].wait(pe, h, j + 1)
                                b = turned[j][1]
                                for t in range(TX):
                                    last = nc.tensor.transpose(bank[b][:, t * P:(t + 1) * P], y[:, j, t * P:(t + 1) * P], ident)
                                inc(last, "tm_turned")
                            for j in (1, 2):
                                for t in range(TC):
                                    o = SEQ + 2 + t * P
                                    last = nc.tensor.transpose(bank[0][:, ((j - 1) * 2 + t) * P:((j - 1) * 2 + t + 1) * P], y[:, j, o:o + P], ident)
                            inc(last, "tm_turned")
                            ev["steps_ready"].wait(pe, h, 4)
                            for n, b in enumerate((4, 5, 6, 7, 0)):
                                if n:
                                    ev["tm_stored"].wait(pe, h, n)
                                u0 = 4 * n
                                for dr in range(2):
                                    m = ((m_le, m_ge), (m_gt, m_lt))[n // 3][dr]
                                    last = nc.tensor.matmul(bank[b][:, 256 * dr:256 * dr + 256], m, R[:, u0 + 2 * dr:u0 + 2 * dr + 2, :], start=True, stop=True)
                                inc(last, "decay_products")
                            ev["qk_scaled"].wait(pe, h, 1)
                            ev["conv_in_filled"].wait(pe, h, 5)
                            ev["z_copied"].wait(pe, h, 1)
                            ev["o_gated"].last(pe, h)
                            for n, (b, t0, nt) in enumerate(((1, 0, 4), (2, 4, 4), (3, 8, 2))):
                                for t in range(nt):
                                    last = nc.tensor.transpose(bank[b][:, t * P:(t + 1) * P], qn[:, t0 + t, :], ident)
                                inc(last, "fm_turned")
                            ev["fm_stored"].wait(pe, h, 3)
                            for n, (b, cs_, qo) in enumerate(((1, (0, 1, 2, 3), 4), (2, (4, 5), 4), (3, (0, 1, 2, 3), 0))):
                                for i, c in enumerate(cs_):
                                    last = nc.tensor.matmul(bank[b][:, i * P:(i + 1) * P], qkT[:, 4 + c, :], qkT[:, qo + c, :], start=True, stop=True)
                                inc(last, "kk_products")
                            if more:
                                pe.wait_ge(ring.ready[0], h * 64 + (16 * ring.n[0] + 128))
                                ev["decay_exp"].wait(pe, h, 4)
                                project("q", 0, 8)
                            for g in range(3):
                                ev["decay_exp"].wait(pe, h, 3) if g == 0 else None
                                ev["x_first"].wait(pe, h, 2 * g + 2)
                                for i in range(4):
                                    last = nc.tensor.transpose(bank[4 + g][:, i * P:(i + 1) * P], X[:, 4 * g + i, :], ident)
                                inc(last, "y_first")
                            ev["decay_exp"].wait(pe, h, 5)
                            ev["p_ready"].wait(pe, h, 2)
                            for n in range(1, LEVELS):
                                for g in range(3):
                                    if n == 1:
                                        ev["y_stored"].wait(pe, h, g + 1)
                                    else:
                                        ev["level_x"].wait(pe, h, 3 * (n - 2) + g + 1)
                                    for i in range(4):
                                        u = 4 * g + i
                                        last = nc.tensor.matmul(bank[g][:, i * P:(i + 1) * P], L[:, u, :], Y[:, u, :], start=True, stop=True)
                                    inc(last, "level_t")
                                for g in range(3):
                                    ev["level_ts"].wait(pe, h, 3 * (n - 1) + g + 1)
                                    for i in range(4):
                                        u = 4 * g + i
                                        last = nc.tensor.matmul(bank[4 + g][:, i * P:(i + 1) * P], X[:, u, :], Ts[:, u, :], start=True, stop=True)
                                    inc(last, "level_dy")
                                if n < LEVELS - 1:
                                    for g in range(3):
                                        ev["level_y"].wait(pe, h, 3 * (n - 1) + g + 1)
                                        for i in range(4):
                                            u = 4 * g + i
                                            last = nc.tensor.transpose(bank[g][:, i * P:(i + 1) * P], Y[:, u, :], ident)
                                        inc(last, "level_x_turned")
                            ev["k_scaled"].wait(pe, h, 6)
                            if more:
                                ev["conv_in_filled"].wait(pe, h, 1, 1)
                            for n, b in enumerate((3, 7)):
                                for i in range(4):
                                    last = nc.tensor.transpose(bank[b][:, i * P:(i + 1) * P], Qe[:, 4 * n + i, :], ident)
                                inc(last, "q_turned")
                            for g in range(3):
                                ev["y_beta"].wait(pe, h, g + 1)
                                for i in range(4):
                                    u = 4 * g + i
                                    last = nc.tensor.matmul(bank[g][:, i * P:(i + 1) * P], Ke[:, u, :], Y[:, u, :], start=True, stop=True)
                                inc(last, "w_products")
                            def fill(n):
                                if not more:
                                    return
                                if n == 0:
                                    ev["w_stored"].wait(pe, h, 2)
                                if n == 4:
                                    ev["w_stored"].wait(pe, h, 3)
                                if n == 8:
                                    ev["conv_in_filled"].wait(pe, h, 3, 1)
                                project(*FILL[n])

                            ev["q_stored"].wait(pe, h, 2)
                            no = 0
                            for s, cd in enumerate(STEPS):
                                vb, sbk = bank[VB[s % 2]], bank[SB[s % 2]]
                                if s >= 2:
                                    ev["v_stored"].wait(pe, h, s - 1)
                                if s > 0:
                                    fill(2 * s - 1)
                                    ev["w_stored"].wait(pe, h, 3) if s == 1 else None
                                    ev["s_stored"].wait(pe, h, s)
                                for dr, c in enumerate(cd):
                                    u = unit(c, dr)
                                    last = nc.tensor.matmul(vb[:, dr * P:(dr + 1) * P], Y[:, u, :], vt[:, c, :], start=True, stop=(s == 0))
                                    if s > 0:
                                        last = nc.tensor.matmul(vb[:, dr * P:(dr + 1) * P], NW[:, u, :], S[:, s % 2, dr, :], start=False, stop=True)
                                inc(last, "v_products")
                                fill(2 * s)
                                ev["v_stored"].wait(pe, h, s + 1)
                                if s == 0:
                                    ev["level_y"].wait(pe, h, 18)
                                for dr, c in enumerate(cd):
                                    last = nc.tensor.matmul(sbk[:, dr * P:(dr + 1) * P], Kt[:, unit(c, dr), :], VN[:, s % 2, dr, :], start=True, stop=True)
                                inc(last, "s_products")
                                if s >= 2:
                                    ob = bank[OB[no % 2]]
                                    if no >= 2:
                                        ev["o_stored"].wait(pe, h, no - 1)
                                    for dr, c in enumerate(cd):
                                        u = unit(c, dr)
                                        nc.tensor.matmul(ob[:, dr * P:(dr + 1) * P], QeT[:, u, :], S[:, s % 2, dr, :], start=True, stop=False)
                                        last = nc.tensor.matmul(ob[:, dr * P:(dr + 1) * P], PT[:, u, :], VN[:, s % 2, dr, :], start=False, stop=True)
                                    inc(last, "o_products")
                                    no += 1
                            if more:
                                ev["conv_in_filled"].wait(pe, h, 4, 1)
                                project("z", 0, 4)
                            ev["o_normed"].wait(pe, h, 1)
                            for t in range(TX):
                                last = nc.tensor.transpose(bank[3][:, t * P:(t + 1) * P], qn[:, t, :], ident)
                            inc(last, "o_turned")
                            if more:
                                project("z", 4, 8)

                        pe.wait_ge(ring.ready[0], 16 * ring.n[0] + 64)
                        for piece in ("q", "ctx", "k", "v", "z"):
                            if piece == "v":
                                ev["conv_in_filled"].wait(pe, 0, 3)
                            if piece == "z":
                                ev["conv_in_filled"].wait(pe, 0, 4)
                            project(piece, 0, 8 * len(PIECES[piece]))
                        with pe.Fori(0, HD - 1) as h:
                            turn(h, True)
                        turn(HD - 1, False)

                    @block.scalar
                    def _(act):
                        def fill(h, ahead, piece):
                            n = ("q", "ctx", "k", "v").index(piece)
                            ev["projected"].wait(act, h, n + 1, ahead)
                            for j, cols, bk, o in PIECES[piece]:
                                dst = SEQ + 3 if piece == "ctx" else 1
                                w = cols.stop - cols.start
                                inc(nc.scalar.copy(cin[:, j, dst:dst + w], bank[bk][:, o:o + w]), "conv_in_filled")

                        def silu(h, ahead, j):
                            ev["conv_done"].wait(act, h, j + 1, ahead)
                            v = y[:, j, 0:SEQ if j == 0 else W3]
                            inc(nc.scalar.activation(v, v, ACT.Silu), "conv_silu")

                        def copy_z(h, ahead):
                            ev["projected"].wait(act, h, 5, ahead)
                            if ahead:
                                ev["z_ready"].wait(act, h, 1)
                            inc(nc.scalar.copy(zr[:], bank[2][:]), "z_copied")

                        def turn(h, more):
                            for j, dst in enumerate((qk[:, 0:4, :], qk[:, 4:8, :], vt[:, 0:4, :])):
                                ev["tm_turned"].wait(act, h, j + 1)
                                inc(nc.scalar.copy(dst, grp(bank[turned[j][1]])), "tm_stored")
                            ev["tm_turned"].wait(act, h, 4)
                            nc.scalar.copy(qk[:, 8:10, :], grp(bank[0])[:, 0:2])
                            inc(nc.scalar.copy(vt[:, 4:6, :], grp(bank[0])[:, 2:4]), "tm_stored")
                            ev["o_gated"].last(act, h)
                            ev["z_copied"].wait(act, h, 1)
                            inc(nc.scalar.activation(zs[:], zr[:], ACT.Silu), "z_ready")
                            for n, b in enumerate((4, 5, 6, 7, 0)):
                                ev["decay_products"].wait(act, h, n + 1)
                                dst = D[:, 4 * n:4 * n + 4, :] if n < 3 else DT[:, 4 * n - 12:4 * n - 8, :]
                                inc(nc.scalar.activation(dst, grp(bank[b]), ACT.Exp), "decay_exp")
                            for n, (b, t0, nt) in enumerate(((1, 0, 4), (2, 4, 4), (3, 8, 2))):
                                ev["fm_turned"].wait(act, h, n + 1)
                                inc(nc.scalar.copy(qkT[:, t0:t0 + nt, :], grp(bank[b])[:, 0:nt]), "fm_stored")
                            for g in range(3):
                                ev["y_first"].wait(act, h, g + 1)
                                inc(nc.scalar.copy(Y[:, 4 * g:4 * g + 4, :], grp(bank[4 + g])), "y_stored")
                            if more:
                                fill(h, 1, "q")
                            for n in range(1, LEVELS - 1):
                                for g in range(3):
                                    ev["level_x_turned"].wait(act, h, 3 * (n - 1) + g + 1)
                                    inc(nc.scalar.copy(X[:, 4 * g:4 * g + 4, :], grp(bank[g])), "level_x")
                            ev["level_t"].wait(act, h, 18)
                            for n, b in enumerate((3, 7)):
                                ev["q_turned"].wait(act, h, n + 1)
                                inc(nc.scalar.copy(QeT[:, 4 * n:4 * n + 4, :], grp(bank[b])), "q_stored")
                            ev["level_dy"].wait(act, h, 18)
                            for g in range(3):
                                ev["w_products"].wait(act, h, g + 1)
                                inc(nc.scalar.mul(NW[:, 4 * g:4 * g + 4, :], grp(bank[g]), -1.0), "w_stored")
                            for s in range(6):
                                ev["v_products"].wait(act, h, s + 1)
                                if s >= 2:
                                    ev["s_products"].wait(act, h, s - 1)
                                if s >= 4:
                                    ev["o_products"].wait(act, h, s - 3)
                                inc(nc.scalar.copy(VN[:, s % 2], bank[VB[s % 2]][:, 0:256].rearrange("p (d n) -> p d n", d=2)), "v_stored")
                                if more and s in (2, 4, 5):
                                    fill(h, 1, {2: "ctx", 4: "k", 5: "v"}[s])
                            if more:
                                for j in range(3):
                                    silu(h, 1, j)
                                copy_z(h, 1)

                        act.wait_ge(s_pad, 1)
                        for piece in ("q", "ctx", "k", "v"):
                            fill(0, 0, piece)
                        copy_z(0, 0)
                        for j in range(3):
                            silu(0, 0, j)
                        with act.Fori(0, HD - 1) as h:
                            turn(h, True)
                        turn(HD - 1, False)

                    @block.gpsimd
                    def _(pool):
                        def steps(h):
                            for dr in range(2):
                                inc(nc.gpsimd.tensor_tensor(units(R)[:, :, dr], per_unit(gu, h, dr), mask((m_gt, m_lt)[dr]), ALU.mult), "steps_ready")
                            rt = R[:, 12:20, :].rearrange("p (g d c) n -> p g d c n", g=2, d=2)
                            for dr in range(2):
                                inc(nc.gpsimd.tensor_tensor(rt[:, :, dr], per_unit(gu, h, dr, 2), mask((m_le, m_ge)[dr], 2), ALU.mult), "steps_ready")

                        def turn(h, more):
                            ev["s_products"].last(pool, h)
                            for dr in range(2):
                                inc(nc.gpsimd.tensor_tensor(units(bm)[:, :, dr], per_unit(bu, h, dr), mask((m_gt, m_lt)[dr]), ALU.mult), "beta_masked")
                            ev["qk_sums"].wait(pool, h, 1)
                            inc(nc.gpsimd.tensor_tensor(ns[:, 1, :], ns[:, 0, :], small[:, 0, 0:TX + TT], ALU.add), "qk_rstd")
                            ev["qk_rstd"].wait(pool, h, 1)
                            inc(nc.gpsimd.tensor_tensor(ns[:, 2, :], ns[:, 1, :], half[:, 0:TX + TT], ALU.pow), "qk_rstd")
                            ev["qk_rstd"].wait(pool, h, 2)
                            inc(nc.gpsimd.tensor_tensor(ns[:, 2, 0:4], ns[:, 2, 0:4], small[:, 2, 0:4], ALU.mult), "qk_rstd")
                            ev["beta_masked"].wait(pool, h, 2)
                            for dr in range(2):
                                ev["decay_exp"].wait(pool, h, 3)
                                inc(nc.gpsimd.tensor_tensor(units(D)[:, :, dr], units(D)[:, :, dr], units(bm)[:, :, dr], ALU.mult), "decay_masked")
                            for dr in range(2):
                                ev["decay_exp"].wait(pool, h, 5)
                                inc(nc.gpsimd.tensor_tensor(units(DT, 2)[:, :, dr], units(DT, 2)[:, :, dr], mask((m_le, m_ge)[dr], 2), ALU.mult), "decay_masked_t")
                            ev["qk_scaled"].wait(pool, h, 1)
                            ev["decay_products"].wait(pool, h, 5)
                            ev["decay_masked"].wait(pool, h, 2)
                            kv = qn[:, 4:10, :].rearrange("p (g c) n -> p g c n", g=3)
                            qv = qn[:, 0:4, :].rearrange("p (g c) n -> p g c n", g=2)
                            for dr in range(2):
                                inc(nc.gpsimd.tensor_tensor(units(Qe, 2)[:, :, dr], qv, per_unit(eg, h, dr, 2), ALU.mult), "k_scaled")
                            for dr in range(2):
                                inc(nc.gpsimd.tensor_tensor(units(Ke)[:, :, dr], kv, per_unit(eg, h, dr), ALU.mult), "k_scaled")
                                inc(nc.gpsimd.tensor_tensor(units(Kt)[:, :, dr], kv, per_unit(et, h, dr), ALU.mult), "k_scaled")
                            if more:
                                ev["w_products"].wait(pool, h, 3)
                                ev["q_turned"].wait(pool, h, 2)
                                steps(h + 1)
                            ev["o_sums"].wait(pool, h, 1)
                            inc(nc.gpsimd.tensor_tensor(ns[:, 1, 0:4], ns[:, 0, 0:4], small[:, 1, 0:4], ALU.add), "o_rstd")
                            ev["o_rstd"].wait(pool, h, 1)
                            inc(nc.gpsimd.tensor_tensor(ns[:, 2, 0:4], ns[:, 1, 0:4], half[:, 0:4], ALU.pow), "o_rstd")

                        steps(0)
                        with pool.Fori(0, HD - 1) as h:
                            turn(h, True)
                        turn(HD - 1, False)

                    @block.vector
                    def _(dve):
                        nc.vector.memset(cin[:], 0.0).then_inc(s_pad, 1)
                        dve.wait_ge(s_pad, 1)
                        def conv(h, ahead, j):
                            ev["conv_in_filled"].wait(dve, h, (1, 4, 5)[j], ahead)
                            w = SEQ if j == 0 else W3
                            n = 2 * j + 6 * ahead
                            tap = lambda a: colconv[:, bass.ds(h + (a * 24 + j * HD + ahead), 1)]
                            nc.vector.tensor_scalar(y[:, j, 0:w], cin[:, j, 1:1 + w], tap(1), None, ALU.mult).then_inc(s_conv, 1)
                            dve.wait_ge(s_conv, h * 6 + (n + 1))
                            nc.vector.scalar_tensor_tensor(y[:, j, 0:w], cin[:, j, 0:w], tap(0), y[:, j, 0:w], ALU.mult, ALU.add).then_inc(s_conv, 1)
                            dve.wait_ge(s_conv, h * 6 + (n + 2))
                            inc(nc.vector.scalar_tensor_tensor(y[:, j, 0:w], cin[:, j, 2:2 + w], tap(2), y[:, j, 0:w], ALU.mult, ALU.add), "conv_done")

                        def turn(h, more):
                            ev["tm_stored"].wait(dve, h, 4)
                            inc(nc.vector.tensor_tensor(sqr[:], qk[:], qk[:], ALU.mult), "squared")
                            ev["squared"].wait(dve, h, 1)
                            inc(nc.vector.reduce_sum(ns[:, 0, :], sqr[:], axis=AX), "qk_sums")
                            ev["qk_rstd"].wait(dve, h, 3)
                            inc(nc.vector.tensor_tensor(qn[:], qk[:], ns[:, 2, :].unsqueeze(2).broadcast_to([P, TX + TT, P]), ALU.mult), "qk_scaled")
                            ev["decay_masked"].wait(dve, h, 2)
                            for g in range(3):
                                ev["kk_products"].wait(dve, h, 1 if g < 2 else 2)
                                kk = (grp(bank[1])[:, 2 * g:2 * g + 2] if g < 2 else grp(bank[2])[:, 0:2])
                                kk = kk.unsqueeze(1).broadcast_to([P, 2, 2, P])
                                inc(nc.vector.tensor_tensor(units(L)[:, g], kk, units(D)[:, g], ALU.mult), "l_ready")
                            ev["decay_masked_t"].wait(dve, h, 2)
                            ev["kk_products"].wait(dve, h, 3)
                            for g in range(2):
                                kq = grp(bank[3])[:, 2 * g:2 * g + 2].unsqueeze(1).broadcast_to([P, 2, 2, P])
                                inc(nc.vector.tensor_tensor(units(PT, 2)[:, g], kq, units(DT, 2)[:, g], ALU.mult), "p_ready")
                            for g in range(3):
                                ev["l_ready"].wait(dve, h, g + 1)
                                for dr in range(2):
                                    m = lev[:, 0, 1 - dr:2 - dr, :].broadcast_to([P, 2, P])
                                    last = nc.vector.tensor_tensor(units(X)[:, g, dr], units(L)[:, g, dr], m, ALU.mult)
                                inc(last, "x_first")
                                ev["x_first"].wait(dve, h, 2 * g + 1)
                                idb = ident.unsqueeze(1).broadcast_to([P, 4, P])
                                inc(nc.vector.tensor_tensor(X[:, 4 * g:4 * g + 4, :], idb, X[:, 4 * g:4 * g + 4, :], ALU.subtract), "x_first")
                            for n in range(1, LEVELS):
                                for g in range(3):
                                    ev["level_t"].wait(dve, h, 3 * (n - 1) + g + 1)
                                    m = lev[:, n].unsqueeze(2).broadcast_to([P, 2, 2, P])
                                    inc(nc.vector.tensor_tensor(units(Ts)[:, g], bankg(bank[g]), m, ALU.mult), "level_ts")
                                for g in range(3):
                                    ev["level_dy"].wait(dve, h, 3 * (n - 1) + g + 1)
                                    yv = Y[:, 4 * g:4 * g + 4, :]
                                    inc(nc.vector.tensor_tensor(yv, yv, grp(bank[4 + g]), ALU.subtract), "level_y")
                            for g in range(3):
                                ev["level_y"].wait(dve, h, 15 + g + 1)
                                yv = Y[:, 4 * g:4 * g + 4, :]
                                bv = bu[:, bass.ds(h, 1), 4 * g:4 * g + 4].rearrange("p a u -> p (a u)").unsqueeze(2).broadcast_to([P, 4, P])
                                inc(nc.vector.tensor_tensor(yv, yv, bv, ALU.mult), "y_beta")
                            for s, cd in enumerate(STEPS):
                                ev["s_products"].wait(dve, h, s + 1)
                                b = bank[SB[s % 2]]
                                if s >= 1:
                                    ev["v_products"].wait(dve, h, s)
                                for dr, c in enumerate(cd):
                                    src = b[:, dr * P:(dr + 1) * P]
                                    dst = S[:, (s + 1) % 2, dr, :]
                                    if s == 0:
                                        last = nc.vector.tensor_copy(dst, src)
                                    else:
                                        if dr == 0:
                                            ev["s_stored"].wait(dve, h, s)
                                            if s >= 3:
                                                ev["o_products"].wait(dve, h, s - 2)
                                        dec = el[:, bass.ds(h, 1), unit(c, dr)]
                                        last = nc.vector.scalar_tensor_tensor(dst, S[:, s % 2, dr, :], dec, src, ALU.mult, ALU.add)
                                inc(last, "s_stored")
                                if s >= 2:
                                    ev["o_products"].wait(dve, h, s - 1)
                                    ob = bank[OB[s % 2]]
                                    if s >= 4:
                                        ev["o_stored"].wait(dve, h, 2)
                                    for dr, c in enumerate(cd):
                                        src = ob[:, dr * P:(dr + 1) * P]
                                        dst = oacc[:, c, :]
                                        if s < 4:
                                            last = nc.vector.tensor_copy(dst, src)
                                        else:
                                            last = nc.vector.tensor_tensor(dst, dst, src, ALU.add)
                                    inc(last, "o_stored")
                                if more and s in (1, 4):
                                    conv(h, 1, s // 4)
                            ev["o_stored"].wait(dve, h, 4)
                            inc(nc.vector.tensor_tensor(sqr[:, 4:8, :], oacc[:, 0:4, :], oacc[:, 0:4, :], ALU.mult), "o_squared")
                            ev["o_squared"].wait(dve, h, 1)
                            inc(nc.vector.reduce_sum(ns[:, 0, 0:4], sqr[:, 4:8, :], axis=AX), "o_sums")
                            if more:
                                conv(h, 1, 2)
                            ev["o_rstd"].wait(dve, h, 2)
                            inc(nc.vector.tensor_tensor(qn[:, 0:4, :], oacc[:, 0:4, :], ns[:, 2, 0:4].unsqueeze(2).broadcast_to([P, 4, P]), ALU.mult), "o_normed")
                            ev["o_turned"].wait(dve, h, 1)
                            og = PT[:, 0:4, :].rearrange("p t n -> p (t n)")
                            nc.vector.tensor_scalar(og, bank[3][:], colof("dn"), HE ** 0.5, ALU.mult, ALU.mult).then_inc(s_gate, 1)
                            dve.wait_ge(s_gate, h * 1 + 1)
                            inc(nc.vector.tensor_tensor(oT[:, bass.ds(h, 1), :].rearrange("p a n -> p (a n)"), og, zs[:], ALU.mult), "o_gated")

                        for j in range(3):
                            conv(0, 0, j)
                        with dve.Fori(0, HD - 1) as h:
                            turn(h, True)
                        turn(HD - 1, False)
                if dbg is not None and upto == 4:
                    for nme, bf in dict(qn=qn, vt=vt, D=D, DT=DT, Y=Y, S=S, oacc=oacc, Kt=Kt, zs=zs).items():
                        dbg(nme, bf[:])
            loop.close()
            ring.passed(4 * HD, 0)
            ring.start_split(plan_mix + plan_ffn + plan_fox + plan_dsw, ring.n[0], ring.n[1])
            if dbg is not None and upto == 4:
                dbg("oT", oT[:]); return

            with ExitStack() as ph:
                fT = sb(ph, "fourier_in_fm", [P, 4, SEQ])
                fa = sb(ph, "fourier_channels", [P, TX, 4, 2 * P])
                x0 = fa[:].rearrange("p t g n -> p t (g n)")
                dft = sb(ph, "dft_tokens", [P, 2, TX, SEQ])
                mh = rounded(dft)[:].rearrange("p a t n -> p (a t) n")
                dfc = sb(ph, "dft_channels", [P, 2 * P])
                fo = sb(ph, "fourier_out_fm", [P, 4, SEQ])
                ga = sb(ph, "gates", [P, 2, 4, SEQ])
                hh = sb(ph, "h_high", [P, KT, SEQ])
                oh = sb(ph, "mix_out_high", [P, HD, SEQ])
                mg = xt[:].rearrange("p t (a n) -> p (t a) n", a=2)
                mgr = rounded(xt)[:].rearrange("p t (a n) -> p (t a) n", a=2)
                fTr, for_, hhr, hTr, ohr, oTr = map(rounded, (fT, fo, hh, hT, oh, oT))
                m_sh, m_so, m_sf, m_sm = map(sem, "mix_h_split mix_delta_split mix_fourier_split mix_merged_split".split())
                m_ld, m_f, m_fe, m_pr, m_g, m_yf, m_t, m_m, m_w = map(sem, (
                    "mix_loads fourier_products fourier_stored mix_products gates_ready fourier_gated delta_gated merged mix_out").split())
                post_act, post_pool, post_dve = post_norm(0, ph, "mix", xin=x0)
                with nc.Block() as block:
                    @block.sync
                    def _(sp):
                        for q in range(2):
                            ring.load_split(sp, q)
                        sp.dma_start(dfc[:], d["k_dft_c"]).then_inc(m_ld, 16)
                        sp.dma_start(dft[:], d["k_dft_t"]).then_inc(m_ld, 16)
                        for q in range(2, len(plan_mix) + 2):
                            ring.load_split(sp, q)
                            if q == 5:
                                sp.wait_ge(m_f, 16)
                                sp.dma_start(x0, d["x"][0].rearrange("(t p) n -> p t n", p=P)).then_inc(m_ld, 16)

                    @block.tensor
                    def _(pe):
                        h_ready = lambda m: pe.wait_ge(m_sh, 4) if m == 0 else None
                        slab_products(pe, ring, 0, bank[0:4], *fm((hhr, hTr)), m_f, 4, before=h_ready)
                        pe.wait_ge(m_ld, 32)
                        pe.wait_ge(m_fe, 4)
                        for t in range(TX):
                            for g in range(4):
                                last = nc.tensor.matmul(bank[4 + t][:, (g % 2) * 256:(g % 2) * 256 + 256] if g < 2 else
                                                        bank[t][:, (g % 2) * 256:(g % 2) * 256 + 256],
                                                        fT[:, g, t * P:(t + 1) * P], dfc[:], start=True, stop=True)
                                if g % 2:
                                    last.then_inc(m_f, 1)
                        for g in range(4):
                            pe.wait_ge(m_fe, 12)
                            n = 0
                            for t in range(TX):
                                for c in range(2):
                                    last = nc.tensor.matmul(bank[4 + g][:], fa[:, t, g, c * P:(c + 1) * P], dft[:, c, t, :], start=(n == 0), stop=(n == 7))
                                    n += 1
                            last.then_inc(m_f, 1)
                        with pe.Fori(0, 2) as i:
                            for n, (src, nk) in enumerate((((hhr, hTr), KT), ((hhr, hTr), KT), ((fTr, for_), 4), ((ohr, oTr), KT))):
                                def before(m):
                                    if n == 0:
                                        pe.wait_ge(m_yf, i * 4)
                                    if n == 1:
                                        pe.wait_ge(m_fe, 16)
                                        pe.wait_ge(m_m, i * 12)
                                    if n == 2 and m == 0:
                                        pe.wait_ge(m_sf, 2)
                                    if n == 3 and m == 0:
                                        pe.wait_ge(m_so, 4)
                                    if n >= 2:
                                        pe.wait_ge(m_g, i * 8 + (4 * (n - 2) + m + 1))

                                slab_products(pe, ring, 2 + 2 * n, bank[4 * (n % 2):4 * (n % 2) + 4], *fm(src), m_pr, i * 16 + (4 * n + 4),
                                              nk=nk, turn=i, per=8, before=before)
                        for j in range(2):
                            all_merged = lambda m: pe.wait_ge(m_m, 24)
                            slab_products(pe, ring, 18 + 2 * j, bank[j:8:2], *tm((mh, mgr)), m_w, 4 * j + 4, before=all_merged)

                    @block.scalar
                    def _(act):
                        for m in range(4):
                            act.wait_ge(m_f, m + 1)
                            nc.scalar.copy(fT[:, m, :], bank[m][:]).then_inc(m_fe, 1)
                        for t in range(TX):
                            for a in range(2):
                                act.wait_ge(m_f, 4 + 2 * t + a + 1)
                                b = bank[4 + t] if a == 0 else bank[t]
                                nc.scalar.copy(fa[:, t, 2 * a:2 * a + 2, :], b[:].rearrange("p (g n) -> p g n", g=2)).then_inc(m_fe, 1)
                        for g in range(4):
                            act.wait_ge(m_f, 12 + g + 1)
                            nc.scalar.copy(fo[:, g, :], bank[4 + g][:]).then_inc(m_fe, 1)
                        with act.Fori(0, 2) as i:
                            act.wait_ge(m_m, i * 12)
                            for n in range(2):
                                for m in range(4):
                                    act.wait_ge(m_pr, i * 16 + (4 * n + m + 1))
                                    nc.scalar.activation(ga[:, n, m, :], bank[4 * n + m][:], ACT.Sigmoid).then_inc(m_g, 1)
                        post_act(act, lambda e, b: e.wait_ge(m_w, 8 if b % 2 else b // 2 + 1))

                    @block.gpsimd
                    def _(pool):
                        post_pool(pool)

                    @block.vector
                    def _(dve):
                        for half in range(2):
                            ring.split(dve, half)
                            c = slice(4 * half, 4 * half + 4)
                            split_all(dve, m_sh, hhr[:, c, :], hT[:, c, 0:SEQ], hTr[:, c, 0:SEQ], 2 * half)
                        for half in range(2):
                            ring.split(dve, 2 + half)
                            c = slice(4 * half, 4 * half + 4)
                            split_all(dve, m_so, ohr[:, c, :], oT[:, c, :], oTr[:, c, :], 2 * half)
                        dve.wait_ge(m_fe, 16)
                        split_all(dve, m_sf, fTr[:], fo[:], for_[:])
                        with dve.Fori(0, 2) as i:
                            for q in (4, 5, 6, 7, 8):
                                ring.split(dve, q, i, 8, size=1024 if q in (6, 7) else 2048)
                            for m in range(4):
                                dve.wait_ge(m_pr, i * 16 + (8 + m + 1))
                                nc.vector.tensor_tensor(ga[:, 0, m, :], ga[:, 0, m, :], bank[m][:], ALU.mult).then_inc(m_yf, 1)
                            for q in (9, 10):
                                ring.split(dve, q, i, 8)
                            for m in range(4):
                                dve.wait_ge(m_pr, i * 16 + (12 + m + 1))
                                nc.vector.tensor_tensor(ga[:, 1, m, :], ga[:, 1, m, :], bank[4 + m][:], ALU.mult).then_inc(m_t, 1)
                                dve.wait_ge(m_t, i * 4 + (m + 1))
                                dve.wait_ge(m_yf, i * 4 + (m + 1))
                                o = mg[:, bass.ds(i * 4 + m, 1), :].rearrange("p a n -> p (a n)")
                                or_ = mgr[:, bass.ds(i * 4 + m, 1), :].rearrange("p a n -> p (a n)")
                                oh_ = mh[:, bass.ds(i * 4 + m, 1), :].rearrange("p a n -> p (a n)")
                                nc.vector.tensor_tensor(o, ga[:, 0, m, :], ga[:, 1, m, :], ALU.add).then_inc(m_m, 1)
                                dve.wait_ge(m_m, i * 12 + (3 * m + 1))
                                split_all(dve, m_m, oh_, o, or_, i * 12 + (3 * m + 1))
                            ring.split(dve, 11, i, 8)
                        for q in (20, 21, 22):
                            ring.split(dve, q)
                        dve.wait_ge(m_ld, 48)
                        post_dve(dve)
                        ring.split(dve, 23)
            ring.passed_split(len(plan_mix))
            if dbg is not None and upto == 5:
                dbg("x1", xt[:]); return
            delta.close()

        if dbg is None or inject is None:
            first_mixer()
            if upto <= 5:
                return
        else:
            ctx_in.close()
            delta.close()
            with nc.Block() as block:
                @block.sync
                def _(sp):
                    s_inj = sem("inject")
                    sp.wait_ge(s_ld, 32)
                    sp.dma_start(xt[:], d["inject"].rearrange("(t p) n -> p t n", p=P)).then_inc(s_inj, 16)
                    sp.wait_ge(s_inj, 16)
                    ring.start_split((plan_ffn if upto == 6 else []) + (plan_fox if upto in (6, 7) else []) + plan_dsw, ring.n[0], ring.n[1])
                    for q in range(2):
                        ring.load_split(sp, q)

                @block.vector
                def _(dve):
                    for q in range(2):
                        ring.split(dve, q)

        def ffn():
            with ExitStack() as fs:
                gT = sb(fs, "ffn_gated_fm", [P, FT, SEQ])
                gh = sb(fs, "ffn_gated_high", [P, FT, SEQ])
                f_sg = sem("ffn_gated_split")

                OWN = 1024
                with ExitStack() as ph:
                    h2 = sb(ph, "ffn_h_fm", [P, KT, SEQ])
                    h2h = sb(ph, "ffn_h_high", [P, KT, SEQ])
                    norm_stage("ffn", [(xt, 0, wsc[:, 2, :], shf[:, 2, :])], h2, hi=h2h)
                    s_rest = [sem(f"ffn_slab_rest{j}") for j in range(2)]
                    pad = sb(ph, "ffn_grid", [P, 2, GRID_R + 2, GRID_C + 2])
                    acc = sb(ph, "ffn_conv", [P, 2, GRID_R, GRID_C])
                    f_sl, f_a, f_u, f_in, f_c, f_s, f_g, f_z = map(sem, (
                        "ffn_gated_low ffn_a_product ffn_u_product ffn_grid_filled ffn_conv_chain ffn_silu ffn_gated ffn_padding").split())
                    with nc.Block() as block:
                        @block.sync
                        def _(sp):
                            for q in range(2, FT + 2):
                                ring.load_split(sp, q)

                        @block.tensor
                        def _(pe):
                            with pe.Fori(0, FT // 2) as i:
                                for j in range(2):
                                    w = ring.halves(j, [P, 2, KT, P])
                                    s, _n = ring.where(j)
                                    ring.wait_split(pe, j, i, 2)
                                    pe.wait_ge(s_rest[j], i * 1 + 1)
                                    pe.wait_ge(f_in, i * 2 + j)
                                    for a in range(2):
                                        if a == 1:
                                            pe.wait_ge(f_g, i * 2)
                                        for k in range(KT):
                                            last = product3(bank[2 * a + j][:], [x[:, a, k, :] for x in w], [x[:, k, :] for x in (rounded(h2h), rounded(h2))], k == 0, k == KT - 1)
                                        last.then_inc((f_a, f_u)[a], 1)
                                    pe.wait_ge(f_u, i * 2 + (j + 1))
                                    pe.sem_inc(ring.used[s], 1)

                        @block.gpsimd
                        def _(pool):
                            for j in range(2):
                                pool.sem_inc(s_rest[j], 1)
                            with pool.Fori(0, FT // 2) as i:
                                for j in range(2):
                                    s, n = ring.where(2 + j)
                                    raw, low, hi = ring.buf[:, s, OWN:2048], ring.bufr[:, s, OWN:2048], ring.bufr[:, s, 2048 + OWN:4096]
                                    pool.wait_ge(ring.rounded[s], i * 1 + (n + 1))
                                    nc.gpsimd.tensor_tensor(low, raw, hi.bitcast(F32), ALU.subtract).then_inc(s_rest[j], 1)
                                    pool.wait_ge(f_sg, i * 2 + (j + 1))
                                    g = [x[:, bass.ds(i * 2 + j, 1), :].rearrange("p a n -> p (a n)") for x in (gT, rounded(gh), rounded(gT))]
                                    nc.gpsimd.tensor_tensor(g[2], g[0], g[1].bitcast(F32), ALU.subtract).then_inc(f_sl, 1)

                        @block.scalar
                        def _(act):
                            act.wait_ge(f_z, 1)
                            with act.Fori(0, FT // 2) as i:
                                for j in range(2):
                                    act.wait_ge(f_a, i * 2 + (j + 1))
                                    act.wait_ge(f_c, i * 18 + 9 * j)
                                    nc.scalar.copy(pad[:, j, 1:1 + GRID_R, 1:1 + GRID_C],
                                                   bank[j][:].rearrange("p (r c) -> p r c", r=GRID_R)).then_inc(f_in, 1)
                                for j in range(2):
                                    act.wait_ge(f_c, i * 18 + (9 * j + 9))
                                    nc.scalar.activation(acc[:, j], acc[:, j], ACT.Silu).then_inc(f_s, 1)

                        @block.vector
                        def _(dve):
                            nc.vector.memset(pad[:], 0.0).then_inc(f_z, 1)
                            with dve.Fori(0, FT // 2) as i:
                                link = Link(dve, f_c, turn=i, per=18)
                                for j in range(2):
                                    dve.wait_ge(f_in, i * 2 + (j + 1))
                                    for n, (a, b) in enumerate([(1, 1)] + [(a, b) for a in range(3) for b in range(3) if (a, b) != (1, 1)]):
                                        tap = colffn[:, bass.ds(i * 2 + ((a * 3 + b) * FT + j), 1)]
                                        src = pad[:, j, a:a + GRID_R, b:b + GRID_C]
                                        if n == 0:
                                            link(nc.vector.tensor_scalar(acc[:, j], src, tap, None, ALU.mult))
                                        else:
                                            link(nc.vector.scalar_tensor_tensor(acc[:, j], src, tap, acc[:, j], ALU.mult, ALU.add))
                                    if j == 0:
                                        ring.split(dve, 2, i, 2, own=OWN)
                                    dve.wait_ge(f_s, i * 2 + (j + 1))
                                    dve.wait_ge(f_u, i * 2 + (j + 1))
                                    g = [x[:, bass.ds(i * 2 + j, 1), :].rearrange("p a n -> p (a n)") for x in (gT, rounded(gh))]
                                    nc.vector.tensor_tensor(g[0], acc[:, j].rearrange("p r c -> p (r c)"), bank[2 + j][:], ALU.mult).then_inc(f_g, 1)
                                    dve.wait_ge(f_g, i * 2 + (j + 1))
                                    nc.vector.tensor_copy(g[1], g[0]).then_inc(f_sg, 1)
                                ring.split(dve, 3, i, 2, own=OWN)
                                link.end()
                ring.passed_split(FT)
                with ExitStack() as ph:
                    w_o = sem("ffn_out_products")
                    post_act, post_pool, post_dve = post_norm(1, ph, "ffn")
                    NS = FT // 2
                    with nc.Block() as block:
                        @block.sync
                        def _(sp):
                            for q in range(2, NS + 2):
                                ring.load_split(sp, q)

                        @block.tensor
                        def _(pe):
                            for n in range(NS):
                                ring.wait_split(pe, n)
                                w = ring.halves(n, [P, 2, DM])
                                s, _n = ring.where(n)
                                for t in range(TX):
                                    for a in range(2):
                                        for k in range(2):
                                            last = product3(bank[2 * t + a][:], [x[:, 2 * n + k, t * P:(t + 1) * P] for x in (rounded(gh), rounded(gT))],
                                                            [x[:, k, 512 * a:512 * a + 512] for x in w], n == 0 and k == 0, n == NS - 1 and k == 1)
                                        if n == NS - 1:
                                            last.then_inc(w_o, 1)
                                if n < NS - 1:
                                    last.then_inc(ring.used[s], 1)
                                else:
                                    pe.wait_ge(w_o, 8)
                                    pe.sem_inc(ring.used[s], 1)

                        @block.scalar
                        def _(act):
                            post_act(act, lambda e, b: e.wait_ge(w_o, b + 1))

                        @block.gpsimd
                        def _(pool):
                            post_pool(pool)

                        @block.vector
                        def _(dve):
                            for q in range(2, NS + 1):
                                ring.split(dve, q)
                            post_dve(dve)
                            ring.split(dve, NS + 1)
                ring.passed_split(NS)

        ffn()
        if upto == 6:
            dbg("x2", xt[:])
            return

        def qkv_project(name, h, QK, V, qn, gain, rope=None, stride=1, gate=None):
            by_rest = lambda x, kk, t: (x[:, kk, t * P:(t + 1) * P] if stride == 1 else
                                        x[:, kk, :].rearrange("p (n s) -> p s n", s=stride)[:, t])
            NQ = 12 if gate is None else 16
            with ExitStack() as ph:
                sem = ph.enter_context(local_sems())
                sqb = sb(ph, name + "_sq", [P, 2, 512])
                ss = sb(ph, name + "_ss", [P, 3, 8, 8])
                wk = sb(ph, name + "_rope_work", [P, 2, 4, 8, 8]) if rope else None
                q_pr, q_sq, q_sm, q_rs, q_n, q_t, q_st, q_ch, v_st = (sem(name + x) for x in (
                    "_projected", "_squared", "_sums", "_rstd", "_normed", "_turned", "_stored", "_rope_chain", "_v_stored"))
                with nc.Block() as block:
                    @block.sync
                    def _(sp):
                        for q in range(2, NQ + 2):
                            ring.load_split(sp, q)

                    @block.tensor
                    def _(pe):
                        def turn_block(s, i, n):
                            for t in range(TX):
                                pe.wait_ge(q_n, i * 8 + (4 * n + t + 1))
                                for m in range(4):
                                    last = nc.tensor.transpose(bank[4 * s + t][:, m * P:(m + 1) * P], qn[:, s, t, m * P:(m + 1) * P], ident)
                                last.then_inc(q_t, 1)

                        pe.sem_inc(q_t, 8)
                        slab_products(pe, ring, 0, bank[0:4], *tm(h, by_rest), q_pr, 4)
                        with pe.Fori(0, 2) as i:
                            free = lambda t: pe.wait_ge(q_st, i * 8 + (t + 1))
                            slab_products(pe, ring, 2, bank[4:8], *tm(h, by_rest), q_pr, i * 8 + 8, turn=i, per=4, before=free)
                            turn_block(0, i, 0)
                            free = lambda t: pe.wait_ge(q_st, i * 8 + (4 + t + 1))
                            slab_products(pe, ring, 4, bank[0:4], *tm(h, by_rest), q_pr, i * 8 + 12, turn=i, per=4, before=free)
                            turn_block(1, i, 1)
                        free = lambda t: pe.wait_ge(q_st, 16 + t + 1)
                        slab_products(pe, ring, 10, bank[4:8], *tm(h, by_rest), q_pr, 24, before=free)
                        if gate is not None:
                            for j in range(2):
                                free = lambda m: pe.wait_ge(v_st, 4 * j + m + 1)
                                slab_products(pe, ring, 12 + 2 * j, bank[4 * j:4 * j + 4], *fm(h), q_pr, 28 + 4 * j, before=free)

                    @block.scalar
                    def _(act):
                        act.sem_inc(q_st, 4)
                        def squares(s):
                            for t in range(TX):
                                n = 4 * s + t
                                act.wait_ge(q_pr, n + 1)
                                if n >= 2:
                                    act.wait_ge(q_sm, n - 1)
                                nc.scalar.activation(sqb[:, n % 2], bank[n % 8][:], ACT.Square).then_inc(q_sq, 1)

                        def store(s):
                            for t in range(TX):
                                act.wait_ge(q_t, 8 + 4 * s + t + 1)
                                dst = QK[:, s // 2, 4 * (s % 2):4 * (s % 2) + 4, t * P:(t + 1) * P]
                                src = bank[4 * (s % 2) + t][:].rearrange("p (m n) -> p m n", m=4)
                                if gain is not None:
                                    nc.scalar.activation(dst, src, ACT.Identity, scale=gain(s // 2)).then_inc(q_st, 1)
                                else:
                                    nc.scalar.copy(dst, src).then_inc(q_st, 1)

                        def store_v(j):
                            for t in range(TX):
                                act.wait_ge(q_pr, 16 + 4 * j + t + 1)
                                nc.scalar.copy(V[:, t, 512 * j:512 * j + 512], bank[4 * j + t][:]).then_inc(v_st, 1)

                        squares(0)
                        for s in range(3):
                            squares(s + 1)
                            store(s)
                        store_v(0)
                        store(3)
                        store_v(1)
                        if gate is not None:
                            for m in range(8):
                                act.wait_ge(q_pr, 24 + m + 1)
                                nc.scalar.activation(gate[:, m, :], bank[m][:], ACT.Silu).then_inc(v_st, 1)

                    @block.gpsimd
                    def _(pool):
                        with pool.Fori(0, 2) as i:
                            for n in range(8):
                                pool.wait_ge(q_sm, i * 8 + (n + 1))
                                nc.gpsimd.tensor_tensor(ss[:, 1, n, :], ss[:, 0, n, :], small[:, 1, 0:8], ALU.add).then_inc(q_rs, 1)
                                pool.wait_ge(q_rs, i * 16 + (2 * n + 1))
                                nc.gpsimd.tensor_tensor(ss[:, 2, n, :], ss[:, 1, n, :], half[:, 0:8], ALU.pow).then_inc(q_rs, 1)

                    @block.vector
                    def _(dve):
                        with dve.Fori(0, 2) as i:
                            link = Link(dve, q_ch, turn=i, per=8 * (5 if rope else 0))
                            def sums(j, t):
                                n = 4 * j + t
                                dve.wait_ge(q_sq, i * 8 + (n + 1))
                                nc.vector.reduce_sum(ss[:, 0, n, :], sqb[:, n % 2].rearrange("p (h n) -> p h n", h=8), axis=AX).then_inc(q_sm, 1)

                            def norm(j, t):
                                n = 4 * j + t
                                dve.wait_ge(q_rs, i * 16 + (2 * n + 2))
                                if t == 0:
                                    dve.wait_ge(q_t, i * 8 + (4 * j + 4))
                                q8 = qn[:, j, t].rearrange("p (h n) -> p h n", h=8)
                                rs = ss[:, 2, n, :].unsqueeze(2).broadcast_to([P, 8, DA])
                                o = nc.vector.tensor_tensor(q8, bank[n][:].rearrange("p (h n) -> p h n", h=8), rs, ALU.mult)
                                if rope is None:
                                    o.then_inc(q_n, 1)
                                else:
                                    link(o)
                                    rope(dve, link, q8, i, t, wk).then_inc(q_n, 1)

                            for j in range(2):
                                sums(j, 0)
                                sums(j, 1)
                                ring.split(dve, 2 * j + 2, i, 4)
                                norm(j, 0)
                                sums(j, 2)
                                norm(j, 1)
                                sums(j, 3)
                                ring.split(dve, 2 * j + 3, i, 4)
                                norm(j, 2)
                                norm(j, 3)
                            link.end()
                        for q in range(10, NQ + 1):
                            ring.split(dve, q)
            ring.passed_split(NQ, left=True)

        def attend(name, QK, V, units, add, out, stride=1, ncT=None, gs=None, stats=None, room=(None, None), hi=None):
            NP = sum(u[4] for u in units)
            NU_ = len(units)
            NB = (NP + 3) // 4
            with ExitStack() as ph:
                sem = ph.enter_context(local_sems())
                qs = room[0] or sb(ph, name + "_q_pair", [P, 2, SEQ])
                sc = sb(ph, name + "_scores", [P, 2, NP, P])
                pT = sb(ph, name + "_probs_t", [P, 2, NP, P]) if room[1] is None else room[1].rearrange("p (a u n) -> p a u n", a=2, u=NP)
                nm = sb(ph, name + "_stats", [P, 3, 2, TX])
                osb = sb(ph, name + "_out_tm", [P, TX, 2, DA])
                cm = sb(ph, name + "_c_masked", [NA, 2, SEQ]) if ncT is not None else None
                crep = sb(ph, name + "_c_rep", [P, 2, SEQ]) if ncT is not None else None
                a_q, a_cm, a_cp, a_cr, a_s, a_mx, a_ex, a_t, a_st, a_o, a_rc, a_os, a_ot, a_out = (sem(name + x) for x in (
                    "_pair_copied", "_c_one_head", "_c_product", "_c_ready", "_scores_ready", "_max_ready", "_probs_ready", "_probs_turned",
                    "_probs_stored", "_out_products", "_sum_inverse", "_out_scaled", "_out_turned", "_out_stored"))
                a_spl = sem(name + "_out_split")
                a_go = sem(name + "_max_begun")
                nbank = 1 + max(u[1] for u in units)

                def wait(eng, s, m, per, n, ahead=0):
                    v = m * per + (ahead * per + n)
                    if not isinstance(v, int) or v > 0:
                        eng.wait_ge(s, v)

                def turns(eng, turn):
                    turn(0, True, False)
                    with eng.Fori(1, KT - 1) as m:
                        turn(m, False, False)
                    turn(KT - 1, False, True)

                with nc.Block() as block:
                    @block.gpsimd
                    def _(pool):
                        def copy_pair(m, ahead):
                            wait(pool, a_s, m, 2 * nbank, 0, ahead)
                            for w in range(2):
                                nc.gpsimd.tensor_copy(qs[:, w], QK[:, w, bass.ds(m + ahead, 1), :].rearrange("p a n -> p (a n)")).then_inc(a_q, 1)

                        copy_pair(0, 0)
                        with pool.Fori(0, KT - 1) as m:
                            copy_pair(m, 1)

                    @block.tensor
                    def _(pe):
                        def c_rows(m, ahead, a):
                            if ncT is None:
                                return
                            wait(pe, a_cm, m, 2, a + 1, ahead)
                            wait(pe, a_cr, m, 2, a, ahead)
                            if a == 0:
                                wait(pe, a_out, m, 1, -1, ahead)
                            nc.tensor.matmul(bank[7][:], m_ones[0:NA, :], cm[:, a, :], start=True, stop=True).then_inc(a_cp, 1)

                        def scores(m, ahead, a):
                            wait(pe, a_q, m, 2, 2, ahead)
                            wait(pe, a_st, m, 2 * NB, (a - 1) * NB, ahead)
                            r = slice(DA * a, DA * a + DA)
                            for n, (q, b, c, k0, nk) in enumerate(units):
                                o = bank[3 * a + b][:, c:c + nk * P]
                                last = nc.tensor.matmul(o, qs[r, 0, q * P:(q + 1) * P], qs[r, 1, k0 * P:(k0 + nk) * P], start=True, stop=(ncT is None))
                                if ncT is not None:
                                    last = nc.tensor.matmul(bank[3 * a + b][:, c + (nk - 1) * P:c + nk * P], ident, att[:, 1, :], start=False, stop=True)
                                if n == NU_ - 1 or units[n + 1][1] != b:
                                    last.then_inc(a_s, 1)

                        def turn_probs(m, a):
                            wait(pe, a_ex, m, 2 * NU_, (a + 1) * NU_)
                            for g in range(NB):
                                for i in range(min(4, NP - 4 * g)):
                                    last = nc.tensor.transpose(bank[3 * a + g][:, i * P:(i + 1) * P], sc[:, a, 4 * g + i, :], ident)
                                last.then_inc(a_t, 1)

                        def outputs(m, ahead, a):
                            wait(pe, a_st, m, 2 * NB, (a + 1) * NB, ahead)
                            wait(pe, a_os, m, 2, a, ahead)
                            i = 0
                            for q, b, c, k0, nk in units:
                                for k in range(nk):
                                    v = V[:, k0 + k, bass.ds(m * P + (ahead * P + DA * a), DA)]
                                    last = nc.tensor.matmul(bank[6][:, q * P + DA * a:q * P + DA * a + DA], pT[:, a, i, :], v, start=(k == 0), stop=(k == nk - 1))
                                    i += 1
                            last.then_inc(a_o, 1)

                        def turn_outputs(m, ahead, rows):
                            wait(pe, a_os, m, 2, 2, ahead)
                            if ncT is not None:
                                wait(pe, a_cr, m, 2, rows, ahead)
                            wait(pe, a_out, m, 1, 0, ahead)
                            for t in range(TX):
                                last = nc.tensor.transpose(bank[7][:, t * P:(t + 1) * P], osb[:, t].rearrange("p a n -> p (a n)"), ident)
                            last.then_inc(a_ot, 1)

                        def turn(m, first, final):
                            scores(m, 0, 1)
                            turn_probs(m, 0)
                            if not first:
                                outputs(m, -1, 1)
                                turn_outputs(m, -1, 4)
                            if not final:
                                scores(m, 1, 0)
                                c_rows(m, 1, 0)
                            turn_probs(m, 1)
                            if not final:
                                c_rows(m, 1, 1)
                            outputs(m, 0, 0)

                        scores(0, 0, 0)
                        c_rows(0, 0, 0)
                        c_rows(0, 0, 1)
                        turns(pe, turn)
                        outputs(KT - 1, 0, 1)
                        turn_outputs(KT - 1, 0, 2)

                    @block.scalar
                    def _(act):
                        def c_rows(m, ahead, a):
                            if ncT is None:
                                return
                            wait(act, a_cp, m, 2, a + 1, ahead)
                            wait(act, a_mx, m, 2 * NU_, (a - 1) * NU_, ahead)
                            nc.scalar.copy(crep[:, a, :], bank[7][:]).then_inc(a_cr, 1)

                        def exps(m, ahead, a):
                            i = 0
                            for n, (q, b, c, k0, nk) in enumerate(units):
                                wait(act, a_mx, m, 2 * NU_, a * NU_ + n + 1, ahead)
                                nc.scalar.activation(sc[:, a, i:i + nk, :], sc[:, a, i:i + nk, :], ACT.Exp, scale=-1.0, bias=nm[:, 0, a, q:q + 1],
                                                     accum_out=nm[:, 1, a, q:q + 1]).then_inc(a_ex, 1)
                                i += nk

                        def store_probs(m, a):
                            wait(act, a_o, m, 2, a - 1)
                            for g in range(NB):
                                w = min(4, NP - 4 * g)
                                wait(act, a_t, m, 2 * NB, a * NB + g + 1)
                                nc.scalar.copy(pT[:, a, 4 * g:4 * g + w, :], grp4(bank[3 * a + g])[:, 0:w]).then_inc(a_st, 1)

                        def turn(m, first, final):
                            store_probs(m, 0)
                            exps(m, 0, 1)
                            if not final:
                                c_rows(m, 1, 0)
                            store_probs(m, 1)
                            if not final:
                                exps(m, 1, 0)
                                c_rows(m, 1, 1)

                        c_rows(0, 0, 0)
                        c_rows(0, 0, 1)
                        exps(0, 0, 0)
                        turns(act, turn)

                    @block.vector
                    def _(dve):
                        def c_one_head(m, ahead):
                            if ncT is None:
                                return
                            wait(dve, a_cp, m, 2, 0, ahead)
                            for a in range(2):
                                nc.vector.tensor_scalar(cm[:, a, :], ncT[:], ident[0:NA, bass.ds(m * 2 + (2 * ahead + a), 1)], None, ALU.mult).then_inc(a_cm, 1)

                        def maxima(m, ahead, a):
                            if ncT is not None:
                                wait(dve, a_cr, m, 2, a + 1, ahead)
                            wait(dve, a_t, m, 2 * NB, (a - 1) * NB, ahead)
                            wait(dve, a_rc, m, 6, 3 * (a - 1), ahead)
                            i = 0
                            for n, (q, b, c, k0, nk) in enumerate(units):
                                if n == 0 or units[n - 1][1] != b:
                                    wait(dve, a_s, m, 2 * nbank, a * nbank + b + 1, ahead)
                                    dve.sem_inc(a_go, 1)
                                plus = crep[:, a, 0:nk * P] if ncT is not None else add(nk)
                                nc.vector.tensor_tensor_reduce(
                                    out=sc[:, a, i:i + nk, :].rearrange("p u n -> p (u n)"), in0=bank[3 * a + b][:, c:c + nk * P], in1=plus,
                                    scale=-1.0, scalar=3.0e38, op0=ALU.add, op1=ALU.min, accum_out=nm[:, 0, a, q:q + 1]).then_inc(a_mx, 1)
                                i += nk

                        def inverse_sums(m, a):
                            wait(dve, a_ex, m, 2 * NU_, (a + 1) * NU_)
                            for kind in range(2):
                                if stats is None:
                                    dve.sem_inc(a_rc, 1)
                                else:
                                    nc.vector.tensor_copy(stats[:, kind, bass.ds(m * 2 + a, 1), :].rearrange("p a u -> p (a u)"), nm[:, kind, a]).then_inc(a_rc, 1)
                            wait(dve, a_os, m, 2, a - 1)
                            nc.vector.reciprocal(nm[:, 2, a], nm[:, 1, a]).then_inc(a_rc, 1)

                        def scale(m, ahead, a):
                            wait(dve, a_rc, m, 6, 3 * (a + 1), ahead)
                            wait(dve, a_ot, m, 1, 0, ahead)
                            wait(dve, a_o, m, 2, a + 1, ahead)
                            nc.vector.tensor_tensor(osb[:, :, a], bank[6][:].rearrange("p (u a n) -> p a u n", u=TX, a=2)[:, a],
                                                    nm[:, 2, a].unsqueeze(2).broadcast_to([P, TX, DA]), ALU.mult).then_inc(a_os, 1)

                        def store(m, ahead):
                            wait(dve, a_ot, m, 1, 1, ahead)
                            o = out[:, bass.ds(m + ahead, 1), :].rearrange("p a n -> p (a n)")
                            if gs is not None:
                                g = gs[:, bass.ds(m + ahead, 1), :].rearrange("p a n -> p (a n)")
                                nc.vector.tensor_tensor(o, bank[7][:], g, ALU.mult).then_inc(a_out, 1)
                            elif stride > 1:
                                nc.vector.tensor_copy(o.rearrange("p (n s) -> p s n", s=stride),
                                                      bank[7][:].rearrange("p (s n) -> p s n", s=stride)).then_inc(a_out, 1)
                            else:
                                nc.vector.tensor_copy(o, bank[7][:]).then_inc(a_out, 1)
                            if hi is not None:
                                oh, ol = (x[:, bass.ds(m + ahead, 1), :].rearrange("p a n -> p (a n)") for x in (rounded(hi), rounded(out)))
                                wait(dve, a_out, m, 1, 1, ahead)
                                nc.vector.tensor_copy(oh, o).then_inc(a_spl, 1)
                                wait(dve, a_spl, m, 2, 1, ahead)
                                nc.vector.tensor_tensor(ol, o, oh.bitcast(F32), ALU.subtract).then_inc(a_spl, 1)

                        def turn(m, first, final):
                            maxima(m, 0, 1)
                            inverse_sums(m, 0)
                            if not final:
                                c_one_head(m, 1)
                            if not first:
                                scale(m, -1, 1)
                                store(m, -1)
                            if not final:
                                maxima(m, 1, 0)
                            scale(m, 0, 0)
                            inverse_sums(m, 1)

                        c_one_head(0, 0)
                        maxima(0, 0, 0)
                        ring.finish_split(dve)
                        turns(dve, turn)
                        scale(KT - 1, 0, 1)
                        store(KT - 1, 0)

        def out_project(name, oT_, hi):
            o_p, o_a = sem(name + "_wo_products"), sem(name + "_residual_added")
            with nc.Block() as block:
                @block.sync
                def _(sp):
                    for q in range(2, 6):
                        ring.load_split(sp, q)

                @block.tensor
                def _(pe):
                    for j in range(2):
                        slab_products(pe, ring, 2 * j, bank[j:8:2], *tm((rounded(hi), rounded(oT_))), o_p, 4 * j + 4)

                @block.vector
                def _(dve):
                    ring.split(dve, 2)
                    ring.split(dve, 3)
                    for j in range(2):
                        for t in range(TX):
                            if j == 1 and t == 0:
                                ring.split(dve, 4)
                            dve.wait_ge(o_p, 4 * j + t + 1)
                            c = slice(512 * j, 512 * j + 512)
                            nc.vector.tensor_tensor(xt[:, t, c], xt[:, t, c], bank[2 * t + j][:], ALU.add).then_inc(o_a, 1)
            ring.passed_split(4, left=True)

        grp4 = lambda b: b[:].rearrange("p (u n) -> p u n", u=4)
        CAUSAL = [(0, 0, 0, 0, 1), (1, 0, P, 0, 2), (2, 1, 0, 0, 3), (3, 2, 0, 0, 4)]
        s_hc = sem("head_constants")

        def fox():
            fw = d["fox_w_in_2"][0].rearrange("(k p) n -> p k n", p=P)
            with ExitStack() as fs:
                QK = sb(fs, "fox_qk_fm", [P, 2, KT, SEQ])
                V = sb(fs, "fox_v_tm", [P, TX, DM])
                gs = sb(fs, "fox_gate_fm", [P, KT, SEQ])
                ncT = sb(fs, "fox_minus_c", [NA, SEQ])
                h = sb(fs, "fox_h_fm", [P, KT, SEQ])
                hh = sb(fs, "fox_h_high", [P, KT, SEQ])
                gcol = sb(fs, "fox_gains", [P, 2])
                wf = sb(fs, "fox_w_f", [P, KT, NA])
                bf = sb(fs, "fox_b_f", [P, NA])
                t = sb(fs, "fox_forget_work", [P, 6, TX, NA])
                with nc.Block() as block:
                    @block.sync
                    def _(sp):
                        sp.dma_start(wf[:], fw[:, :, 4 * DM:4 * DM + NA]).then_inc(s_hc, 16)
                        sp.dma_start(bf[:], d["fox_b_f_2"].broadcast_to([P, NA])).then_inc(s_hc, 16)
                        for a in range(2):
                            for i, g in enumerate(("fox_q_norm_2", "fox_k_norm_2")):
                                sp.dma_start(gcol[DA * a:DA * a + DA, i:i + 1], d[g].rearrange("a n -> n a")).then_inc(s_hc, 16)
                        sp.wait_ge(s_hc, 16 * 6)
                o, n = ROWS_A["g2"]
                norm_stage("fox", [(xt, 0, col[:, o:o + KT], None)], h)
                g_mm, g_d, g_a, g_s = sem("forget_products"), sem("forget_dve_chain"), sem("forget_act"), sem("fox_h_split")
                with nc.Block() as block:
                    @block.tensor
                    def _(pe):
                        for b in range(TX):
                            for k in range(KT):
                                last = nc.tensor.matmul(bank[0][:, NA * b:NA * b + NA], h[:, k, b * P:(b + 1) * P], wf[:, k, :], start=(k == 0), stop=(k == KT - 1))
                        last.then_inc(g_mm, 1)
                        pe.wait_ge(g_d, 10)
                        for b in range(TX):
                            for s in range(b + 1):
                                last = nc.tensor.matmul(bank[1][0:NA, b * P:(b + 1) * P], t[:, 5, s, :], m_le if s == b else m_ones, start=(s == 0), stop=(s == b))
                        last.then_inc(g_mm, 1)

                    @block.vector
                    def _(dve):
                        link = Link(dve, g_d)
                        dve.wait_ge(g_mm, 1)
                        f = bank[0][:, 0:TX * NA].rearrange("p (b n) -> p b n", n=NA)
                        link(nc.vector.tensor_scalar(gcol[:, 1:2], gcol[:, 1:2], float(DA) ** 0.5, None, ALU.mult))
                        link(nc.vector.tensor_tensor(t[:, 0], f, bf[:].unsqueeze(1).broadcast_to([P, TX, NA]), ALU.add))
                        link(nc.vector.tensor_scalar(t[:, 1], t[:, 0], -1.0, None, ALU.mult))
                        link(nc.vector.tensor_tensor(t[:, 2], t[:, 0], t[:, 1], ALU.min))
                        dve.wait_ge(g_a, 2)
                        link(nc.vector.tensor_scalar(t[:, 1], t[:, 3], 1.0, None, ALU.add))
                        link(nc.vector.tensor_scalar(t[:, 1], t[:, 1], -1.0, None, ALU.add))
                        link(nc.vector.tensor_tensor(t[:, 1], t[:, 3], t[:, 1], ALU.subtract))
                        link(nc.vector.tensor_tensor(t[:, 1], t[:, 4], t[:, 1], ALU.add))
                        link(nc.vector.tensor_scalar(t[:, 0], t[:, 0], 0.0, None, ALU.min))
                        link(nc.vector.tensor_tensor(t[:, 5], t[:, 0], t[:, 1], ALU.subtract))
                        split_all(dve, g_s, rounded(hh)[:], h[:], rounded(h)[:])

                    @block.scalar
                    def _(act):
                        act.wait_ge(g_d, 4)
                        nc.scalar.activation(t[:, 3], t[:, 2], ACT.Exp).then_inc(g_a, 1)
                        act.wait_ge(g_a, 1)
                        nc.scalar.activation(t[:, 4], t[:, 3], ACT.Ln, bias=1.0).then_inc(g_a, 1)
                        act.wait_ge(g_mm, 2)
                        nc.scalar.mul(ncT[:], bank[1][0:NA, :], -1.0).then_inc(g_a, 1)
                qkv_project("fox", (rounded(hh), rounded(h)), QK, V, gs[:].rearrange("p (j t) n -> p j t n", j=2), lambda i: gcol[:, i:i + 1], gate=gs)
                attend("fox", QK, V, CAUSAL, None, h, ncT=ncT, gs=gs, hi=hh)
                out_project("fox", h, hh)

        if upto != 8:
            fox()
        if upto == 7:
            dbg("x3", xt[:])
            return

        def gate_project(name, h, dst):
            p, s = sem(name + "_gate_products"), sem(name + "_gate_stored")
            with nc.Block() as block:
                @block.sync
                def _(sp):
                    for q in range(2, 6):
                        ring.load_split(sp, q)

                @block.tensor
                def _(pe):
                    for j in range(2):
                        slab_products(pe, ring, 2 * j, bank[4 * j:4 * j + 4], *fm(h), p, 4 * j + 4)

                @block.vector
                def _(dve):
                    for q in range(2, 5):
                        ring.split(dve, q)

                @block.scalar
                def _(act):
                    for m in range(8):
                        act.wait_ge(p, m + 1)
                        nc.scalar.activation(dst[:, m, :], bank[m][:], ACT.Silu).then_inc(s, 1)
            ring.passed_split(4, left=True)

        def dsw():
            C1 = 6.28125
            C2 = float(np.float32(round((2 * math.pi - C1) * 2.0 ** 19) / 2.0 ** 19))
            C3 = 2 * math.pi - C1 - C2
            MAGIC = 1.5 * 2.0 ** 23
            TOP = 3.1415925
            with ExitStack() as fs:
                O = sb(fs, "dsw_out_fm", [P, NG, KT, SEQ])
                h = sb(fs, "dsw_h_fm", [P, KT, SEQ])
                hh = sb(fs, "dsw_h_high", [P, KT, SEQ])
                QK = sb(fs, "dsw_qk_fm", [P, 2, KT, SEQ])
                V = sb(fs, "dsw_v_tm", [P, TX, DM])
                stats = sb(fs, "dsw_stats", [P, NG, 2, NA, TX])
                gains = sb(fs, "dsw_gains", [P, NG, 2, DA])
                cs = sb(fs, "rope_cos_sin", [P, 2, 2 * TX, 8])
                with ExitStack() as ph:
                    pi = sb(ph, "positions", [P, 2 * TX], I32)
                    inv = sb(ph, "inverse_frequencies", [P, 8])
                    t = sb(ph, "rope_setup", [P, 6, 2 * TX, 8])
                    r_l, r_d, r_a = sem("rope_loads"), sem("rope_setup_chain"), sem("rope_tables")
                    with nc.Block() as block:
                        @block.sync
                        def _(sp):
                            for b in range(TX):
                                sp.dma_start(pi[:, b:b + 1], d["positions_2"][:, b * P:(b + 1) * P].rearrange("a p -> p a")).then_inc(r_l, 16)
                            sp.dma_start(pi[:, TX:2 * TX], d["positions_2"].rearrange("a (p s) -> p (a s)", s=4)).then_inc(r_l, 16)
                            sp.dma_start(inv[:], d["k_inv"]).then_inc(r_l, 16)
                            for i, g in enumerate(("dsw_q_norm_2", "dsw_k_norm_2")):
                                sp.dma_start(gains[:, :, i, :], d[g].broadcast_to([P, NG, DA])).then_inc(r_l, 16)

                        @block.vector
                        def _(dve):
                            link = Link(dve, r_d)
                            dve.wait_ge(r_l, 16 * (TX + 4))
                            link(nc.vector.tensor_scalar(gains[:, :, 1, :], gains[:, :, 1, :], float(DA) ** 0.5, None, ALU.mult))
                            link(nc.vector.tensor_copy(t[:, 0, :, 0], pi[:]))
                            link(nc.vector.tensor_tensor(t[:, 1], t[:, 0, :, 0:1].broadcast_to([P, 2 * TX, 8]), inv[:].unsqueeze(1).broadcast_to([P, 2 * TX, 8]), ALU.mult))
                            link(nc.vector.tensor_scalar(t[:, 2], t[:, 1], 1.0 / (2 * math.pi), MAGIC, ALU.mult, ALU.add))
                            link(nc.vector.tensor_scalar(t[:, 2], t[:, 2], -MAGIC, None, ALU.add))
                            for c in (C1, C2, C3):
                                link(nc.vector.scalar_tensor_tensor(t[:, 1], t[:, 2], -c, t[:, 1], ALU.mult, ALU.add))
                            link(nc.vector.tensor_scalar(t[:, 3], t[:, 1], TOP, -TOP, ALU.min, ALU.max))
                            link(nc.vector.tensor_scalar(t[:, 4], t[:, 1], math.pi / 2, None, ALU.add))
                            link(nc.vector.tensor_scalar(t[:, 5], t[:, 4], math.pi, -2 * math.pi, ALU.is_gt, ALU.mult))
                            link(nc.vector.tensor_tensor(t[:, 4], t[:, 4], t[:, 5], ALU.add))
                            link(nc.vector.tensor_scalar(t[:, 4], t[:, 4], TOP, -TOP, ALU.min, ALU.max))

                        @block.scalar
                        def _(act):
                            act.wait_ge(r_d, 13)
                            nc.scalar.activation(cs[:, 0], t[:, 4], ACT.Sin).then_inc(r_a, 1)
                            nc.scalar.activation(cs[:, 1], t[:, 3], ACT.Sin).then_inc(r_a, 1)
                o, n = ROWS_A["g2"]
                norm_stage("dsw", [(xt, 0, col[:, o + KT:o + 2 * KT], None)], h, hi=hh, xn=V)
                for g in range(NG):
                    def rope(dve, link, q8, i, t, wk, g=g):
                        gv = gains[:, g, bass.ds(i, 1), :].broadcast_to([P, 8, DA])
                        link(nc.vector.tensor_tensor(q8, q8, gv, ALU.mult))
                        r = q8[:, :, 0:ROT].rearrange("p h (a n) -> p a h n", a=2)
                        c = cs[:, 0, (TX if g else 0) + t, :].unsqueeze(1).broadcast_to([P, 8, 8])
                        s = cs[:, 1, (TX if g else 0) + t, :].unsqueeze(1).broadcast_to([P, 8, 8])
                        for a in range(2):
                            last = nc.vector.tensor_tensor(wk[:, t % 2, a], r[:, a], c, ALU.mult)
                        link(last)
                        link(nc.vector.tensor_tensor(wk[:, t % 2, 2], r[:, 1], s, ALU.mult))
                        link(nc.vector.tensor_tensor(wk[:, t % 2, 3], r[:, 0], s, ALU.mult))
                        nc.vector.tensor_tensor(r[:, 0], wk[:, t % 2, 0], wk[:, t % 2, 2], ALU.subtract)
                        return nc.vector.tensor_tensor(r[:, 1], wk[:, t % 2, 1], wk[:, t % 2, 3], ALU.add)

                    name = f"dsw{g}"
                    st = 1 if g == 0 else 4
                    qkv_project(name, (rounded(hh), rounded(h)), QK, V, O[:, g].rearrange("p (j t) n -> p j t n", j=2), None, rope, stride=st)
                    attend(name, QK, V, BAND if g == 0 else BLOCKS,
                           (lambda nk: att[:, 2 - nk:2, :].rearrange("p a n -> p (a n)")) if g == 0 else (lambda nk, g=g: att[:, g, :]),
                           O[:, g], stride=st, stats=stats[:, g],
                           room=(gtrow[:, 0].rearrange("p (w n) -> p w n", w=2),
                                 gtrow[:, 1] if g else O[:, 1].rearrange("p k n -> p (k n)")[:, 0:14 * P]))
                gs = QK[:, 0]
                gate_project("dsw", (rounded(hh), rounded(h)), gs)
                with ExitStack() as ph:
                    lse = sb(ph, "dsw_lse", [P, NG, TX, NA])
                    lt = V[0:NA].rearrange("p t n -> p (t n)")[:, 0:(NG + 2) * SEQ].rearrange("p (g n) -> p g n", g=NG + 2)
                    hs = sb(ph, "head_to_rows", [NA, NA // 2, P])
                    w = QK[:, 1, 0:2 * NG].rearrange("p (b g) n -> p b g n", b=2)
                    c_s, c_l, c_a, c_d, c_t, c_e, c_r, c_m, c_o = map(sem, (
                        "combine_split combine_loads combine_ln combine_dve combine_turned combine_act combine_rep combine_scaled combine_out").split())
                    with nc.Block() as block:
                        @block.sync
                        def _(sp):
                            sp.dma_start(hs[:], d["k_hs"]).then_inc(c_l, 16)

                        @block.scalar
                        def _(act):
                            nc.scalar.activation(stats[:, :, 1], stats[:, :, 1], ACT.Ln).then_inc(c_a, 1)
                            for g in range(NG):
                                act.wait_ge(c_t, g + 1)
                                if g == 0:
                                    nc.scalar.copy(lt[:, g, :], bank[g][0:NA, :]).then_inc(c_a, 1)
                                else:
                                    nc.scalar.copy(lt[:, g, :].rearrange("p (n s) -> p s n", s=4), bank[g][0:NA, :].rearrange("p (s n) -> p s n", s=4)).then_inc(c_a, 1)
                            act.wait_ge(c_d, 6)
                            nc.scalar.activation(lt[:, 0:NG, :], lt[:, 0:NG, :], ACT.Exp).then_inc(c_a, 1)

                        @block.tensor
                        def _(pe):
                            pe.wait_ge(c_d, 1)
                            for g in range(NG):
                                for b in range(TX):
                                    last = nc.tensor.transpose(bank[g][0:NA, b * P:(b + 1) * P], lse[:, g, b, :], ident)
                                last.then_inc(c_t, 1)
                            pe.wait_ge(c_l, 16)
                            pe.wait_ge(c_d, 10)
                            for m in range(KT):
                                for g in range(NG):
                                    if m >= 2:
                                        pe.wait_ge(c_m, NG * (m - 2) + g + 1)
                                    nc.tensor.matmul(bank[3 * (m % 2) + g][:], hs[:, m, :], lt[:, g, :], start=True, stop=True).then_inc(c_r, 1)

                        @block.vector
                        def _(dve):
                            link = Link(dve, c_d)
                            dve.wait_ge(c_a, 1)
                            link(nc.vector.tensor_tensor(lse[:].rearrange("p g t h -> p g h t"), stats[:, :, 1], stats[:, :, 0], ALU.subtract))
                            dve.wait_ge(c_a, 4)
                            link(nc.vector.tensor_tensor(lt[:, 3, :], lt[:, 0, :], lt[:, 1, :], ALU.max))
                            link(nc.vector.tensor_tensor(lt[:, 3, :], lt[:, 3, :], lt[:, 2, :], ALU.max))
                            for g in range(NG):
                                link(nc.vector.tensor_tensor(lt[:, g, :], lt[:, g, :], lt[:, 3, :], ALU.subtract))
                            dve.wait_ge(c_a, 5)
                            link(nc.vector.tensor_tensor(lt[:, 3, :], lt[:, 0, :], lt[:, 1, :], ALU.add))
                            link(nc.vector.tensor_tensor(lt[:, 3, :], lt[:, 3, :], lt[:, 2, :], ALU.add))
                            link(nc.vector.reciprocal(lt[:, 4, :], lt[:, 3, :]))
                            link(nc.vector.tensor_tensor(lt[:, 0:NG, :], lt[:, 0:NG, :], lt[:, 4:5, :].broadcast_to([NA, NG, SEQ]), ALU.mult))
                            for m in range(KT + 2):
                                if m >= 2:
                                    dve.wait_ge(c_o, 3 * (m - 1))
                                    split_all(dve, c_s, rounded(hh)[:, m - 2, :], h[:, m - 2, :], rounded(h)[:, m - 2, :], 2 * (m - 2))
                                for g in range(NG if m < KT else 0):
                                    dve.wait_ge(c_r, NG * m + g + 1)
                                    nc.vector.tensor_tensor(w[:, m % 2, g], O[:, g, m, :], bank[3 * (m % 2) + g][:], ALU.mult).then_inc(c_m, 1)

                            ring.finish_split(dve)

                        @block.gpsimd
                        def _(pool):
                            for m in range(KT):
                                pool.wait_ge(c_m, NG * (m + 1))
                                v = w[:, m % 2]
                                nc.gpsimd.tensor_tensor(v[:, 0], v[:, 0], v[:, 1], ALU.add).then_inc(c_o, 1)
                                pool.wait_ge(c_o, 3 * m + 1)
                                nc.gpsimd.tensor_tensor(v[:, 0], v[:, 0], v[:, 2], ALU.add).then_inc(c_o, 1)
                                pool.wait_ge(c_o, 3 * m + 2)
                                nc.gpsimd.tensor_tensor(h[:, m, :], v[:, 0], gs[:, m, :], ALU.mult).then_inc(c_o, 1)
                out_project("dsw", h, hh)

        BAND = [(0, 0, 0, 0, 1), (1, 0, P, 0, 2), (2, 1, 0, 1, 2), (3, 1, 2 * P, 2, 2)]
        BLOCKS = [(b, 0, P * b, b, 1) for b in range(TX)]
        dsw()
        s_out = sem("out_stored")
        with nc.Block() as block:
            @block.sync
            def _(sp):
                sp.dma_start(out[0].rearrange("(t p) n -> p t n", p=P), xt[:]).then_inc(s_out, 16)
                sp.wait_ge(s_out, 16)



_OUTS = [((1, SEQ, DM), "float32")]
_INS = ["x", "c", "ctx", "c_ctx", "w_ada", "b_ada", "norm_pre_mix", "norm_post_mix", "norm_pre_ffn", "norm_post_ffn",
        "w_in", "conv_qkv", "a_log", "dt_bias", "dn_norm", "w_fourier", "w_dn", "w_out", "w_up", "conv_ffn", "w_down",
        "positions_2", "norm_g_2", "fox_w_in_2", "fox_b_f_2", "fox_q_norm_2", "fox_k_norm_2", "fox_w_out_2",
        "dsw_w_in_2", "dsw_q_norm_2", "dsw_k_norm_2", "dsw_w_out_2"]


def kernel(**inputs):
    import concourse.bacc as bacc
    from concourse.bass_utils import run_bass_kernel_spmd

    nc = bacc.Bacc("TRN2", target_bir_lowering=False, num_devices=1)
    arrays, d = {}, {}
    for name, a in [(n, inputs[n]) for n in _INS] + list(constants().items()):
        a = np.ascontiguousarray(a)
        arrays["in_" + name] = a
        d[name] = nc.dram_tensor("in_" + name, a.shape, mybir.dt.from_np(a.dtype), kind="ExternalInput").ap()
    shape, dtype = _OUTS[0]
    out = nc.dram_tensor("out_0_dram", shape, F32, kind="ExternalOutput").ap()
    build(nc, d, out)
    r = run_bass_kernel_spmd(nc, [arrays], core_ids=[0])
    return r.results[0]["out_0_dram"]
```
